# Optimizing a Trainium2 kernel written in Bass

```python
import jax, jax.numpy as jnp
from jax import lax
import numpy as np

D_MODEL = 2048
BATCH = 1
SEQ = 256
DEPTH = 1
DEC_BATCH = 8
DEC_SEQ = 4
PAST_LEN = 2048
PAGE_SIZE = 128

MIX_WIDTH = D_MODEL
ATTN_WIDTH = MIX_WIDTH // 2
POOL_WIDTH = MIX_WIDTH - ATTN_WIDTH
HEAD_DIM = 128
N_HEADS = ATTN_WIDTH // HEAD_DIM
MOBA_BLOCK = 256
MOBA_TOPK = 3
Q_CHUNK = 16
POOL_WINDOWS = (2, 4, 8, 16)
N_POOL_GROUPS = len(POOL_WINDOWS)
POOL_GROUP_W = POOL_WIDTH // N_POOL_GROUPS
POOL_HIST = max(POOL_WINDOWS) - 1
IN_WIDTH = 3 * ATTN_WIDTH + POOL_WIDTH
D_FF = -(-8 * D_MODEL // (3 * 256)) * 256
RMS_EPS = 1e-6
NEG = -1e30

kernel_name = 'moba_pool_hybrid_step'

def rmsnorm(x, g):
    xf = x.astype(jnp.float32)
    y = xf * lax.rsqrt(jnp.mean(xf * xf, axis=-1, keepdims=True) + RMS_EPS)
    return (y * g.astype(jnp.float32)).astype(x.dtype)

def alibi_slopes():
    return jnp.exp2(-8.0 * jnp.arange(1, N_HEADS + 1, dtype=jnp.float32) / N_HEADS)

def moba_select(q, q_pos, k_mean):
    s = jnp.einsum('bhqd,bnhd->bhqn', q.astype(jnp.float32), k_mean)
    nb = k_mean.shape[1]
    q_blk = q_pos // MOBA_BLOCK
    past = jnp.arange(nb)[None, :] < q_blk[:, None]
    s = jnp.where(past, s, NEG)
    _, idx = lax.top_k(s, min(MOBA_TOPK, nb))
    valid = idx < q_blk[:, None]
    return idx, valid

def moba_attend(q, q_pos, k_sel, v_sel, idx, valid, k_own, v_own, own_start, slopes):
    B, H, Tq, D = q.shape
    KS = idx.shape[-1]
    n_sel = KS * MOBA_BLOCK
    scale = D ** -0.5
    offs = jnp.arange(MOBA_BLOCK, dtype=jnp.int32)
    s_sel = jnp.einsum('bhqd,bhqjkd->bhqjk', q, k_sel, preferred_element_type=jnp.float32) * scale
    dist_sel = (q_pos[:, None, None] - (idx[..., None] * MOBA_BLOCK + offs)).astype(jnp.float32)
    s_sel = jnp.where(valid[..., None], s_sel - slopes[:, None, None, None] * dist_sel, NEG)
    s_own = jnp.einsum('bhqd,bkhd->bhqk', q, k_own, preferred_element_type=jnp.float32) * scale
    dist_own = (q_pos[:, None] - (own_start + offs)[None, :]).astype(jnp.float32)
    s_own = jnp.where(dist_own >= 0, s_own - slopes[:, None, None] * dist_own, NEG)
    s = jnp.concatenate([s_sel.reshape(B, H, Tq, n_sel), s_own], axis=-1)
    p = jax.nn.softmax(s, axis=-1).astype(v_own.dtype)
    o = (jnp.einsum('bhqjk,bhqjkd->bhqd', p[..., :n_sel].reshape(B, H, Tq, KS, MOBA_BLOCK), v_sel,
                    preferred_element_type=jnp.float32)
         + jnp.einsum('bhqk,bkhd->bhqd', p[..., n_sel:], v_own, preferred_element_type=jnp.float32))
    return o.astype(q.dtype)

def moba_prompt(q, k, v, slopes):
    B, T, H, D = q.shape
    nb = -(-T // MOBA_BLOCK)
    pad = ((0, 0), (0, nb * MOBA_BLOCK - T), (0, 0), (0, 0))
    kb = jnp.pad(k, pad).reshape(B, nb, MOBA_BLOCK, H, D)
    vb = jnp.pad(v, pad).reshape(B, nb, MOBA_BLOCK, H, D)
    k_mean = jnp.mean(kb.astype(jnp.float32), axis=2)
    qh = q.transpose(0, 2, 1, 3)
    bi = jnp.arange(B)[:, None, None, None]
    hi = jnp.arange(H)[None, :, None, None]

    def chunk(c):
        start = c * Q_CHUNK
        q_c = lax.dynamic_slice_in_dim(qh, start, Q_CHUNK, axis=2)
        q_pos = start + jnp.arange(Q_CHUNK, dtype=jnp.int32)
        idx, valid = moba_select(q_c, q_pos, k_mean)
        k_sel = kb[bi, idx, :, hi, :]
        v_sel = vb[bi, idx, :, hi, :]
        ob = start // MOBA_BLOCK
        k_own = lax.dynamic_index_in_dim(kb, ob, axis=1, keepdims=False)
        v_own = lax.dynamic_index_in_dim(vb, ob, axis=1, keepdims=False)
        return moba_attend(q_c, q_pos, k_sel, v_sel, idx, valid, k_own, v_own, ob * MOBA_BLOCK, slopes)

    o = lax.map(chunk, jnp.arange(T // Q_CHUNK, dtype=jnp.int32))
    return o.transpose(1, 0, 3, 2, 4).reshape(B, T, H * D)

def moba_sample(q, k_new, v_new, cache_k, cache_v, page_table, slopes):
    DB, Tn, H, D = q.shape
    n_pages = page_table.shape[1]
    past = n_pages * PAGE_SIZE
    k_past = cache_k[page_table].reshape(DB, past, H, D)
    L = past + Tn
    nb = -(-L // MOBA_BLOCK)
    kb = jnp.pad(jnp.concatenate([k_past, k_new.astype(k_past.dtype)], axis=1),
                 ((0, 0), (0, nb * MOBA_BLOCK - L), (0, 0), (0, 0))).reshape(DB, nb, MOBA_BLOCK, H, D)
    k_mean = jnp.mean(kb.astype(jnp.float32), axis=2)
    qh = q.transpose(0, 2, 1, 3)
    q_pos = past + jnp.arange(Tn, dtype=jnp.int32)
    idx, valid = moba_select(qh, q_pos, k_mean)
    KS = idx.shape[-1]
    bi = jnp.arange(DB)[:, None, None, None]
    hi = jnp.arange(H)[None, :, None, None]
    k_sel = kb[bi, idx, :, hi, :]
    ppb = MOBA_BLOCK // PAGE_SIZE
    lp = jnp.minimum(idx[..., None] * ppb + jnp.arange(ppb), n_pages - 1)
    phys = page_table[bi[..., None], lp]
    v_sel = cache_v[phys, :, hi[..., None], :].reshape(DB, H, Tn, KS, MOBA_BLOCK, D)
    ob = past // MOBA_BLOCK
    own_start = ob * MOBA_BLOCK
    k_own = kb[:, ob]
    v_own_past = cache_v[page_table[:, own_start // PAGE_SIZE:]].reshape(DB, past - own_start, H, D)
    v_own = jnp.pad(jnp.concatenate([v_own_past, v_new.astype(v_own_past.dtype)], axis=1),
                    ((0, 0), (0, MOBA_BLOCK - (past - own_start) - Tn), (0, 0), (0, 0)))
    o = moba_attend(qh, q_pos, k_sel, v_sel, idx, valid, k_own, v_own, own_start, slopes)
    return o.transpose(0, 2, 1, 3).reshape(DB, Tn, H * D)

def pool_mixer(u, hist, start_pos, w_pool, pool_scale):
    B, T, C = u.shape
    uf = u.astype(jnp.float32)
    ext = jnp.concatenate([hist.astype(jnp.float32), uf], axis=1)
    csum = jnp.concatenate([jnp.zeros((B, 1, C), jnp.float32), lax.cumsum(ext, axis=1)], axis=1)
    pos = start_pos + jnp.arange(T, dtype=jnp.int32)
    outs = []
    for g, w in enumerate(POOL_WINDOWS):
        sl = slice(g * POOL_GROUP_W, (g + 1) * POOL_GROUP_W)
        win_sum = csum[:, POOL_HIST + 1:, sl] - csum[:, POOL_HIST + 1 - w:POOL_HIST + 1 - w + T, sl]
        cnt = jnp.minimum(pos + 1, w).astype(jnp.float32)[None, :, None]
        outs.append(win_sum / cnt - uf[..., sl])
    d = jnp.concatenate(outs, axis=-1).reshape(B, T, N_POOL_GROUPS, POOL_GROUP_W)
    y = jnp.einsum('btgc,gce->btge', d, w_pool.astype(jnp.float32)).reshape(B, T, C) * pool_scale.astype(jnp.float32)
    new_hist = ext[:, -POOL_HIST:]
    return y.astype(u.dtype), new_hist.astype(u.dtype)

def trunk_layer(x, hist, start_pos, attend, norm1_g, w_in, w_pool, pool_scale, w_out,
                norm2_g, w_gate, w_up, w_down):
    B, T, _ = x.shape
    h = rmsnorm(x, norm1_g)
    z = h @ w_in
    q, k, v, u = jnp.split(z, [ATTN_WIDTH, 2 * ATTN_WIDTH, 3 * ATTN_WIDTH], axis=-1)
    q = q.reshape(B, T, N_HEADS, HEAD_DIM)
    k = k.reshape(B, T, N_HEADS, HEAD_DIM)
    v = v.reshape(B, T, N_HEADS, HEAD_DIM)
    a = attend(q, k, v)
    p, new_hist = pool_mixer(u, hist, start_pos, w_pool, pool_scale)
    x = x + jnp.concatenate([a, p.astype(a.dtype)], axis=-1) @ w_out
    h2 = rmsnorm(x, norm2_g)
    x = x + (jax.nn.silu(h2 @ w_gate) * (h2 @ w_up)) @ w_down
    return x, k, v, new_hist

def setup_inputs(seed: int = 0) -> dict:
    key = jax.random.key(seed)
    ks = jax.random.split(key, 16)
    nrm = jax.random.normal
    f32 = jnp.float32
    n_pages = PAST_LEN // PAGE_SIZE
    n_used = DEC_BATCH * n_pages
    n_pool = n_used + n_used // 4
    page_table = jax.random.permutation(ks[5], n_pool)[:n_used].reshape(DEC_BATCH, n_pages).astype(jnp.int32)
    return {
        'x_prompt': nrm(ks[0], (BATCH, SEQ, D_MODEL), f32),
        'x_sample': nrm(ks[1], (DEC_BATCH, DEC_SEQ, D_MODEL), f32),
        'cache_k': nrm(ks[2], (DEPTH, n_pool, PAGE_SIZE, N_HEADS, HEAD_DIM), f32),
        'cache_v': nrm(ks[3], (DEPTH, n_pool, PAGE_SIZE, N_HEADS, HEAD_DIM), f32),
        'state_pool': nrm(ks[4], (DEPTH, DEC_BATCH, POOL_HIST, POOL_WIDTH), f32),
        'page_table': page_table,
        'norm1_g': 1.0 + 0.1 * nrm(ks[6], (DEPTH, D_MODEL), f32),
        'w_in': nrm(ks[7], (DEPTH, D_MODEL, IN_WIDTH), f32) * D_MODEL ** -0.5,
        'w_pool': nrm(ks[8], (DEPTH, N_POOL_GROUPS, POOL_GROUP_W, POOL_GROUP_W), f32) * POOL_GROUP_W ** -0.5,
        'pool_scale': 1.0 + 0.1 * nrm(ks[9], (DEPTH, POOL_WIDTH), f32),
        'w_out': nrm(ks[10], (DEPTH, MIX_WIDTH, D_MODEL), f32) * MIX_WIDTH ** -0.5,
        'norm2_g': 1.0 + 0.1 * nrm(ks[11], (DEPTH, D_MODEL), f32),
        'w_gate': nrm(ks[12], (DEPTH, D_MODEL, D_FF), f32) * D_MODEL ** -0.5,
        'w_up': nrm(ks[13], (DEPTH, D_MODEL, D_FF), f32) * D_MODEL ** -0.5,
        'w_down': nrm(ks[14], (DEPTH, D_FF, D_MODEL), f32) * D_FF ** -0.5,
        'norm_f_g': 1.0 + 0.1 * nrm(ks[15], (D_MODEL,), f32),
    }

def reference(x_prompt, x_sample, cache_k, cache_v, state_pool, page_table, norm1_g, w_in, w_pool,
              pool_scale, w_out, norm2_g, w_gate, w_up, w_down, norm_f_g):
    slopes = alibi_slopes()
    past_len = page_table.shape[1] * PAGE_SIZE
    zero_hist = jnp.zeros((x_prompt.shape[0], POOL_HIST, POOL_WIDTH), x_prompt.dtype)
    hp, hs = x_prompt, x_sample
    kp, vp, sp, ksm, vsm, ssm = [], [], [], [], [], []
    for l in range(DEPTH):
        lw = (norm1_g[l], w_in[l], w_pool[l], pool_scale[l], w_out[l], norm2_g[l],
              w_gate[l], w_up[l], w_down[l])
        hp, k1, v1, s1 = trunk_layer(hp, zero_hist, 0,
                                     lambda q, k, v: moba_prompt(q, k, v, slopes), *lw)
        ck, cv = cache_k[l], cache_v[l]
        hs, k2, v2, s2 = trunk_layer(hs, state_pool[l], past_len,
                                     lambda q, k, v: moba_sample(q, k, v, ck, cv, page_table, slopes), *lw)
        kp.append(k1); vp.append(v1); sp.append(s1)
        ksm.append(k2); vsm.append(v2); ssm.append(s2)
    y_prompt = rmsnorm(hp, norm_f_g)
    y_sample = rmsnorm(hs, norm_f_g)
    k_prompt = jnp.stack(kp)
    v_prompt = jnp.stack(vp)
    pool_prompt = jnp.stack(sp)
    k_sample = jnp.stack(ksm)
    v_sample = jnp.stack(vsm)
    pool_sample = jnp.stack(ssm)
    return (y_prompt, y_sample, k_prompt, v_prompt, pool_prompt, k_sample, v_sample, pool_sample)


_drawn_inputs = setup_inputs


def setup_inputs(seed=0):
    import zlib

    import numpy as np

    out = dict(_drawn_inputs(seed))
    spreads = {}
    factors = {}
    for name, (base, spread) in spreads.items():
        noise = np.random.default_rng([zlib.crc32(name.encode()), seed]).standard_normal(out[name].shape)
        drawn = base * np.exp(spread * noise) if base else spread * noise
        out[name] = __import__('jax').numpy.asarray(drawn.astype(out[name].dtype))
    for name, factor in factors.items():
        out[name] = (out[name] * factor).astype(out[name].dtype)
    return out
```

```python
from contextlib import ExitStack

import numpy as np

import concourse.bass as bass
from concourse import mybir

F32 = mybir.dt.float32
F32R = mybir.dt.float32r
I32 = mybir.dt.int32
ALU = mybir.AluOpType
ACT = mybir.ActivationFunctionType
AX = mybir.AxisListType

P = 128
D = 2048
KC = D // P
TP = 256
NB, NQ = 8, 4
TS = NB * NQ
T = TP + TS
H, DH = 8, 128
AW = H * DH
NPAGES = 16
NQUADS = NPAGES // 4
PAST = NPAGES * P
FF = 5632
NG = FF // 512
HIST = 15
WINDOWS = (2, 4, 8, 16)
EPS = 1e-6
SCALE = DH ** -0.5
NEG = -1e30
TOPK = 3
ZQ, ZK, ZV, ZU = 0, 8, 16, 24
T_Q = 0
T_KVU = T_Q + 16
T_OUT = T_KVU + 8 * NB
T_FF = T_OUT + 32
T_END = T_FF + 24 * NG
CW = 384
SLOTS = 4
TE = 2 * 512
QT0 = 4
QT = QT0 + 8
DVE_STEPS = 15


def tables():
    p = np.arange(P)
    g, h, q = p // 32, (p // 4) % H, p % NQ
    slope = 2.0 ** -(h + 1.0)
    j4, r, n8 = np.arange(4), np.arange(P), np.arange(8)
    key = (4 * j4[None, :, None] + g[:, None, None]) * P + r[None, None, :]
    t16 = np.arange(16)
    qi, ki = p[:, None], np.arange(TP)[None, :]
    parts = {
        "ident": np.eye(P),
        "ones": np.ones((P, P)),
        "same": (p[:, None] % 32 == p[None, :] % 32),
        "headsel": (h[:, None, None] == n8[None, :, None]) & (p[:, None, None] % 32 == np.arange(32)),
        "past_bias": slope[:, None, None] * (key - (PAST + q[:, None, None])),
        "half": (g[:, None] // 2 == np.arange(2)),
        "gsel": (g[:, None] == j4[None, :]),
        "before": n8[None, None, :] < (2 * j4[None, :, None] + g[:, None, None] // 2),
        "own_bias": np.where(np.arange(NQ) <= q[:, None], slope[:, None] * (np.arange(NQ) - q[:, None]), NEG),
        "batch_of": (p[:, None] // NQ == n8[None, :]),
        "rel": np.concatenate(
            [np.where(ki[:, :P] <= qi, ki[:, :P] - qi, -1e33), np.where(ki <= qi + P, ki - (qi + P), -1e33)], 1),
        "inv_count": np.broadcast_to(1.0 / np.minimum(t16 + 1, np.array(WINDOWS)[:, None]), (P, 4, 16)),
    }
    at, cols = {}, 0
    flat = []
    for name, a in parts.items():
        a = np.asarray(a, np.float64).reshape(P, -1)
        at[name] = (cols, cols + a.shape[1])
        cols += a.shape[1]
        flat.append(a)
    return np.concatenate(flat, 1).astype(np.float32), at


class Steps:

    def __init__(self, eng, sem):
        self.eng, self.sem, self.base, self.k = eng, sem, 0, 0

    def did(self, ins):
        ins.then_inc(self.sem, 1)
        self.k += 1

    def settle(self):
        self.eng.wait_ge(self.sem, self.base + self.k)

    def link(self, ins):
        self.did(ins)
        self.settle()


def tile_at(k, i=0, per=0):
    return k + per * i, k // SLOTS + (per // SLOTS) * i, k % SLOTS


def step_program(nc, A, O, at):
    ctx = ExitStack()
    with ctx:
        def sem(name):
            return ctx.enter_context(nc.semaphore(name))

        def sb(name, shape, dt=F32, stack=None):
            return (stack or ctx).enter_context(nc.sbuf_tensor(name, shape, dt))

        tab = sb("tab", [P, A["tables"].shape[1]])
        xT = sb("xT", [P, KC, T])
        hh = sb("hh", [P, KC, T], F32R)
        hl = sb("hl", [P, KC, T], F32R)
        w_raw = sb("w_raw", [P, SLOTS, TE])
        w_hi = sb("w_hi", [P, SLOTS, TE], F32R)
        w_lo = sb("w_lo", [P, SLOTS, TE], F32R)
        gains = sb("gains", [P, 40])
        rstd = sb("rstd", [P, T])
        sq = sb("sq", [P, 2, T])
        nrm = sb("nrm", [P, 2, T])
        mid = ExitStack()
        z = sb("z", [P, 32, T], stack=mid)
        o_all = sb("o_all", [32, NB, DH], stack=mid)
        m_all = sb("m_all", [32, NB], stack=mid)
        l_all = sb("l_all", [32, NB], stack=mid)
        kv = ExitStack()
        kpage = sb("kpage", [P, 2, 4, AW], stack=kv)
        vpage = sb("vpage", [P, 4, AW], stack=kv)
        kT = sb("kT", [P, 2, 512], stack=kv)
        ss = sb("ss", [P, 4, P], stack=kv)
        pT = sb("pT", [P, 4, P], stack=kv)
        osb = sb("osb", [P, AW], stack=kv)
        qz = sb("qz", [P, H * 36], stack=kv)
        pages = sb("pages", [1, NB * NPAGES], I32, stack=kv)
        d4 = sb("d4", [P, 4], stack=kv)
        dn = sb("dn", [P, 4, 2], stack=kv)
        bsc = sb("bsc", [P, 8], stack=kv)
        bsh = sb("bsh", [P, 4, 2], stack=kv)
        bown = sb("bown", [P, 4], stack=kv)
        gt = sb("gt", [P, 4, 8], stack=kv)
        eq = sb("eq", [P, 4, 8], stack=kv)
        cnt = sb("cnt", [P, 4], stack=kv)
        mx = sb("mx", [P, 1], stack=kv)
        dm = sb("dm", [P, 4], stack=kv)
        negm = sb("negm", [P, 1], stack=kv)
        lsum = sb("lsum", [P, 1], stack=kv)
        kv.close()
        pre = ExitStack()
        xs = sb("xs", [P, 3, D], stack=pre)
        vec = sb("vec", [40, P], stack=pre)
        pre.close()
        post = ExitStack()
        ktok = sb("ktok", [P, 2, AW], stack=post)
        vtok = sb("vtok", [P, 2, AW], stack=post)
        stok = sb("stok", [P, AW], stack=post)
        qza = sb("qza", [P, NB, H * 36], stack=post)
        rbias = sb("rbias", [P, 2, 384], stack=post)
        px = sb("px", [P, 2, 384], stack=post)
        ptp = sb("ptp", [P, 2, 384], stack=post)
        pm = sb("pm", [P, 2, 2], stack=post)
        pl = sb("pl", [P, 2, 2], stack=post)
        wpool = sb("wpool", [P, 4, 2, 256], stack=post)
        hist = sb("hist", [NB * HIST, AW], stack=post)
        ext = sb("ext", [P, 8, NB, HIST + NQ], stack=post)
        win = sb("win", [P, 2, 2, TP], stack=post)
        wins = sb("wins", [P, 2, 2, NB, HIST + NQ], stack=post)
        dpool = sb("dpool", [P, 2, 2, T], stack=post)
        so = sb("so", [32, NB, NQ], stack=post)
        mo = sb("mo", [32, NB], stack=post)
        mm_ = sb("mm_", [32, NB], stack=post)
        eo = sb("eo", [32, NB], stack=post)
        lo_ = sb("lo_", [32, NB], stack=post)
        pTo = sb("pTo", [32, 32], stack=post)
        pTb = sb("pTb", [32, H, NB, NQ], stack=post)
        t1 = sb("t1", [P, NB, 32], stack=post)
        mixs = sb("mixs", [P, H, TS], stack=post)
        post.close()
        mid.close()
        late = ExitStack()
        sg = sb("sg", [P, 4, T], stack=late)
        af = sb("af", [P, 2, T], stack=late)
        ah = sb("ah", [P, 4, T], F32R, stack=late)
        al = sb("al", [P, 4, T], F32R, stack=late)
        gf = sb("gf", [P, D], stack=late)
        yt = sb("yt", [P, 3, D], stack=late)
        rf = sb("rf", [P, 3], stack=late)
        late.close()

        bank = [ctx.enter_context(nc.psum_tensor(f"bank{n}", [P, 512], F32)) for n in range(8)]
        WB = bank[0:3]
        KTP = bank[3:5]
        S = bank[5]
        OB = bank[6:8]

        def tb(name):
            a, b = at[name]
            return tab[:, a:b]

        ident, ones, same = tb("ident"), tb("ones"), tb("same")
        headsel = tb("headsel").rearrange("p (h c) -> p h c", h=H)
        past_bias = tb("past_bias")
        half = tb("half")
        before = tb("before").rearrange("p (j m) -> p j m", j=4)
        inv_count = tb("inv_count").rearrange("p (g t) -> p g t", g=4)

        tab_in, x_in, vec_in, pages_in = sem("tab_in"), sem("x_in"), sem("vec_in"), sem("pages_in")
        w_in_s = [sem(f"w_slot{n}_in") for n in range(SLOTS)]
        hi_ready, lo_ready, w_used = sem("hi_ready"), sem("lo_ready"), sem("w_used")
        k_in = [sem("k_in0"), sem("k_in1")]
        v_in = sem("v_in")
        vecT, gains_ready = sem("vec_transposed"), sem("gains_ready")
        xT_in, x_ready = sem("x_transposed"), sem("x_ready")
        sq_ready, sq_used = sem("sq_ready"), sem("sq_used")
        ms_ready, root_ready = sem("ms_ready"), sem("root_ready")
        nrm_ready, nrm_hi, h_ready = sem("nrm_ready"), sem("nrm_hi"), sem("h_ready")
        z_ready = sem("z_ready")
        qz_ready = sem("qz_ready")
        kt_in, kt_out, qk_done = sem("kt_in"), sem("kt_out"), sem("qk_done")
        dn_ready, bs_done = sem("dn_ready"), sem("bs_done")
        dm_ready, mx_done, m_ready = sem("dm_ready"), sem("mx_done"), sem("m_ready")
        p_ready, l_done, l_saved = sem("p_ready"), sem("l_done"), sem("l_saved")
        pt_in, pt_ready, v_done = sem("pt_in"), sem("pt_ready"), sem("v_done")
        o6_taken, o7_taken = sem("o6_taken"), sem("o7_taken")
        comb_done, comb_saved = sem("comb_done"), sem("comb_saved")
        tok_in, tok_act, tok_dve = sem("tok_in"), sem("tok_act"), sem("tok_dve")
        late_in, hist_in, wpool_in, gf_in = sem("late_in"), sem("hist_in"), sem("wpool_in"), sem("gf_in")
        hist_T, ext_ready = sem("hist_transposed"), sem("ext_ready")
        a_in, a_out = sem("a_in"), sem("a_out")
        rb_ready, pm_ready, pe_ready, pn_ready = sem("rbias_ready"), sem("pm_ready"), sem("pexp_ready"), sem("pn_ready")
        pt2_in, pt2_ready, po_in = sem("ptp_in"), sem("ptp_ready"), sem("po_in")
        po_hi, mix_ready = sem("po_hi"), sem("mix_ready")
        d_ready, y_in, y_sc, y_hi, pool_mix = sem("d_ready"), sem("y_in"), sem("y_scaled"), sem("y_hi"), sem("pool_mix")
        qza_ready, so_in, so_sub, so_exp = sem("qza_ready"), sem("so_in"), sem("so_sub"), sem("so_exp")
        own_ready, pTo_in, pTb_ready, t1_in, t2_in = (
            sem("own_ready"), sem("pTo_in"), sem("pTb_ready"), sem("t1_in"), sem("t2_in"))
        smix, smix_hi, smix_ready = sem("smix"), sem("smix_hi"), sem("smix_ready")
        quad_taken = [sem("quadA_taken"), sem("quadB_taken")]
        sg_ready, af_ready, ah_ready, act_ready = sem("sg_ready"), sem("af_ready"), sem("ah_ready"), sem("act_ready")
        fms, froot = sem("fms"), sem("froot")
        fy_in, fy_out = sem("fy_in"), sem("fy_out")
        dve_own, act_own, pool_own = sem("dve_own"), sem("act_own"), sem("pool_own")
        stored = sem("stored")

        ck = A["cache_k"][0].rearrange("n t h d -> n t (h d)")
        cv = A["cache_v"][0].rearrange("n t h d -> n t (h d)")
        w_in_d, w_out_d = A["w_in"][0], A["w_out"][0]
        wg_d, wu_d, wd_d = A["w_gate"][0], A["w_up"][0], A["w_down"][0]

        def tok_dst(n):
            half_ = n % 2
            kind, part = (n // 2) // 3, (n // 2) % 3
            cols = slice(512 * half_, 512 * half_ + 512)
            if kind < 2 and part < 2:
                return P, (vtok, ktok)[kind][:, part, cols]
            rows, at_ = ((TS, 32 * kind), (TS, 64), (HIST, 96))[0 if kind < 2 else 1 + part]
            return rows, stok[at_:at_ + rows, cols]

        def tok_src(n):
            half_ = n % 2
            kind, part = (n // 2) // 3, (n // 2) % 3
            chunk = (ZV, ZK, ZU)[kind] + 4 * half_
            if kind < 2:
                a = P * part
                return chunk, a, a + (P if part < 2 else TS)
            return (chunk, TP, T) if part == 0 else (chunk, TP - HIST, TP)

        block = ctx.enter_context(nc.Block())

        @block.sync
        def _(sp):
            xp, xsam = A["x_prompt"][0], A["x_sample"].rearrange("b q d -> (b q) d")
            sp.dma_start(tab[:, :], A["tables"]).then_inc(tab_in, 16)
            for n in range(2):
                sp.dma_start(xs[:, n, :], xp[n * P:(n + 1) * P, :]).then_inc(x_in, 16)
            sp.dma_start(xs[0:TS, 2, :], xsam).then_inc(x_in, 16)
            sp.dma_start(vec[0:16, :], A["norm1_g"][0].rearrange("(c p) -> c p", p=P)).then_inc(vec_in, 16)
            sp.dma_start(vec[16:32, :], A["norm2_g"][0].rearrange("(c p) -> c p", p=P)).then_inc(vec_in, 16)
            sp.dma_start(vec[32:40, :], A["pool_scale"][0].rearrange("(c p) -> c p", p=P)).then_inc(vec_in, 16)

            def load(t, src, free=True):
                n, _, s = t
                if free:
                    sp.wait_ge(lo_ready, n - 3)
                w = src.shape[1]
                sp.dma_start(w_raw[:, s, 0:2 * w].rearrange("p (k n) -> p k n", k=2),
                             src.rearrange("(k p) n -> p k n", p=P)).then_inc(w_in_s[s], 16)

            for k in range(16):
                c, j = k // 8, k % 8
                load(tile_at(T_Q + k), w_in_d[256 * j:256 * j + 256, 512 * c:512 * c + 512], free=k >= SLOTS)
            sp.wait_ge(xT_in, KC)
            sp.wait_ge(vecT, 1)
            sp.dma_start(pages[:, :], A["page_table"].rearrange("b n -> (b n)").rearrange("(a n) -> a n", a=1)
                         ).then_inc(pages_in, 16)
            sp.wait_ge(pages_in, 16)

            def page(pool, b, n):
                e = NPAGES * b + n
                idx = sp.value_load(pages[0:1, bass.ds(e, 1)], min_val=0, max_val=pool.shape[0] - 1)
                return pool[bass.ds(idx, 1), :, :].rearrange("a t n -> (a t) n")

            def stream(i, has_k, has_v, first=False):
                for j in range(NQUADS):
                    if has_k:
                        if not (first and j < 2):
                            sp.wait_ge(kt_in, 32 * i + 8 * j - 8)
                        for g in range(4):
                            sp.dma_start(kpage[:, j % 2, g, :], page(ck, i, 4 * j + g)).then_inc(k_in[j % 2], 16)
                        for k in (2 * j, 2 * j + 1):
                            src = w_in_d[256 * k:256 * k + 256, bass.ds(AW + CW * i, CW)]
                            load(tile_at(T_KVU + k, i, 8), src)
                    if has_v:
                        if not (first and j == 0):
                            sp.wait_ge(v_done, 4 * i + j - 4)
                        for g in range(4):
                            sp.dma_start(vpage[:, g, :], page(cv, i - 1, 4 * j + g)).then_inc(v_in, 16)

            stream(0, True, False, first=True)
            for j in range(NQUADS):
                sp.wait_ge(kt_in, 32 + 8 * j - 8)
                for g in range(4):
                    sp.dma_start(kpage[:, j % 2, g, :], page(ck, 1, 4 * j + g)).then_inc(k_in[j % 2], 16)
                for k in (2 * j, 2 * j + 1):
                    load(tile_at(T_KVU + k, 1, 8), w_in_d[256 * k:256 * k + 256, AW + CW:AW + 2 * CW])
                if j:
                    sp.wait_ge(v_done, j)
                for g in range(4):
                    sp.dma_start(vpage[:, g, :], page(cv, 0, 4 * j + g)).then_inc(v_in, 16)
            with sp.Fori(2, NB) as i:
                stream(i, True, True)
            stream(NB, False, True)

            def load_out(k):
                c, j = k // 8, k % 8
                load(tile_at(T_OUT + k), w_out_d[256 * j:256 * j + 256, 512 * c:512 * c + 512])

            for k in range(4):
                load_out(k)
            sp.wait_ge(comb_done, NB)
            sp.dma_start(hist[:, :], A["state_pool"][0].rearrange("b i c -> (b i) c")).then_inc(hist_in, 16)
            sp.dma_start(wpool[:, :, :, :], A["w_pool"][0].rearrange("g (k p) e -> p g k e", p=P)).then_inc(wpool_in, 16)
            for k in range(4, 8):
                load_out(k)
            n_stores = 0

            def store(dst, src):
                nonlocal n_stores
                sp.dma_start(dst, src).then_inc(stored, 16)
                n_stores += 1

            kp, vp = O["k_prompt"][0, 0].rearrange("t h d -> t (h d)"), O["v_prompt"][0, 0].rearrange("t h d -> t (h d)")
            ks = O["k_sample"][0].rearrange("b q h d -> (b q) (h d)")
            vs = O["v_sample"][0].rearrange("b q h d -> (b q) (h d)")
            sp.wait_ge(tok_act, 8)
            sp.wait_ge(tok_dve, 8)
            for n in range(2):
                store(kp[n * P:(n + 1) * P, :], ktok[:, n, :])
                store(vp[n * P:(n + 1) * P, :], vtok[:, n, :])
            store(vs, stok[0:TS, :])
            store(ks, stok[TS:2 * TS, :])
            store(O["pool_prompt"][0, 0], stok[96:96 + HIST, :])
            store(O["pool_sample"][0, :, 0:HIST - NQ, :], A["state_pool"][0, :, NQ:HIST, :])
            for b in range(NB):
                store(O["pool_sample"][0, b, HIST - NQ:HIST, :], stok[64 + NQ * b:64 + NQ * b + NQ, :])
            for k in range(8, 16):
                load_out(k)
            with sp.Fori(1, 2) as i:
                for k in range(16):
                    src = w_out_d[256 * (k % 8):256 * (k % 8) + 256, bass.ds(1024 * i + 512 * (k // 8), 512)]
                    load(tile_at(T_OUT + k, i, 16), src)

            def load_gu(w, t0, g):
                for k in range(8):
                    load(tile_at(*((t0[0] + k,) + t0[1:])), w[256 * k:256 * k + 256, bass.ds(512 * g, 512)])

            def load_down(t0, g):
                for k in range(8):
                    c, j = k // 2, k % 2
                    load(tile_at(*((t0[0] + k,) + t0[1:])),
                         wd_d[bass.ds(512 * g + 256 * j, 256), 512 * c:512 * c + 512])

            load_gu(wg_d, (T_FF,), 0)
            with sp.Fori(0, NG - 1) as g:
                load_gu(wu_d, (T_FF + 8, g, 24), g)
                load_gu(wg_d, (T_FF + 16, g, 24), g + 1)
                load_down((T_FF + 24, g, 24), g)
            load_gu(wu_d, (T_END - 16,), NG - 1)
            sp.dma_start(gf[:, :], A["norm_f_g"].partition_broadcast(P)).then_inc(gf_in, 16)
            load_down((T_END - 8,), NG - 1)
            for n in range(3):
                rows = P if n < 2 else TS
                sp.wait_ge(fy_out, 4 * n + 4)
                dst = O["y_prompt"][0, n * P:(n + 1) * P, :] if n < 2 else O["y_sample"].rearrange("b q d -> (b q) d")
                store(dst, yt[0:rows, n, :])
            sp.wait_ge(stored, 16 * n_stores)

        @block.scalar
        def _(act):
            own = Steps(act, act_own)

            def copy(out, in_):
                return nc.scalar.activation(out, in_, ACT.Copy)

            def hi(t, free=True):
                n, turn, s = t
                act.wait_ge(w_in_s[s], 16 * turn + 16)
                if free:
                    act.wait_ge(w_used, n - 3)
                copy(w_hi[:, s, :], w_raw[:, s, :]).then_inc(hi_ready, 1)

            def norm(stage):
                for c in range(KC):
                    n = KC * stage + c
                    if stage == 0:
                        act.wait_ge(x_ready, c + 1)
                    else:
                        act.wait_ge(quad_taken[c // 4 % 2], QT0 + 4 * (c // 8) + c % 4 + 1)
                    if n >= 2:
                        act.wait_ge(sq_used, n - 1)
                    nc.scalar.activation(sq[:, c % 2, :], xT[:, c, :], ACT.Square).then_inc(sq_ready, 1)
                act.wait_ge(ms_ready, stage + 1)
                nc.scalar.activation(rstd[:, :], rstd[:, :], ACT.Sqrt).then_inc(root_ready, 1)
                for c in range(KC):
                    act.wait_ge(nrm_ready, KC * stage + c + 1)
                    copy(hh[:, c, :], nrm[:, c % 2, :]).then_inc(nrm_hi, 1)

            for k in range(SLOTS):
                hi(tile_at(k), False)
            norm(0)
            for k in range(SLOTS, 16):
                hi(tile_at(k))

            def kv_step(i, has_k, has_v, has_comb, first=False):
                for j in range(NQUADS):
                    if j == 0 and has_v and not has_k:
                        softmax_early(i, has_comb)
                        softmax_late(i)
                    if has_k:
                        for h in range(H):
                            n = 32 * i + 8 * j + h
                            act.wait_ge(kt_in, n + 1)
                            if not (first and j == 0 and h < 2):
                                act.wait_ge(qk_done, n - 1)
                            copy(kT[:, h % 2, :], KTP[h % 2][:, :]).then_inc(kt_out, 1)
                            if j == 0 and h == 4 and has_v:
                                softmax_early(i, has_comb)
                        if j == 0 and has_v:
                            softmax_late(i)
                if has_v:
                    act.wait_ge(v_done, 4 * i)
                    if has_comb:
                        act.wait_ge(comb_done, i - 1)
                    copy(osb[:, 0:512], OB[0][:, :]).then_inc(o6_taken, 1)

            def softmax_early(i, has_comb):
                if has_comb:
                    save_comb(i - 2, i - 1)

            def save_comb(b, count):
                act.wait_ge(comb_done, count)
                copy(o_all[:, bass.ds(b, 1), :].rearrange("p a d -> p (a d)"), OB[0][0:32, 0:DH]).then_inc(comb_saved, 1)

            def softmax_late(i):
                act.wait_ge(m_ready, i)
                nc.scalar.activation(ss[:, :, :], ss[:, :, :], ACT.Exp, bias=negm[:, 0:1],
                                     accum_out=lsum[:, 0:1]).then_inc(p_ready, 1)
                act.wait_ge(pt_in, i)
                copy(pT[:, :, :], OB[0][:, :].rearrange("p (j k) -> p j k", j=4)).then_inc(pt_ready, 1)

            kv_step(0, True, False, False, first=True)
            kv_step(1, True, True, False)
            with act.Fori(2, NB) as i:
                kv_step(i, True, True, True)
            kv_step(NB, False, True, True)
            save_comb(NB - 1, NB)

            for n in range(0, 16, 2):
                act.wait_ge(tok_in, n + 1)
                rows, dst = tok_dst(n)
                copy(dst, bank[n % 4][0:rows, :]).then_inc(tok_act, 1)
            for k in range(SLOTS):
                hi(tile_at(T_OUT + k))
            for s in range(H + 2):
                if s < H:
                    if s >= 2:
                        act.wait_ge(a_out, s - 1)
                    nc.scalar.activation(rbias[:, s % 2, :], tb("rel"), ACT.Copy,
                                         scale=2.0 ** -(s + 1)).then_inc(rb_ready, 1)
                    act.wait_ge(pm_ready, 2 * s + 2)
                    for n, (a, b) in enumerate(((0, P), (P, 384))):
                        nc.scalar.activation(px[:, s % 2, a:b], px[:, s % 2, a:b], ACT.Exp,
                                             bias=pm[:, s % 2, n:n + 1],
                                             accum_out=pl[:, s % 2, n:n + 1]).then_inc(pe_ready, 1)
                if 1 <= s <= H:
                    act.wait_ge(pt2_in, s)
                    if s >= 3:
                        act.wait_ge(po_in, s - 2)
                    copy(ptp[:, (s - 1) % 2, :], bank[6 + (s - 1) % 2][:, 0:384]).then_inc(pt2_ready, 1)
                if s >= 2:
                    act.wait_ge(po_in, s - 1)
                    copy(hh[:, s - 2, 0:TP], bank[2 + s % 2][:, 0:TP]).then_inc(po_hi, 1)
            act.wait_ge(so_sub, 2)
            nc.scalar.activation(so[:, :, :], so[:, :, :], ACT.Exp).then_inc(so_exp, 1)
            nc.scalar.activation(eo[:, :], eo[:, :], ACT.Exp).then_inc(so_exp, 1)
            for n in range(8):
                act.wait_ge(y_sc, n + 1)
                copy(hh[:, 8 + n, :], nrm[:, n % 2, :]).then_inc(y_hi, 1)
            act.wait_ge(smix, 1)
            copy(hh[:, 0:H, TP:T], mixs[:, :, :]).then_inc(smix_hi, 1)
            with act.Fori(0, 2) as i:
                for k in range(16):
                    hi(tile_at(T_OUT + 4 + k, i, 16))
            norm(1)

            def silu(base):
                act.wait_ge(w_used, base)
                for m in range(4):
                    nc.scalar.activation(sg[:, m, :], bank[m][:, 0:T], ACT.Silu).then_inc(sg_ready, 1)

            def act_hi(g):
                for m in range(4):
                    act.wait_ge(af_ready, 4 * g + m + 1)
                    copy(ah[:, m, :], af[:, m % 2, :]).then_inc(ah_ready, 1)

            for k in range(8):
                hi(tile_at(T_FF + 4 + k))
            silu(T_FF + 8)
            with act.Fori(0, NG - 1) as g:
                for k in range(24):
                    hi(tile_at(T_FF + 12 + k, g, 24))
                    if k == 7:
                        act_hi(g)
                    if k == 15:
                        act.wait_ge(af_ready, 4 * g + 4)
                        silu(T_FF + 24 + 24 * g)
            for k in range(12):
                hi(tile_at(T_END - 12 + k))
                if k == 7:
                    act_hi(NG - 1)
            for c in range(KC):
                act.wait_ge(x_ready, KC + c + 1)
                act.wait_ge(sq_used, 2 * KC + c - 1)
                nc.scalar.activation(sq[:, c % 2, :], xT[:, c, :], ACT.Square).then_inc(sq_ready, 1)
            act.wait_ge(fms, 3)
            nc.scalar.activation(rf[:, :], rf[:, :], ACT.Sqrt).then_inc(froot, 1)

        @block.vector
        def _(dve):
            own = Steps(dve, dve_own)
            V = nc.vector

            def lo(t, width=TE):
                n, _, s = t
                dve.wait_ge(hi_ready, n + 1)
                V.tensor_tensor(w_lo[:, s, 0:width], w_raw[:, s, 0:width], w_hi[:, s, 0:width].bitcast(F32),
                                ALU.subtract).then_inc(lo_ready, 1)

            def hi_lo(t):
                n, turn, s = t
                dve.wait_ge(w_in_s[s], 16 * turn + 16)
                dve.wait_ge(w_used, n - 3)
                V.tensor_copy(w_hi[:, s, 0:2 * CW], w_raw[:, s, 0:2 * CW]).then_inc(hi_ready, 1)
                lo(t, 2 * CW)

            def norm(stage):
                dve.wait_ge(sq_used, KC * stage + KC)
                V.tensor_scalar(rstd[:, :], bank[7][:, 0:T], 1.0 / D, EPS, ALU.mult, ALU.add).then_inc(ms_ready, 1)
                dve.wait_ge(root_ready, stage + 1)
                own.link(V.reciprocal(rstd[:, :], rstd[:, :]))

                def scaled(c):
                    if KC * stage + c >= 2:
                        dve.wait_ge(h_ready, KC * stage + c - 1)
                    V.scalar_tensor_tensor(nrm[:, c % 2, :], xT[:, c, :], gains[:, 16 * stage + c:16 * stage + c + 1],
                                           rstd[:, :], ALU.mult, ALU.mult).then_inc(nrm_ready, 1)

                scaled(0)
                for c in range(KC):
                    if c + 1 < KC:
                        scaled(c + 1)
                    dve.wait_ge(nrm_hi, KC * stage + c + 1)
                    V.tensor_tensor(hl[:, c, :], nrm[:, c % 2, :], hh[:, c, :].bitcast(F32),
                                    ALU.subtract).then_inc(h_ready, 1)

            for k in range(SLOTS):
                lo(tile_at(k))
            dve.wait_ge(vecT, 1)
            V.tensor_copy(gains[:, :], bank[6][:, 0:40]).then_inc(gains_ready, 1)
            dve.wait_ge(gains_ready, 1)
            for c in range(KC):
                dve.wait_ge(xT_in, c + 1)
                V.tensor_copy(xT[:, c, :], bank[c % 4][:, 0:T]).then_inc(x_ready, 1)
            norm(0)
            own.link(V.memset(qz[:, :], 0.0))
            for k in range(16):
                if k < 12:
                    lo(tile_at(4 + k))
                if k % 8 == 7:
                    c = k // 8
                    dve.wait_ge(w_used, T_Q + 8 * c + 8)
                    for m in range(4):
                        V.tensor_copy(z[:, 4 * c + m, :], bank[4 * c + m][:, 0:T]).then_inc(quad_taken[c], 1)
            for c in range(2):
                dve.wait_ge(quad_taken[c], QT0)

            def pad_q(b):
                cols = bass.ds(TP + NQ * b, NQ)
                return V.tensor_copy(qz[:, :].rearrange("p (h s) -> p h s", s=36)[:, :, 0:NQ], z[:, ZQ:ZQ + H, cols])

            def kv_step(i, has_k, has_v, has_comb, first=False):
                if has_v:
                    dve.wait_ge(qk_done, 32 * i)
                if has_k:
                    pad_q(i).then_inc(qz_ready, 1)
                if has_v:
                    if has_comb:
                        dve.wait_ge(pt_in, i - 1)
                    own.did(V.scalar_tensor_tensor(ss[:, :, :].rearrange("p j k -> p (j k)"), S[:, :], SCALE, past_bias,
                                                   ALU.mult, ALU.add))
                    own.did(V.tensor_reduce(d4[:, :], S[:, :].rearrange("p (j k) -> p j k", j=4), AX.X, ALU.add))
                    own.settle()
                    V.tensor_tensor(dn[:, :, :], d4[:, :].unsqueeze(2).to_broadcast([P, 4, 2]),
                                    half.unsqueeze(1).to_broadcast([P, 4, 2]), ALU.mult).then_inc(dn_ready, 1)
                    dve.wait_ge(bs_done, i)
                    own.link(V.tensor_copy(bsc[:, :], OB[1][:, 0:8]))
                    own.link(V.tensor_tensor(bsh[:, :, :], bsc[:, :].rearrange("p (j u) -> p j u", u=2),
                                             half.unsqueeze(1).to_broadcast([P, 4, 2]), ALU.mult))
                    own.link(V.tensor_reduce(bown[:, :], bsh[:, :, :], AX.X, ALU.add))
                    every = bsc[:, :].unsqueeze(1).to_broadcast([P, 4, 8])
                    mine = bown[:, :].unsqueeze(2).to_broadcast([P, 4, 8])
                    own.did(V.tensor_tensor(gt[:, :, :], every, mine, ALU.is_gt))
                    own.link(V.tensor_tensor(eq[:, :, :], every, mine, ALU.is_equal))
                    own.link(V.tensor_tensor(eq[:, :, :], eq[:, :, :], before, ALU.mult))
                    own.link(V.tensor_tensor(gt[:, :, :], gt[:, :, :], eq[:, :, :], ALU.add))
                    own.link(V.tensor_reduce(cnt[:, :], gt[:, :, :], AX.X, ALU.add))
                    own.link(V.tensor_scalar(cnt[:, :], cnt[:, :], float(TOPK), NEG, ALU.is_ge, ALU.mult))
                    own.link(V.tensor_tensor(ss[:, :, :], ss[:, :, :], cnt[:, :].unsqueeze(2).to_broadcast([P, 4, P]),
                                             ALU.add))
                    own.link(V.tensor_reduce(mx[:, :], ss[:, :, :].rearrange("p j k -> p (j k)"), AX.X, ALU.max))
                    V.tensor_scalar(dm[:, :], tb("gsel"), mx[:, 0:1], None, ALU.mult).then_inc(dm_ready, 1)
                if has_k:
                    hi_lo(tile_at(T_KVU, i, 8))
                if has_v:
                    dve.wait_ge(mx_done, i)
                    own.link(V.tensor_reduce(mx[:, :], OB[1][:, 8:12], AX.X, ALU.max))
                    V.tensor_scalar(negm[:, :], mx[:, :], -1.0, None, ALU.mult).then_inc(m_ready, 1)
                    own.did(V.tensor_copy(m_all[:, bass.ds(i - 1, 1)], mx[0:32, :]))
                if has_k:
                    hi_lo(tile_at(T_KVU + 1, i, 8))
                if has_v:
                    dve.wait_ge(l_done, i)
                    V.tensor_copy(l_all[:, bass.ds(i - 1, 1)], OB[1][0:32, 12:13]).then_inc(l_saved, 1)
                if has_k:
                    for k in range(2, 8):
                        hi_lo(tile_at(T_KVU + k, i, 8))
                    dve.wait_ge(w_used, T_KVU + 8 + 8 * i)
                    for m in range(3):
                        V.tensor_copy(z[:, bass.ds(ZK + 3 * i + m, 1), :].rearrange("p a t -> p (a t)"),
                                      WB[m][:, 0:T]).then_inc(z_ready, 1)
                if has_v:
                    dve.wait_ge(v_done, 4 * i)
                    if has_comb:
                        dve.wait_ge(comb_done, i - 1)
                    V.tensor_copy(osb[:, 512:1024], OB[1][:, :]).then_inc(o7_taken, 1)

            kv_step(0, True, False, False, first=True)
            kv_step(1, True, True, False)
            done, own.k = own.k, 0
            with dve.Fori(2, NB) as i:
                own.base = done + DVE_STEPS * (i - 2)
                kv_step(i, True, True, True)
                assert own.k == DVE_STEPS
            own.base, own.k = done + DVE_STEPS * (NB - 2), 0
            kv_step(NB, False, True, True)

            for n in range(1, 16, 2):
                dve.wait_ge(tok_in, n + 1)
                rows, dst = tok_dst(n)
                V.tensor_copy(dst, bank[n % 4][0:rows, :]).then_inc(tok_dve, 1)
            dve.wait_ge(hist_T, 1)
            for n in range(2):
                V.tensor_copy(ext[:, 4 * n:4 * n + 4, :, 0:HIST],
                              bank[4 + n][:, 0:480].rearrange("p (c b i) -> p c b i", c=4, b=NB)).then_inc(ext_ready, 1)
            own.link(V.memset(qza[:, :, :], 0.0))
            V.tensor_copy(qza[:, :, :].rearrange("p b (h s) -> p b h s", s=36)[:, :, :, 0:NQ],
                          z[:, ZQ:ZQ + H, TP:T].rearrange("p h (b q) -> p b h q", b=NB)).then_inc(qza_ready, 1)
            for k in range(SLOTS):
                lo(tile_at(T_OUT + k))
            for s in range(H + 2):
                if s < H:
                    dve.wait_ge(a_in, s + 1)
                    dve.wait_ge(rb_ready, s + 1)
                    if s >= 2:
                        dve.wait_ge(pt2_in, s - 1)
                    V.scalar_tensor_tensor(px[:, s % 2, :], bank[4 + s % 2][:, 0:384], SCALE, rbias[:, s % 2, :],
                                           ALU.mult, ALU.add).then_inc(a_out, 1)
                    dve.wait_ge(a_out, s + 1)
                    for n, (a, b) in enumerate(((0, P), (P, 384))):
                        V.tensor_reduce(pm[:, s % 2, n:n + 1], px[:, s % 2, a:b], AX.X, ALU.max,
                                        negate=True).then_inc(pm_ready, 1)
                if 1 <= s <= H:
                    u = (s - 1) % 2
                    dve.wait_ge(pe_ready, 2 * s)
                    own.link(V.reciprocal(pl[:, u, :], pl[:, u, :]))
                    for n, (a, b) in enumerate(((0, P), (P, 384))):
                        V.tensor_scalar(px[:, u, a:b], px[:, u, a:b], pl[:, u, n:n + 1], None,
                                        ALU.mult).then_inc(pn_ready, 1)
                if s >= 2:
                    dve.wait_ge(po_hi, s - 1)
                    V.tensor_tensor(hl[:, s - 2, 0:TP], bank[2 + s % 2][:, 0:TP], hh[:, s - 2, 0:TP].bitcast(F32),
                                    ALU.subtract).then_inc(mix_ready, 1)
            dve.wait_ge(so_in, 1)
            own.link(V.scalar_tensor_tensor(so[:, :, :], bank[0][0:32, 0:32].rearrange("p (b k) -> p b k", b=NB), SCALE,
                                            tb("own_bias")[0:32, :].unsqueeze(1).to_broadcast([32, NB, NQ]),
                                            ALU.mult, ALU.add))
            own.link(V.tensor_reduce(mo[:, :], so[:, :, :], AX.X, ALU.max))
            own.link(V.tensor_tensor(mm_[:, :], mo[:, :], m_all[:, :], ALU.max))
            V.tensor_tensor(so[:, :, :], so[:, :, :], mm_[:, :].unsqueeze(2).to_broadcast([32, NB, NQ]),
                            ALU.subtract).then_inc(so_sub, 1)
            V.tensor_tensor(eo[:, :], m_all[:, :], mm_[:, :], ALU.subtract).then_inc(so_sub, 1)
            dve.wait_ge(so_exp, 2)
            dve.wait_ge(l_saved, NB)
            own.did(V.tensor_reduce(lo_[:, :], so[:, :, :], AX.X, ALU.add))
            own.did(V.tensor_tensor(mo[:, :], l_all[:, :], eo[:, :], ALU.mult))
            own.settle()
            own.link(V.tensor_tensor(lo_[:, :], lo_[:, :], mo[:, :], ALU.add))
            own.link(V.reciprocal(lo_[:, :], lo_[:, :]))
            own.did(V.tensor_tensor(so[:, :, :], so[:, :, :], lo_[:, :].unsqueeze(2).to_broadcast([32, NB, NQ]), ALU.mult))
            own.link(V.tensor_tensor(eo[:, :], eo[:, :], lo_[:, :], ALU.mult))
            dve.wait_ge(comb_saved, NB)
            V.tensor_tensor(o_all[:, :, :], o_all[:, :, :], eo[:, :].unsqueeze(2).to_broadcast([32, NB, DH]),
                            ALU.mult).then_inc(own_ready, 1)
            dve.wait_ge(pTo_in, 1)
            own.link(V.tensor_copy(pTo[:, :], bank[1][0:32, 0:32]))
            V.tensor_tensor(pTb[:, :, :, :], pTo[:, :].rearrange("p (h q) -> p h q", h=H).unsqueeze(2).to_broadcast(
                [32, H, NB, NQ]), tb("batch_of")[0:32, :].unsqueeze(1).unsqueeze(3).to_broadcast([32, H, NB, NQ]),
                ALU.mult).then_inc(pTb_ready, 1)
            for n in range(8):
                dve.wait_ge(y_in, n + 1)
                if n >= 2:
                    dve.wait_ge(y_hi, n - 1)
                V.tensor_scalar(nrm[:, n % 2, :], bank[4 + n % 2][:, 0:T], gains[:, 32 + n:33 + n], None,
                                ALU.mult).then_inc(y_sc, 1)
                dve.wait_ge(y_hi, n + 1)
                V.tensor_tensor(hl[:, 8 + n, :], nrm[:, n % 2, :], hh[:, 8 + n, :].bitcast(F32),
                                ALU.subtract).then_inc(pool_mix, 1)
            dve.wait_ge(t1_in, 1)
            own.link(V.tensor_copy(t1[:, :, :], bank[2][:, 0:256].rearrange("p (b c) -> p b c", b=NB)))
            dve.wait_ge(t2_in, 1)
            V.tensor_tensor(mixs[:, :, :].rearrange("p h (b q) -> p h b q", b=NB),
                            bank[3][:, 0:256].rearrange("p (h b q) -> p h b q", h=H, b=NB),
                            t1[:, :, :].rearrange("p b (h q) -> p h b q", h=H), ALU.add).then_inc(smix, 1)
            dve.wait_ge(smix_hi, 1)
            V.tensor_tensor(hl[:, 0:H, TP:T], mixs[:, :, :], hh[:, 0:H, TP:T].bitcast(F32),
                            ALU.subtract).then_inc(smix_ready, 1)

            def add_group(quad, m0, used):
                dve.wait_ge(w_used, used)
                for m in range(4):
                    ins = V.tensor_tensor(xT[:, m0 + m, :], xT[:, m0 + m, :], bank[4 * quad + m][:, 0:T], ALU.add)
                    ins.then_inc(quad_taken[quad], 1)

            def add_out(quad, c, used):
                dve.wait_ge(w_used, used)
                for m in range(4):
                    chunk = xT[:, bass.ds(4 * c + m, 1), :].rearrange("p a t -> p (a t)")
                    V.tensor_tensor(chunk, chunk, bank[4 * quad + m][:, 0:T], ALU.add).then_inc(quad_taken[quad], 1)

            with dve.Fori(0, 2) as i:
                for k in range(16):
                    lo(tile_at(T_OUT + 4 + k, i, 16))
                    if k % 8 == 7:
                        quad = k // 8
                        add_out(quad, 2 * i + quad, T_OUT + 16 * i + 8 * quad + 8)
            norm(1)

            def mul_act(g):
                def product(m):
                    dve.wait_ge(sg_ready, 4 * g + m + 1)
                    if m >= 2:
                        dve.wait_ge(act_ready, 4 * g + m - 1)
                    V.tensor_tensor(af[:, m % 2, :], sg[:, m, :], bank[4 + m][:, 0:T], ALU.mult).then_inc(af_ready, 1)

                dve.wait_ge(w_used, T_FF + 16 + 24 * g)
                product(0)
                for m in range(4):
                    if m < 3:
                        product(m + 1)
                    dve.wait_ge(ah_ready, 4 * g + m + 1)
                    V.tensor_tensor(al[:, m, :], af[:, m % 2, :], ah[:, m, :].bitcast(F32),
                                    ALU.subtract).then_inc(act_ready, 1)

            for k in range(8):
                lo(tile_at(T_FF + 4 + k))
            with dve.Fori(0, NG - 1) as g:
                for k in range(24):
                    lo(tile_at(T_FF + 12 + k, g, 24))
                    if k == 7:
                        mul_act(g)
                    if k >= 16 and k % 2 == 1:
                        c = (k - 17) // 2
                        add_group((c + 1) % 2, 4 * c, T_FF + 24 + 24 * g + 2 * c + 2)
            for k in range(12):
                lo(tile_at(T_END - 12 + k))
                if k == 7:
                    mul_act(NG - 1)
            for c in range(4):
                dve.wait_ge(w_used, T_END - 8 + 2 * c + 2)
                for m in range(4):
                    V.tensor_tensor(xT[:, 4 * c + m, :], xT[:, 4 * c + m, :], bank[4 * (c % 2) + m][:, 0:T],
                                    ALU.add).then_inc(x_ready, 1)
            dve.wait_ge(sq_used, 3 * KC)
            dve.wait_ge(stored, 16 * STORES)
            own.link(V.memset(rf[:, :], 1.0))
            for n in range(3):
                rows = P if n < 2 else TS
                V.tensor_scalar(rf[0:rows, n:n + 1], bank[4 + n][0:rows, 0:1], 1.0 / D, EPS, ALU.mult,
                                ALU.add).then_inc(fms, 1)
            dve.wait_ge(froot, 1)
            own.link(V.reciprocal(rf[:, :], rf[:, :]))
            dve.wait_ge(gf_in, 16)
            for n in range(12):
                part, c = n // 4, n % 4
                rows = P if part < 2 else TS
                dve.wait_ge(fy_in, n + 1)
                V.scalar_tensor_tensor(yt[0:rows, part, 512 * c:512 * c + 512], bank[n % 4][0:rows, :],
                                       rf[0:rows, part:part + 1], gf[0:rows, 512 * c:512 * c + 512],
                                       ALU.mult, ALU.mult).then_inc(fy_out, 1)

        @block.gpsimd
        def _(pool):
            own = Steps(pool, pool_own)
            G = nc.gpsimd
            pool.wait_ge(ext_ready, 2)
            pool.wait_ge(z_ready, 3 * NB)
            for c in range(8):
                own.did(G.tensor_copy(ext[:, c, :, HIST:HIST + NQ],
                                      z[:, ZU + c, TP:T].rearrange("p (b q) -> p b q", b=NB)))
            own.settle()
            for g, w in enumerate(WINDOWS):
                u_p, u_s = z[:, ZU + 2 * g:ZU + 2 * g + 2, 0:TP], ext[:, 2 * g:2 * g + 2, :, :]
                src_p, src_s, n, shift = u_p, u_s, 0, 1
                while shift < w:
                    dst_p, dst_s = win[:, n % 2, :, :], wins[:, n % 2, :, :, :]
                    L = HIST + NQ
                    own.did(G.tensor_copy(dst_p[:, :, 0:shift], src_p[:, :, 0:shift]))
                    own.did(G.tensor_tensor(dst_p[:, :, shift:TP], src_p[:, :, shift:TP], src_p[:, :, 0:TP - shift],
                                            ALU.add))
                    for c in range(2):
                        own.did(G.tensor_tensor(dst_s[:, c, :, 2 * shift - 1:L], src_s[:, c, :, 2 * shift - 1:L],
                                                src_s[:, c, :, shift - 1:L - shift], ALU.add))
                    own.settle()
                    src_p, src_s, n, shift = dst_p, dst_s, n + 1, 2 * shift
                d = dpool[:, g % 2, :, :]
                if g >= 2:
                    pool.wait_ge(y_in, 2 * g - 2)
                own.did(G.tensor_tensor(d[:, :, 0:16], src_p[:, :, 0:16],
                                        inv_count[:, g, :].unsqueeze(1).to_broadcast([P, 2, 16]), ALU.mult))
                own.did(G.tensor_scalar(d[:, :, 16:TP], src_p[:, :, 16:TP], 1.0 / w, None, ALU.mult))
                for c in range(2):
                    own.did(G.tensor_scalar(d[:, c, TP:T].rearrange("p (b q) -> p b q", b=NB), src_s[:, c, :, HIST:L],
                                            1.0 / w, None, ALU.mult))
                own.settle()
                G.tensor_tensor(d[:, :, :], d[:, :, :], z[:, ZU + 2 * g:ZU + 2 * g + 2, :],
                                ALU.subtract).then_inc(d_ready, 1)

        @block.tensor
        def _(pe):
            PE = nc.tensor

            def w_tile(t, width, chunks, banks, xh, xl, start, stop):
                n, _, s = t
                pe.wait_ge(lo_ready, n + 1)
                for m, out in enumerate(banks):
                    for i, c in enumerate(chunks):
                        a = width * i + P * m
                        wh, wl = w_hi[:, s, a:a + P], w_lo[:, s, a:a + P]
                        o = out[:, 0:T]
                        PE.matmul(o, wh, xh[:, c, :], start=start and i == 0, stop=False)
                        PE.matmul(o, wh, xl[:, c, :], start=False, stop=False)
                        last = PE.matmul(o, wl, xh[:, c, :], start=False, stop=stop and i == 1)
                last.then_inc(w_used, 1)

            def turn(out, in_, rows):
                return PE.transpose(out, in_, ident[0:rows, 0:rows])

            pe.wait_ge(tab_in, 16)
            pe.wait_ge(vec_in, 48)
            turn(bank[6][:, 0:40], vec[:, :], 40).then_inc(vecT, 1)
            pe.wait_ge(x_in, 48)

            def sum_sq(stage, c):
                pe.wait_ge(sq_ready, KC * stage + c + 1)
                PE.matmul(bank[7][:, 0:T], ones, sq[:, c % 2, :], start=c == 0, stop=c == KC - 1).then_inc(sq_used, 1)

            for c in range(KC):
                if c >= 4:
                    pe.wait_ge(x_ready, c - 3)
                for n in range(3):
                    rows = P if n < 2 else TS
                    last = turn(bank[c % 4][:, P * n:P * n + rows], xs[0:rows, n, P * c:P * c + P], rows)
                last.then_inc(xT_in, 1)
                if c:
                    sum_sq(0, c - 1)
            sum_sq(0, KC - 1)
            for k in range(16):
                c, j = k // 8, k % 8
                if c == 0:
                    pe.wait_ge(h_ready, 2 * j + 2)
                if k == 8:
                    pe.wait_ge(ms_ready, 1)
                    pe.wait_ge(gains_ready, 1)
                w_tile(tile_at(k), 512, (2 * j, 2 * j + 1), bank[4 * c:4 * c + 4], hh, hl, j == 0, j == 7)

            def kv_step(i, has_k, has_v, has_comb, first=False):
                def transposes(j, h):
                    n = 32 * i + 8 * j + h
                    if first and j == 0 and h < 2:
                        for c in range(2):
                            pe.wait_ge(quad_taken[c], QT0)
                    else:
                        pe.wait_ge(kt_out, n - 1)
                    if h == 0:
                        pe.wait_ge(k_in[j % 2], 128 * i + 64 * (j // 2) + 64)
                    for g in range(4):
                        last = turn(KTP[h % 2][:, P * g:P * g + P], kpage[:, j % 2, g, DH * h:DH * h + DH], P)
                    last.then_inc(kt_in, 1)

                def logits(j, h):
                    n = 32 * i + 8 * j + h
                    pe.wait_ge(kt_out, n + 1)
                    if j == 0 and h == 0:
                        pe.wait_ge(qz_ready, i + 1)
                        if not first:
                            pe.wait_ge(dn_ready, i)
                    for g in range(4):
                        last = PE.matmul(S[32 * g:32 * g + 32, P * j:P * j + P], qz[:, 32 * h:32 * h + 32],
                                         kT[:, h % 2, P * g:P * g + P], start=h == 0, stop=h == H - 1)
                    last.then_inc(qk_done, 1)

                def block_sums():
                    pe.wait_ge(dn_ready, i)
                    if has_comb:
                        pe.wait_ge(o7_taken, i - 1)
                    PE.matmul(OB[1][:, 0:8], same, dn[:, :, :].rearrange("p j u -> p (j u)"), start=True,
                              stop=True).then_inc(bs_done, 1)

                def joint_max():
                    pe.wait_ge(dm_ready, i)
                    PE.matmul(OB[1][:, 8:12], same, dm[:, :], start=True, stop=True).then_inc(mx_done, 1)

                def p_turned():
                    pe.wait_ge(p_ready, i)
                    pe.wait_ge(m_ready, i)
                    PE.matmul(OB[1][:, 12:13], same, lsum[:, :], start=True, stop=True).then_inc(l_done, 1)
                    if has_comb:
                        pe.wait_ge(comb_saved, i - 1)
                    for j in range(4):
                        last = turn(OB[0][:, P * j:P * j + P], ss[:, j, :], P)
                    last.then_inc(pt_in, 1)

                def values(j):
                    pe.wait_ge(v_in, 256 * i + 64 * j - 192)
                    if j == 0:
                        pe.wait_ge(pt_ready, i)
                        pe.wait_ge(l_saved, i)
                    for x in range(2):
                        for g in range(4):
                            last = PE.matmul(OB[x][32 * g:32 * g + 32, :], pT[:, j, 32 * g:32 * g + 32],
                                             vpage[:, g, 512 * x:512 * x + 512], start=j == 0, stop=j == NQUADS - 1)
                    last.then_inc(v_done, 1)

                if not has_k:
                    block_sums()
                    if has_comb:
                        combine(i - 1)
                    joint_max()
                    p_turned()
                for j in range(NQUADS):
                    if has_k:
                        transposes(j, 0)
                        for h in range(1, H):
                            transposes(j, h)
                            logits(j, h - 1)
                            if j == 0 and has_v:
                                if h == 2:
                                    block_sums()
                                if h == 3 and has_comb:
                                    combine(i - 1)
                                if h == 5:
                                    joint_max()
                        if j == 0 and not first:
                            pe.wait_ge(z_ready, 3 * i)
                        for k in (2 * j, 2 * j + 1):
                            w_tile(tile_at(T_KVU + k, i, 8), CW, (2 * k, 2 * k + 1), WB, hh, hl, k == 0, k == 7)
                            if k % 2 == 0:
                                logits(j, H - 1)
                                if j == 0 and has_v:
                                    p_turned()
                    if has_v:
                        values(j)

            def combine(count):
                pe.wait_ge(o6_taken, count)
                pe.wait_ge(o7_taken, count)
                for h in range(H):
                    last = PE.matmul(OB[0][0:32, 0:DH], headsel[:, h, :], osb[:, DH * h:DH * h + DH],
                                     start=h == 0, stop=h == H - 1)
                last.then_inc(comb_done, 1)

            kv_step(0, True, False, False, first=True)
            kv_step(1, True, True, False)
            with pe.Fori(2, NB) as i:
                kv_step(i, True, True, True)
            kv_step(NB, False, True, True)
            combine(NB)

            pe.wait_ge(z_ready, 3 * NB)
            for n in range(16):
                chunk, a, b = tok_src(n)
                if n >= 4:
                    pe.wait_ge((tok_act, tok_dve)[n % 2], (n - 4) // 2 + 1)
                for m in range(4):
                    last = turn(bank[n % 4][0:b - a, P * m:P * m + P], z[:, chunk + m, a:b], P)
                last.then_inc(tok_in, 1)
            pe.wait_ge(hist_in, 16)
            for n in range(2):
                for m in range(4):
                    last = turn(bank[4 + n][:, 120 * m:120 * m + 120], hist[:, 512 * n + P * m:512 * n + P * m + P],
                                NB * HIST)
            last.then_inc(hist_T, 1)
            pe.wait_ge(tok_act, 8)
            pe.wait_ge(tok_dve, 8)
            for s in range(H + 2):
                if s < H:
                    if s < 2:
                        pe.wait_ge(ext_ready, 2)
                    else:
                        pe.wait_ge(a_out, s - 1)
                    A_ = bank[4 + s % 2]
                    PE.matmul(A_[:, 0:P], z[:, ZQ + s, 0:P], z[:, ZK + s, 0:P], start=True, stop=True)
                    PE.matmul(A_[:, P:384], z[:, ZQ + s, P:TP], z[:, ZK + s, 0:TP], start=True,
                              stop=True).then_inc(a_in, 1)
                if s >= 2:
                    h = s - 2
                    o = bank[2 + h % 2]
                    pe.wait_ge(pt2_ready, h + 1)
                    if h >= 2:
                        pe.wait_ge(mix_ready, h - 1)
                    PE.matmul(o[:, 0:TP], vtok[:, 0, DH * h:DH * h + DH], ptp[:, h % 2, 0:TP], start=True, stop=False)
                    PE.matmul(o[:, P:TP], vtok[:, 1, DH * h:DH * h + DH], ptp[:, h % 2, TP:384], start=False,
                              stop=True).then_inc(po_in, 1)
                if 1 <= s <= H:
                    h = s - 1
                    pe.wait_ge(pn_ready, 2 * h + 2)
                    if h == 0:
                        pe.wait_ge(comb_saved, NB)
                    if h >= 2:
                        pe.wait_ge(pt2_ready, h - 1)
                    B_ = bank[6 + h % 2]
                    turn(B_[:, 0:P], px[:, h % 2, 0:P], P)
                    turn(B_[:, P:TP], px[:, h % 2, P:TP], P)
                    turn(B_[:, TP:384], px[:, h % 2, TP:384], P).then_inc(pt2_in, 1)
            pe.wait_ge(qza_ready, 1)
            for b in range(NB):
                for h in range(H):
                    last = PE.matmul(bank[0][0:32, NQ * b:NQ * b + NQ], qza[:, b, 32 * h:32 * h + 32],
                                     z[:, ZK + h, TP + NQ * b:TP + NQ * b + NQ], start=h == 0, stop=h == H - 1)
            last.then_inc(so_in, 1)
            pe.wait_ge(wpool_in, 16)
            pe.wait_ge(a_out, H)

            def mixer(n):
                g, e = n // 2, n % 2
                pe.wait_ge(d_ready, g + 1)
                if n >= 2:
                    pe.wait_ge(y_sc, n - 1)
                for c in range(2):
                    last = PE.matmul(bank[4 + n % 2][:, 0:T], wpool[:, g, c, P * e:P * e + P], dpool[:, g % 2, c, :],
                                     start=c == 0, stop=c == 1)
                last.then_inc(y_in, 1)

            pe.wait_ge(own_ready, 1)
            turn(bank[1][0:32, 0:32], so[:, :, :].rearrange("p b k -> p (b k)"), 32).then_inc(pTo_in, 1)
            pe.wait_ge(mix_ready, H)
            for b in range(NB):
                last = turn(bank[2][:, 32 * b:32 * b + 32], o_all[:, b, :], 32)
            last.then_inc(t1_in, 1)
            pe.wait_ge(pTb_ready, 1)
            for h in range(H):
                last = PE.matmul(bank[3][:, 32 * h:32 * h + 32], stok[0:TS, DH * h:DH * h + DH],
                                 pTb[:, h, :, :].rearrange("p b q -> p (b q)"), start=True, stop=True)
            last.then_inc(t2_in, 1)
            for n in range(8):
                mixer(n)
            pe.wait_ge(mix_ready, H)
            pe.wait_ge(pool_mix, 8)
            pe.wait_ge(smix_ready, 1)
            with pe.Fori(0, 2) as i:
                for k in range(16):
                    c, j = k // 8, k % 8
                    if j == 0:
                        pe.wait_ge(quad_taken[c], QT0 + 4 * i)
                    w_tile(tile_at(T_OUT + k, i, 16), 512, (2 * j, 2 * j + 1), bank[4 * c:4 * c + 4], hh, hl,
                           j == 0, j == 7)
            pe.wait_ge(quad_taken[1], QT)
            for c in range(KC):
                sum_sq(1, c)

            def gate_up(t0, quad):
                for j in range(8):
                    w_tile(tile_at(*((t0[0] + j,) + t0[1:])), 512, (2 * j, 2 * j + 1), bank[4 * quad:4 * quad + 4],
                           hh, hl, j == 0, j == 7)

            pe.wait_ge(quad_taken[0], QT)
            for j in range(8):
                pe.wait_ge(h_ready, KC + 2 * j + 2)
                w_tile(tile_at(T_FF + j), 512, (2 * j, 2 * j + 1), bank[0:4], hh, hl, j == 0, j == 7)
            pe.wait_ge(ms_ready, 2)

            def down(t0, g, quads, taken):
                for c in range(4):
                    quad = quads[c]
                    if taken[c]:
                        pe.wait_ge(*taken[c])
                    if c == 0:
                        pe.wait_ge(af_ready, 4 * g + 4)
                    for j in range(2):
                        if c == 0:
                            pe.wait_ge(act_ready, 4 * g + 2 * j + 2)
                        w_tile(tile_at(*((t0[0] + 2 * c + j,) + t0[1:])), 512, (2 * j, 2 * j + 1),
                               bank[4 * quad:4 * quad + 4], ah, al, j == 0, j == 1)

            with pe.Fori(0, NG - 1) as g:
                pe.wait_ge(quad_taken[1], QT + 8 * g)
                gate_up((T_FF + 8, g, 24), 1)
                pe.wait_ge(sg_ready, 4 * g + 4)
                pe.wait_ge(quad_taken[0], QT + 8 * g)
                gate_up((T_FF + 16, g, 24), 0)
                down((T_FF + 24, g, 24), g, (1, 0, 1, 0),
                     (None, (sg_ready, 4 * g + 8), (quad_taken[1], QT + 4 + 8 * g), (quad_taken[0], QT + 4 + 8 * g)))
            pe.wait_ge(quad_taken[1], QT + 8 * (NG - 1))
            gate_up((T_END - 16,), 1)
            pe.wait_ge(quad_taken[0], QT + 8 * (NG - 1))
            pe.wait_ge(sg_ready, 4 * NG)
            down((T_END - 8,), NG - 1, (0, 1, 0, 1),
                 (None, (act_ready, 4 * NG), (x_ready, KC + 4), (x_ready, KC + 8)))
            pe.wait_ge(x_ready, 2 * KC)
            for c in range(KC):
                pe.wait_ge(sq_ready, 2 * KC + c + 1)
                for n in range(3):
                    rows = P if n < 2 else TS
                    last = PE.matmul(bank[4 + n][0:rows, 0:1], sq[:, c % 2, P * n:P * n + rows], ones[:, 0:1],
                                     start=c == 0, stop=c == KC - 1)
                last.then_inc(sq_used, 1)
            for n in range(12):
                part, c = n // 4, n % 4
                rows = P if part < 2 else TS
                if n >= 4:
                    pe.wait_ge(fy_out, n - 3)
                for m in range(4):
                    last = turn(bank[n % 4][0:rows, P * m:P * m + P], xT[:, 4 * c + m, P * part:P * part + rows], P)
                last.then_inc(fy_in, 1)


STORES = 6 + 1 + 1 + NB

_INS = ["x_prompt", "x_sample", "cache_k", "cache_v", "state_pool", "page_table", "norm1_g", "w_in", "w_pool",
        "pool_scale", "w_out", "norm2_g", "w_gate", "w_up", "w_down", "norm_f_g"]
_OUTS = [("y_prompt", (1, TP, D)), ("y_sample", (NB, NQ, D)), ("k_prompt", (1, 1, TP, H, DH)),
         ("v_prompt", (1, 1, TP, H, DH)), ("pool_prompt", (1, 1, HIST, AW)), ("k_sample", (1, NB, NQ, H, DH)),
         ("v_sample", (1, NB, NQ, H, DH)), ("pool_sample", (1, NB, HIST, AW))]


def kernel(**inputs):
    import concourse.bacc as bacc
    from concourse.bass_utils import run_bass_kernel_spmd

    nc = bacc.Bacc("TRN2", target_bir_lowering=False, num_devices=1, dynamic_dma_scratch_size=64)
    table, at = tables()
    arrays = {name: np.ascontiguousarray(inputs[name]) for name in _INS}
    arrays["tables"] = table
    ins = {name: nc.dram_tensor(f"in_{name}", a.shape, mybir.dt.from_np(a.dtype), kind="ExternalInput").ap()
           for name, a in arrays.items()}
    outs = {name: nc.dram_tensor(f"out_{name}", shape, F32, kind="ExternalOutput").ap() for name, shape in _OUTS}
    step_program(nc, ins, outs, at)
    r = run_bass_kernel_spmd(nc, [{f"in_{name}": a for name, a in arrays.items()}], core_ids=[0])
    return tuple(r.results[0][f"out_{name}"] for name, _ in _OUTS)
```

```python
from contextlib import ExitStack

import numpy as np

import concourse.bass as bass
from concourse import mybir

F32 = mybir.dt.float32
F32R = mybir.dt.float32r
I32 = mybir.dt.int32
ALU = mybir.AluOpType
ACT = mybir.ActivationFunctionType
AX = mybir.AxisListType

P = 128
D = 2048
KC = D // P
TP = 256
NB, NQ = 8, 4
TS = NB * NQ
T = TP + TS
H, DH = 8, 128
AW = H * DH
NPAGES = 16
NQUADS = NPAGES // 4
PAST = NPAGES * P
FF = 5632
NG = FF // 512
HIST = 15
WINDOWS = (2, 4, 8, 16)
EPS = 1e-6
SCALE = DH ** -0.5
NEG = -1e30
TOPK = 3
ZQ, ZK, ZV, ZU = 0, 8, 16, 24
T_Q = 0
T_KVU = T_Q + 16
T_OUT = T_KVU + 8 * NB
T_FF = T_OUT + 32
T_END = T_FF + 24 * NG
CW = 384
SLOTS = 4
TE = 2 * 512
QT0 = 4
QT = QT0 + 8
DVE_STEPS = 15


def tables():
    p = np.arange(P)
    g, h, q = p // 32, (p // 4) % H, p % NQ
    slope = 2.0 ** -(h + 1.0)
    j4, r, n8 = np.arange(4), np.arange(P), np.arange(8)
    key = (4 * j4[None, :, None] + g[:, None, None]) * P + r[None, None, :]
    t16 = np.arange(16)
    qi, ki = p[:, None], np.arange(TP)[None, :]
    parts = {
        "ident": np.eye(P),
        "ones": np.ones((P, P)),
        "same": (p[:, None] % 32 == p[None, :] % 32),
        "headsel": (h[:, None, None] == n8[None, :, None]) & (p[:, None, None] % 32 == np.arange(32)),
        "past_bias": slope[:, None, None] * (key - (PAST + q[:, None, None])),
        "half": (g[:, None] // 2 == np.arange(2)),
        "gsel": (g[:, None] == j4[None, :]),
        "before": n8[None, None, :] < (2 * j4[None, :, None] + g[:, None, None] // 2),
        "own_bias": np.where(np.arange(NQ) <= q[:, None], slope[:, None] * (np.arange(NQ) - q[:, None]), NEG),
        "batch_of": (p[:, None] // NQ == n8[None, :]),
        "rel": np.concatenate(
            [np.where(ki[:, :P] <= qi, ki[:, :P] - qi, -1e33), np.where(ki <= qi + P, ki - (qi + P), -1e33)], 1),
        "inv_count": np.broadcast_to(1.0 / np.minimum(t16 + 1, np.array(WINDOWS)[:, None]), (P, 4, 16)),
    }
    at, cols = {}, 0
    flat = []
    for name, a in parts.items():
        a = np.asarray(a, np.float64).reshape(P, -1)
        at[name] = (cols, cols + a.shape[1])
        cols += a.shape[1]
        flat.append(a)
    return np.concatenate(flat, 1).astype(np.float32), at


class Steps:

    def __init__(self, eng, sem):
        self.eng, self.sem, self.base, self.k = eng, sem, 0, 0

    def did(self, ins):
        ins.then_inc(self.sem, 1)
        self.k += 1

    def settle(self):
        self.eng.wait_ge(self.sem, self.base + self.k)

    def link(self, ins):
        self.did(ins)
        self.settle()


def tile_at(k, i=0, per=0):
    return k + per * i, k // SLOTS + (per // SLOTS) * i, k % SLOTS


def step_program(nc, A, O, at):
    ctx = ExitStack()
    with ctx:
        def sem(name):
            return ctx.enter_context(nc.semaphore(name))

        def sb(name, shape, dt=F32, stack=None):
            return (stack or ctx).enter_context(nc.sbuf_tensor(name, shape, dt))

        tab = sb("tab", [P, A["tables"].shape[1]])
        xT = sb("xT", [P, KC, T])
        hh = sb("hh", [P, KC, T], F32R)
        hl = sb("hl", [P, KC, T], F32R)
        w_raw = sb("w_raw", [P, SLOTS, TE])
        w_hi = sb("w_hi", [P, SLOTS, TE], F32R)
        w_lo = sb("w_lo", [P, SLOTS, TE], F32R)
        gains = sb("gains", [P, 56])
        rstd = sb("rstd", [P, T])
        ms = sb("ms", [P, T])
        ssq = sb("ssq", [P, T])
        sq = sb("sq", [P, 2, T])
        nrm = sb("nrm", [P, 2, T])
        mid = ExitStack()
        z = sb("z", [P, 32, T], stack=mid)
        o_all = sb("o_all", [32, NB, DH], stack=mid)
        m_all = sb("m_all", [32, NB], stack=mid)
        l_all = sb("l_all", [32, NB], stack=mid)
        win = sb("win", [P, 2, 2, TP], stack=mid)
        kv = ExitStack()
        kpage = sb("kpage", [P, 2, 4, AW], stack=kv)
        kT = sb("kT", [P, 2, 512], stack=kv)
        qz = sb("qz", [P, H * 36], stack=kv)
        pages = sb("pages", [1, NB * NPAGES], I32, stack=kv)
        vpage = sb("vpage", [P, 4, AW], stack=kv)
        ss = sb("ss", [P, 4, P], stack=kv)
        pT = sb("pT", [P, 4, P], stack=kv)
        osb = sb("osb", [P, AW], stack=kv)
        d4 = sb("d4", [P, 4], stack=kv)
        dn = sb("dn", [P, 4, 2], stack=kv)
        bsc = sb("bsc", [P, 8], stack=kv)
        bsh = sb("bsh", [P, 4, 2], stack=kv)
        bown = sb("bown", [P, 4], stack=kv)
        gt = sb("gt", [P, 4, 8], stack=kv)
        eq = sb("eq", [P, 4, 8], stack=kv)
        cnt = sb("cnt", [P, 4], stack=kv)
        mx = sb("mx", [P, 1], stack=kv)
        dm = sb("dm", [P, 4], stack=kv)
        negm = sb("negm", [P, 1], stack=kv)
        lsum = sb("lsum", [P, 1], stack=kv)
        kv.close()
        pre = ExitStack()
        xs = sb("xs", [P, 3, D], stack=pre)
        vec = sb("vec", [56, P], stack=pre)
        pre.close()
        post = ExitStack()
        vtok = sb("vtok", [P, 2, AW], stack=post)
        stok = sb("stok", [P, AW], stack=post)
        px = sb("px", [P, 2, 384], stack=post)
        ptp = sb("ptp", [P, 2, 384], stack=post)
        pm = sb("pm", [P, 2, 2], stack=post)
        pl = sb("pl", [P, 2, 2], stack=post)
        wpool = sb("wpool", [P, 4, 2, 256], stack=post)
        hist = sb("hist", [NB * HIST, AW], stack=post)
        ext = sb("ext", [P, 8, NB, HIST + NQ], stack=post)
        wins = sb("wins", [P, 2, 2, NB, HIST + NQ], stack=post)
        ktok = sb("ktok", [P, 2, AW], stack=post)
        qza = sb("qza", [P, NB, H * 36], stack=post)
        so = sb("so", [32, NB, NQ], stack=post)
        mo = sb("mo", [32, NB], stack=post)
        mm_ = sb("mm_", [32, NB], stack=post)
        eo = sb("eo", [32, NB], stack=post)
        lo_ = sb("lo_", [32, NB], stack=post)
        pTo = sb("pTo", [32, 32], stack=post)
        pTb = sb("pTb", [32, H, NB, NQ], stack=post)
        t1 = sb("t1", [P, NB, 32], stack=post)
        mixs = sb("mixs", [P, H, TS], stack=post)
        post.close()
        mid.close()
        late = ExitStack()
        sg = sb("sg", [P, 4, T], stack=late)
        af = sb("af", [P, 2, T], stack=late)
        ah = sb("ah", [P, 4, T], F32R, stack=late)
        al = sb("al", [P, 4, T], F32R, stack=late)
        yt = sb("yt", [P, 3, D], stack=late)
        rf = sb("rf", [P, 3], stack=late)
        fm = sb("fm", [P, 3], stack=late)
        ft = sb("ft", [P, 3], stack=late)
        late.close()

        bank = [ctx.enter_context(nc.psum_tensor(f"bank{n}", [P, 512], F32)) for n in range(8)]
        WB = bank[0:3]
        KTP = bank[3:5]
        S = bank[5]
        OB = bank[6:8]

        def tb(name):
            a, b = at[name]
            return tab[:, a:b]

        ident, ones, same = tb("ident"), tb("ones"), tb("same")
        headsel = tb("headsel").rearrange("p (h c) -> p h c", h=H)
        past_bias = tb("past_bias")
        half = tb("half")
        before = tb("before").rearrange("p (j m) -> p j m", j=4)
        inv_count = tb("inv_count").rearrange("p (g t) -> p g t", g=4)

        tab_in, x_in, vec_in, pages_in = sem("tab_in"), sem("x_in"), sem("vec_in"), sem("pages_in")
        w_in_s = [sem(f"w_slot{n}_in") for n in range(SLOTS)]
        hi_ready, lo_ready, w_used = sem("hi_ready"), sem("lo_ready"), sem("w_used")
        k_in = [sem("k_in0"), sem("k_in1")]
        v_in = sem("v_in")
        vecT, gains_ready = sem("vec_transposed"), sem("gains_ready")
        xT_in, x_ready = sem("x_transposed"), sem("x_ready")
        sq_ready, sq_added, sq_summed = sem("sq_ready"), sem("sq_added"), sem("sq_summed")
        ms_ready, root_ready, rf_ready = sem("ms_ready"), sem("root_ready"), sem("rf_ready")
        nrm_ready, nrm_hi, h_ready = sem("nrm_ready"), sem("nrm_hi"), sem("h_ready")
        z_ready = sem("z_ready")
        qz_ready = sem("qz_ready")
        kt_in, kt_out, qk_done = sem("kt_in"), sem("kt_out"), sem("qk_done")
        dn_ready, bs_done = sem("dn_ready"), sem("bs_done")
        dm_ready, mx_done, m_ready = sem("dm_ready"), sem("mx_done"), sem("m_ready")
        p_ready, l_done, l_saved = sem("p_ready"), sem("l_done"), sem("l_saved")
        pt_in, pt_ready, v_done = sem("pt_in"), sem("pt_ready"), sem("v_done")
        o6_taken, o7_taken = sem("o6_taken"), sem("o7_taken")
        comb_done, comb_saved = sem("comb_done"), sem("comb_saved")
        tok_in, tok_act, tok_dve = sem("tok_in"), sem("tok_act"), sem("tok_dve")
        hist_in, wpool_in = sem("hist_in"), sem("wpool_in")
        hist_T, ext_ready = sem("hist_transposed"), sem("ext_ready")
        a_in, a_out, a_bias = sem("a_in"), sem("a_out"), sem("a_bias")
        pm_ready, pe_ready, pn_ready = sem("pm_ready"), sem("pexp_ready"), sem("pn_ready")
        pt2_in, pt2_ready, po_in = sem("ptp_in"), sem("ptp_ready"), sem("po_in")
        po_hi, mix_ready = sem("po_hi"), sem("mix_ready")
        d_ready, y_in, y_sc, y_hi, pool_mix = sem("d_ready"), sem("y_in"), sem("y_scaled"), sem("y_hi"), sem("pool_mix")
        qza_ready, so_in, so_sub, so_exp = sem("qza_ready"), sem("so_in"), sem("so_sub"), sem("so_exp")
        own_ready, pTo_in, pTb_ready, t1_in, t2_in = (
            sem("own_ready"), sem("pTo_in"), sem("pTb_ready"), sem("t1_in"), sem("t2_in"))
        smix, smix_hi, smix_ready = sem("smix"), sem("smix_hi"), sem("smix_ready")
        quad_taken = [sem("quadA_taken"), sem("quadB_taken")]
        gs_ready, sg_ready, sr_ready, af_ready, ah_ready, act_ready = (
            sem("gs_ready"), sem("sg_ready"), sem("sr_ready"), sem("af_ready"), sem("ah_ready"), sem("act_ready"))
        fms, froot = sem("fms"), sem("froot")
        xf_ready, fy_in, fy_act, fy_dve = sem("xf_ready"), sem("fy_in"), sem("fy_act"), sem("fy_dve")
        dve_own, act_own, pool_own = sem("dve_own"), sem("act_own"), sem("pool_own")
        stored = sem("stored")

        ck = A["cache_k"][0].rearrange("n t h d -> n t (h d)")
        cv = A["cache_v"][0].rearrange("n t h d -> n t (h d)")
        w_in_d, w_out_d = A["w_in"][0], A["w_out"][0]
        wg_d, wu_d, wd_d = A["w_gate"][0], A["w_up"][0], A["w_down"][0]

        def final_step(n):
            part = n // 4
            return part, n % 4, P if part < 2 else TS

        def pool_chunk(r):
            return 8 + 2 * (3 - r // 2) + r % 2

        def tok_dst(n):
            half_ = n % 2
            kind, part = (n // 2) // 3, (n // 2) % 3
            cols = slice(512 * half_, 512 * half_ + 512)
            if kind < 2 and part < 2:
                return P, (vtok, ktok)[kind][:, part, cols]
            rows, at_ = ((TS, 32 * kind), (TS, 64), (HIST, 96))[0 if kind < 2 else 1 + part]
            return rows, stok[at_:at_ + rows, cols]

        def tok_src(n):
            half_ = n % 2
            kind, part = (n // 2) // 3, (n // 2) % 3
            chunk = (ZV, ZK, ZU)[kind] + 4 * half_
            if kind < 2:
                a = P * part
                return chunk, a, a + (P if part < 2 else TS)
            return (chunk, TP, T) if part == 0 else (chunk, TP - HIST, TP)

        block = ctx.enter_context(nc.Block())

        @block.sync
        def _(sp):
            xp, xsam = A["x_prompt"][0], A["x_sample"].rearrange("b q d -> (b q) d")
            sp.dma_start(tab[:, :], A["tables"]).then_inc(tab_in, 16)
            for n in range(2):
                sp.dma_start(xs[:, n, :], xp[n * P:(n + 1) * P, :]).then_inc(x_in, 16)
            sp.dma_start(xs[0:TS, 2, :], xsam).then_inc(x_in, 16)
            for n, name in enumerate(("norm1_g", "norm2_g", "norm_f_g", "pool_scale")):
                g = A[name] if name == "norm_f_g" else A[name][0]
                sp.dma_start(vec[16 * n:min(16 * n + 16, 56), :], g.rearrange("(c p) -> c p", p=P)).then_inc(vec_in, 16)

            def load(t, src, free=True):
                n, _, s = t
                if free:
                    sp.wait_ge(lo_ready, n - 3)
                w = src.shape[1]
                sp.dma_start(w_raw[:, s, 0:2 * w].rearrange("p (k n) -> p k n", k=2),
                             src.rearrange("(k p) n -> p k n", p=P)).then_inc(w_in_s[s], 16)

            for k in range(16):
                c, j = k // 8, k % 8
                load(tile_at(T_Q + k), w_in_d[256 * j:256 * j + 256, 512 * c:512 * c + 512], free=k >= SLOTS)
            sp.wait_ge(xT_in, KC)
            sp.wait_ge(vecT, 1)
            sp.dma_start(pages[:, :], A["page_table"].rearrange("b n -> (b n)").rearrange("(a n) -> a n", a=1)
                         ).then_inc(pages_in, 16)
            sp.wait_ge(pages_in, 16)

            def page(pool, b, n):
                e = NPAGES * b + n
                idx = sp.value_load(pages[0:1, bass.ds(e, 1)], min_val=0, max_val=pool.shape[0] - 1)
                return pool[bass.ds(idx, 1), :, :].rearrange("a t n -> (a t) n")

            def load_k(i, j, free=True):
                if free:
                    sp.wait_ge(kt_in, 32 * i + 8 * j - 8)
                for g in range(4):
                    sp.dma_start(kpage[:, j % 2, g, :], page(ck, i, 4 * j + g)).then_inc(k_in[j % 2], 16)

            def load_v(i, j, free=True):
                if free:
                    sp.wait_ge(v_done, 4 * i + j - 4)
                for g in range(4):
                    sp.dma_start(vpage[:, g, :], page(cv, i - 1, 4 * j + g)).then_inc(v_in, 16)

            def stream(i, has_v, next_k=True, first_v=False):
                for j in range(NQUADS):
                    for k in (2 * j, 2 * j + 1):
                        load(tile_at(T_KVU + k, i, 8), w_in_d[256 * k:256 * k + 256, bass.ds(AW + CW * i, CW)])
                    if j < NQUADS - 1:
                        load_k(i, j + 1, not (j == 0 and not has_v))
                    elif next_k:
                        load_k(i + 1, 0)
                    if has_v:
                        load_v(i, j, not (first_v and j == 0))

            load_k(0, 0, False)
            stream(0, False)
            stream(1, True, first_v=True)
            with sp.Fori(2, NB - 1) as i:
                stream(i, True)
            stream(NB - 1, True, next_k=False)
            sp.wait_ge(qk_done, 32 * NB)
            sp.dma_start(hist[:, :], A["state_pool"][0].rearrange("b i c -> (b i) c")).then_inc(hist_in, 16)
            load_v(NB, 0)
            sp.dma_start(wpool[:, :, :, :], A["w_pool"][0].rearrange("g (k p) e -> p g k e", p=P)).then_inc(wpool_in, 16)
            load_v(NB, 1)

            def load_out(k):
                c, j = k // 8, k % 8
                load(tile_at(T_OUT + k), w_out_d[256 * j:256 * j + 256, 512 * c:512 * c + 512])

            for k in range(4):
                load_out(k)
            load_v(NB, 2)
            load_v(NB, 3)
            for k in range(4, 8):
                load_out(k)
            n_stores = 0

            def store(dst, src):
                nonlocal n_stores
                sp.dma_start(dst, src).then_inc(stored, 16)
                n_stores += 1

            kp, vp = O["k_prompt"][0, 0].rearrange("t h d -> t (h d)"), O["v_prompt"][0, 0].rearrange("t h d -> t (h d)")
            ks = O["k_sample"][0].rearrange("b q h d -> (b q) (h d)")
            vs = O["v_sample"][0].rearrange("b q h d -> (b q) (h d)")
            sp.wait_ge(tok_act, 8)
            sp.wait_ge(tok_dve, 8)
            for n in range(2):
                store(kp[n * P:(n + 1) * P, :], ktok[:, n, :])
                store(vp[n * P:(n + 1) * P, :], vtok[:, n, :])
            store(vs, stok[0:TS, :])
            store(ks, stok[TS:2 * TS, :])
            store(O["pool_prompt"][0, 0], stok[96:96 + HIST, :])
            store(O["pool_sample"][0, :, 0:HIST - NQ, :], A["state_pool"][0, :, NQ:HIST, :])
            for b in range(NB):
                store(O["pool_sample"][0, b, HIST - NQ:HIST, :], stok[64 + NQ * b:64 + NQ * b + NQ, :])
            for k in range(8, 16):
                load_out(k)
            with sp.Fori(1, 2) as i:
                for k in range(16):
                    src = w_out_d[256 * (k % 8):256 * (k % 8) + 256, bass.ds(1024 * i + 512 * (k // 8), 512)]
                    load(tile_at(T_OUT + k, i, 16), src)

            def load_gu(w, t0, g):
                for k in range(8):
                    load(tile_at(*((t0[0] + k,) + t0[1:])), w[256 * k:256 * k + 256, bass.ds(512 * g, 512)])

            def load_down(t0, g):
                for k in range(8):
                    c, j = k // 2, k % 2
                    load(tile_at(*((t0[0] + k,) + t0[1:])),
                         wd_d[bass.ds(512 * g + 256 * j, 256), 512 * c:512 * c + 512])

            load_gu(wg_d, (T_FF,), 0)
            with sp.Fori(0, NG - 1) as g:
                load_gu(wu_d, (T_FF + 8, g, 24), g)
                load_gu(wg_d, (T_FF + 16, g, 24), g + 1)
                load_down((T_FF + 24, g, 24), g)
            load_gu(wu_d, (T_END - 16,), NG - 1)
            load_down((T_END - 8,), NG - 1)
            for n in range(3):
                rows = P if n < 2 else TS
                sp.wait_ge(fy_act, 2 * n + 2)
                sp.wait_ge(fy_dve, 2 * n + 2)
                dst = O["y_prompt"][0, n * P:(n + 1) * P, :] if n < 2 else O["y_sample"].rearrange("b q d -> (b q) d")
                store(dst, yt[0:rows, n, :])
            sp.wait_ge(stored, 16 * n_stores)

        @block.scalar
        def _(act):
            own = Steps(act, act_own)

            def copy(out, in_):
                return nc.scalar.activation(out, in_, ACT.Copy)

            def hi(t, free=True):
                n, turn, s = t
                act.wait_ge(w_in_s[s], 16 * turn + 16)
                if free:
                    act.wait_ge(w_used, n - 3)
                copy(w_hi[:, s, :], w_raw[:, s, :]).then_inc(hi_ready, 1)

            def square(stage, c):
                n = KC * stage + c
                if n >= 2:
                    act.wait_ge(sq_added, n - 1)
                nc.scalar.activation(sq[:, c % 2, :], xT[:, c, :], ACT.Square).then_inc(sq_ready, 1)

            def gained(stage, c):
                act.wait_ge(nrm_ready, KC * stage + c + 1)
                copy(hh[:, c, :], nrm[:, c % 2, :]).then_inc(nrm_hi, 1)

            def root(stage):
                act.wait_ge(ms_ready, stage + 1)
                nc.scalar.activation(rstd[:, :], ms[:, :], ACT.Sqrt).then_inc(root_ready, 1)

            for c in range(KC):
                act.wait_ge(x_ready, c + 1)
                gained(0, c)
                square(0, c)
                if c % 2:
                    hi(tile_at(c // 2), c // 2 >= SLOTS)
            for k in range(4, 6):
                hi(tile_at(4 + k))
            root(0)
            for k in range(6, 12):
                hi(tile_at(4 + k))

            def kv_step(i, has_v, has_comb, first=False):
                for j in range(NQUADS):
                    for h in range(H):
                        n = 32 * i + 8 * j + h
                        act.wait_ge(kt_in, n + 1)
                        if not (first and j == 0 and h < 2):
                            act.wait_ge(qk_done, n - 1)
                        copy(kT[:, h % 2, :], KTP[h % 2][:, :]).then_inc(kt_out, 1)
                        if j == 0 and h == 4 and has_comb:
                            save_comb(i - 2, i - 1)
                    if j == 0 and has_v:
                        softmax_late(i)
                if has_v:
                    act.wait_ge(v_done, 4 * i)
                    if has_comb:
                        act.wait_ge(comb_done, i - 1)
                    copy(osb[:, 0:512], OB[0][:, :]).then_inc(o6_taken, 1)

            def save_comb(b, count):
                act.wait_ge(comb_done, count)
                copy(o_all[:, bass.ds(b, 1), :].rearrange("p a d -> p (a d)"), OB[0][0:32, 0:DH]).then_inc(comb_saved, 1)

            def softmax_late(i):
                act.wait_ge(m_ready, i)
                nc.scalar.activation(ss[:, :, :], ss[:, :, :], ACT.Exp, bias=negm[:, 0:1],
                                     accum_out=lsum[:, 0:1]).then_inc(p_ready, 1)
                act.wait_ge(pt_in, i)
                copy(pT[:, :, :], OB[0][:, :].rearrange("p (j k) -> p j k", j=4)).then_inc(pt_ready, 1)

            kv_step(0, False, False, first=True)
            kv_step(1, True, False)
            with act.Fori(2, NB) as i:
                kv_step(i, True, True)

            def rows_out(n):
                act.wait_ge(tok_in, n + 1)
                rows, dst = tok_dst(n)
                copy(dst, bank[n % 4][0:rows, :]).then_inc(tok_act, 1)

            rows_out(0)
            save_comb(NB - 2, NB - 1)
            rows_out(2)
            rows_out(4)
            softmax_late(NB)

            def mixed_hi(r):
                act.wait_ge(y_sc, r + 1)
                copy(hh[:, pool_chunk(r), :], nrm[:, r % 2, :]).then_inc(y_hi, 1)

            for s in range(H + 2):
                if s < H:
                    act.wait_ge(a_in, s + 1)
                    if s >= 2:
                        act.wait_ge(pt2_in, s - 1)
                    nc.scalar.activation(px[:, s % 2, :], bank[4 + s % 2][:, 0:384], ACT.Copy, scale=SCALE).then_inc(a_out, 1)
                if 1 <= s <= H:
                    u = (s - 1) % 2
                    act.wait_ge(pm_ready, 2 * s)
                    for n, (a, b) in enumerate(((0, P), (P, 384))):
                        nc.scalar.activation(px[:, u, a:b], px[:, u, a:b], ACT.Exp, bias=pm[:, u, n:n + 1],
                                             accum_out=pl[:, u, n:n + 1]).then_inc(pe_ready, 1)
                if s >= 2:
                    h = s - 2
                    act.wait_ge(pt2_in, h + 1)
                    if h >= 2:
                        act.wait_ge(po_in, h - 1)
                    copy(ptp[:, h % 2, :], bank[h % 2][:, 0:384]).then_inc(pt2_ready, 1)
                if s >= 3:
                    act.wait_ge(po_in, s - 2)
                    copy(hh[:, s - 3, 0:TP], bank[2 + (s - 3) % 2][:, 0:TP]).then_inc(po_hi, 1)
            mixed_hi(0)
            mixed_hi(1)
            act.wait_ge(po_in, H)
            copy(hh[:, H - 1, 0:TP], bank[2 + (H - 1) % 2][:, 0:TP]).then_inc(po_hi, 1)
            act.wait_ge(v_done, 4 * NB)
            act.wait_ge(comb_done, NB - 1)
            copy(osb[:, 0:512], OB[0][:, :]).then_inc(o6_taken, 1)
            save_comb(NB - 1, NB)
            act.wait_ge(so_sub, 2)
            nc.scalar.activation(so[:, :, :], so[:, :, :], ACT.Exp).then_inc(so_exp, 1)
            nc.scalar.activation(eo[:, :], eo[:, :], ACT.Exp).then_inc(so_exp, 1)
            for n in range(6, 16, 2):
                rows_out(n)
            mixed_hi(2)
            mixed_hi(3)
            for k in range(SLOTS):
                hi(tile_at(T_OUT + k))
            act.wait_ge(smix, 1)
            copy(hh[:, 0:H, TP:T], mixs[:, :, :]).then_inc(smix_hi, 1)
            for r in range(4, 8):
                mixed_hi(r)
            with act.Fori(0, 2) as i:
                for k in range(16):
                    hi(tile_at(T_OUT + 4 + k, i, 16))
            for c in range(KC):
                gained(1, c)
                act.wait_ge(quad_taken[c // 4 % 2], QT0 + 4 * (c // 8) + c % 4 + 1)
                square(1, c)
                if c % 2 and c >= 5:
                    hi(tile_at(T_FF + 4 + (c - 5) // 2))
            hi(tile_at(T_FF + 10))
            root(1)
            hi(tile_at(T_FF + 11))

            def silu(g):
                for m in range(4):
                    act.wait_ge(gs_ready, 4 * g + m + 1)
                    nc.scalar.activation(sg[:, m, :], sg[:, m, :], ACT.Silu).then_inc(sg_ready, 1)

            def act_hi(g):
                for m in range(4):
                    act.wait_ge(af_ready, 4 * g + m + 1)
                    copy(ah[:, m, :], af[:, m % 2, :]).then_inc(ah_ready, 1)

            silu(0)
            with act.Fori(0, NG - 1) as g:
                for k in range(24):
                    hi(tile_at(T_FF + 12 + k, g, 24))
                    if k == 7:
                        act_hi(g)
                    if k == 15:
                        silu(g + 1)
            for k in range(12):
                hi(tile_at(T_END - 12 + k))
                if k == 7:
                    act_hi(NG - 1)
            for c in range(KC):
                act.wait_ge(x_ready, KC + c + 1)
                square(2, c)
            act.wait_ge(fms, 3)
            nc.scalar.activation(rf[:, :], fm[:, :], ACT.Sqrt).then_inc(froot, 1)
            act.wait_ge(rf_ready, 1)
            for n in range(0, 12, 2):
                part, c, rows = final_step(n)
                act.wait_ge(fy_in, n + 1)
                nc.scalar.activation(yt[0:rows, part, 512 * c:512 * c + 512], bank[n % 8][0:rows, :], ACT.Copy,
                                     scale=rf[0:rows, part:part + 1]).then_inc(fy_act, 1)

        @block.vector
        def _(dve):
            own = Steps(dve, dve_own)
            V = nc.vector

            def lo(t, width=TE):
                n, _, s = t
                dve.wait_ge(hi_ready, n + 1)
                V.tensor_tensor(w_lo[:, s, 0:width], w_raw[:, s, 0:width], w_hi[:, s, 0:width].bitcast(F32),
                                ALU.subtract).then_inc(lo_ready, 1)

            def hi_lo(t):
                n, turn, s = t
                dve.wait_ge(w_in_s[s], 16 * turn + 16)
                dve.wait_ge(w_used, n - 3)
                V.tensor_copy(w_hi[:, s, 0:2 * CW], w_raw[:, s, 0:2 * CW]).then_inc(hi_ready, 1)
                lo(t, 2 * CW)

            def gained(stage, c):
                if KC * stage + c >= 2:
                    dve.wait_ge(h_ready, KC * stage + c - 1)
                V.tensor_scalar(nrm[:, c % 2, :], xT[:, c, :], gains[:, 16 * stage + c:16 * stage + c + 1], None,
                                ALU.mult).then_inc(nrm_ready, 1)

            def gained_lo(stage, c):
                dve.wait_ge(nrm_hi, KC * stage + c + 1)
                V.tensor_tensor(hl[:, c, :], nrm[:, c % 2, :], hh[:, c, :].bitcast(F32),
                                ALU.subtract).then_inc(h_ready, 1)

            def mean_sq(stage):
                dve.wait_ge(sq_summed, stage + 1)
                V.tensor_scalar(ms[:, :], bank[7][:, 0:T], 1.0 / D, EPS, ALU.mult, ALU.add).then_inc(ms_ready, 1)

            def inverse_root(r, mean, tmp):
                own.link(V.reciprocal(r, r))
                own.link(V.tensor_tensor(tmp, r, r, ALU.mult))
                own.link(V.tensor_tensor(tmp, tmp, mean, ALU.mult))
                own.link(V.tensor_scalar(tmp, tmp, -0.5, 1.5, ALU.mult, ALU.add))
                return V.tensor_tensor(r, r, tmp, ALU.mult)

            def rstd_of(stage):
                dve.wait_ge(root_ready, stage + 1)
                dve.wait_ge(h_ready, KC * stage + KC)
                own.link(inverse_root(rstd[:, :], ms[:, :], nrm[:, 0, :]))

            dve.wait_ge(vecT, 1)
            V.tensor_copy(gains[:, :], bank[6][:, 0:56]).then_inc(gains_ready, 1)
            dve.wait_ge(gains_ready, 1)
            for c in range(KC + 1):
                if c < KC:
                    dve.wait_ge(xT_in, c + 1)
                    V.tensor_copy(xT[:, c, :], bank[4 + c % 2][:, 0:T]).then_inc(x_ready, 1)
                    dve.wait_ge(x_ready, c + 1)
                    gained(0, c)
                if c:
                    gained_lo(0, c - 1)
                    if c % 2 == 0:
                        lo(tile_at(c // 2 - 1))
            for k in range(4, 6):
                lo(tile_at(4 + k))
            mean_sq(0)
            rstd_of(0)
            own.link(V.memset(qz[:, :], 0.0))
            for k in range(6, 16):
                if k < 12:
                    lo(tile_at(4 + k))
                if k % 8 == 7:
                    c = k // 8
                    dve.wait_ge(w_used, T_Q + 8 * c + 8)
                    for m in range(4):
                        V.tensor_tensor(z[:, 4 * c + m, :], bank[4 * c + m][:, 0:T], rstd[:, :],
                                        ALU.mult).then_inc(quad_taken[c], 1)
            for c in range(2):
                dve.wait_ge(quad_taken[c], QT0)

            def pad_q(b):
                cols = bass.ds(TP + NQ * b, NQ)
                return V.tensor_copy(qz[:, :].rearrange("p (h s) -> p h s", s=36)[:, :, 0:NQ], z[:, ZQ:ZQ + H, cols])

            def scaled_logits(i, has_comb):
                if has_comb:
                    dve.wait_ge(pt_in, i - 1)
                own.did(V.scalar_tensor_tensor(ss[:, :, :].rearrange("p j k -> p (j k)"), S[:, :], SCALE, past_bias,
                                               ALU.mult, ALU.add))
                own.did(V.tensor_reduce(d4[:, :], S[:, :].rearrange("p (j k) -> p j k", j=4), AX.X, ALU.add))
                own.settle()
                V.tensor_tensor(dn[:, :, :], d4[:, :].unsqueeze(2).to_broadcast([P, 4, 2]),
                                half.unsqueeze(1).to_broadcast([P, 4, 2]), ALU.mult).then_inc(dn_ready, 1)

            def select_blocks(i):
                dve.wait_ge(bs_done, i)
                own.link(V.tensor_copy(bsc[:, :], OB[1][:, 0:8]))
                own.link(V.tensor_tensor(bsh[:, :, :], bsc[:, :].rearrange("p (j u) -> p j u", u=2),
                                         half.unsqueeze(1).to_broadcast([P, 4, 2]), ALU.mult))
                own.link(V.tensor_reduce(bown[:, :], bsh[:, :, :], AX.X, ALU.add))
                every = bsc[:, :].unsqueeze(1).to_broadcast([P, 4, 8])
                mine = bown[:, :].unsqueeze(2).to_broadcast([P, 4, 8])
                own.did(V.tensor_tensor(gt[:, :, :], every, mine, ALU.is_gt))
                own.link(V.tensor_tensor(eq[:, :, :], every, mine, ALU.is_equal))
                own.link(V.tensor_tensor(eq[:, :, :], eq[:, :, :], before, ALU.mult))
                own.link(V.tensor_tensor(gt[:, :, :], gt[:, :, :], eq[:, :, :], ALU.add))
                own.link(V.tensor_reduce(cnt[:, :], gt[:, :, :], AX.X, ALU.add))
                own.link(V.tensor_scalar(cnt[:, :], cnt[:, :], float(TOPK), NEG, ALU.is_ge, ALU.mult))
                own.link(V.tensor_tensor(ss[:, :, :], ss[:, :, :], cnt[:, :].unsqueeze(2).to_broadcast([P, 4, P]),
                                         ALU.add))
                own.link(V.tensor_reduce(mx[:, :], ss[:, :, :].rearrange("p j k -> p (j k)"), AX.X, ALU.max))
                V.tensor_scalar(dm[:, :], tb("gsel"), mx[:, 0:1], None, ALU.mult).then_inc(dm_ready, 1)

            def joint_max(i):
                dve.wait_ge(mx_done, i)
                own.link(V.tensor_reduce(mx[:, :], OB[1][:, 8:12], AX.X, ALU.max))
                V.tensor_scalar(negm[:, :], mx[:, :], -1.0, None, ALU.mult).then_inc(m_ready, 1)
                own.did(V.tensor_copy(m_all[:, bass.ds(i - 1, 1)], mx[0:32, :]))

            def joint_sum(i):
                dve.wait_ge(l_done, i)
                V.tensor_copy(l_all[:, bass.ds(i - 1, 1)], OB[1][0:32, 12:13]).then_inc(l_saved, 1)

            def kv_step(i, has_v, has_comb):
                if has_v:
                    dve.wait_ge(qk_done, 32 * i)
                pad_q(i).then_inc(qz_ready, 1)
                if has_v:
                    scaled_logits(i, has_comb)
                    select_blocks(i)
                hi_lo(tile_at(T_KVU, i, 8))
                if has_v:
                    joint_max(i)
                hi_lo(tile_at(T_KVU + 1, i, 8))
                if has_v:
                    joint_sum(i)
                for k in range(2, 8):
                    hi_lo(tile_at(T_KVU + k, i, 8))
                dve.wait_ge(w_used, T_KVU + 8 + 8 * i)
                for m in range(3):
                    V.tensor_tensor(z[:, bass.ds(ZK + 3 * i + m, 1), :].rearrange("p a t -> p (a t)"),
                                    WB[m][:, 0:T], rstd[:, :], ALU.mult).then_inc(z_ready, 1)
                if has_v:
                    dve.wait_ge(v_done, 4 * i)
                    if has_comb:
                        dve.wait_ge(comb_done, i - 1)
                    V.tensor_copy(osb[:, 512:1024], OB[1][:, :]).then_inc(o7_taken, 1)

            kv_step(0, False, False)
            kv_step(1, True, False)
            done, own.k = own.k, 0
            with dve.Fori(2, NB) as i:
                own.base = done + DVE_STEPS * (i - 2)
                kv_step(i, True, True)
                assert own.k == DVE_STEPS
            own.base, own.k = done + DVE_STEPS * (NB - 2), 0

            def rows_out(n):
                dve.wait_ge(tok_in, n + 1)
                rows, dst = tok_dst(n)
                V.tensor_copy(dst, bank[n % 4][0:rows, :]).then_inc(tok_dve, 1)

            dve.wait_ge(qk_done, 32 * NB)
            scaled_logits(NB, True)
            rows_out(1)
            select_blocks(NB)
            rows_out(3)
            joint_max(NB)
            rows_out(5)
            joint_sum(NB)
            dve.wait_ge(hist_T, 1)
            for n in range(2):
                V.tensor_copy(ext[:, 4 * n:4 * n + 4, :, 0:HIST],
                              bank[2 + n][:, 0:480].rearrange("p (c b i) -> p c b i", c=4, b=NB)).then_inc(ext_ready, 1)

            def mixed_lo(r):
                c = pool_chunk(r)
                dve.wait_ge(y_in, r + 1)
                if r >= 2:
                    dve.wait_ge(pool_mix, r - 1)
                V.tensor_scalar(nrm[:, r % 2, :], bank[4 + r % 2][:, 0:T], gains[:, 40 + c:41 + c], None,
                                ALU.mult).then_inc(y_sc, 1)
                dve.wait_ge(y_hi, r + 1)
                V.tensor_tensor(hl[:, c, :], nrm[:, r % 2, :], hh[:, c, :].bitcast(F32),
                                ALU.subtract).then_inc(pool_mix, 1)

            def head_lo(h):
                dve.wait_ge(po_hi, h + 1)
                V.tensor_tensor(hl[:, h, 0:TP], bank[2 + h % 2][:, 0:TP], hh[:, h, 0:TP].bitcast(F32),
                                ALU.subtract).then_inc(mix_ready, 1)

            for s in range(H + 2):
                if s < H:
                    dve.wait_ge(a_out, s + 1)
                    own.link(V.scalar_tensor_tensor(px[:, s % 2, :], tb("rel"), 2.0 ** -(s + 1), px[:, s % 2, :],
                                                    ALU.mult, ALU.add))
                    for n, (a, b) in enumerate(((0, P), (P, 384))):
                        V.tensor_reduce(pm[:, s % 2, n:n + 1], px[:, s % 2, a:b], AX.X, ALU.max,
                                        negate=True).then_inc(pm_ready, 1)
                if 1 <= s <= H:
                    u = (s - 1) % 2
                    dve.wait_ge(pe_ready, 2 * s)
                    own.link(V.reciprocal(pl[:, u, :], pl[:, u, :]))
                    for n, (a, b) in enumerate(((0, P), (P, 384))):
                        V.tensor_scalar(px[:, u, a:b], px[:, u, a:b], pl[:, u, n:n + 1], None,
                                        ALU.mult).then_inc(pn_ready, 1)
                if s >= 3:
                    head_lo(s - 3)
            mixed_lo(0)
            mixed_lo(1)
            head_lo(H - 1)
            dve.wait_ge(v_done, 4 * NB)
            dve.wait_ge(comb_done, NB - 1)
            V.tensor_copy(osb[:, 512:1024], OB[1][:, :]).then_inc(o7_taken, 1)
            dve.wait_ge(comb_done, NB)
            own.link(V.memset(qza[:, :, :], 0.0))
            V.tensor_copy(qza[:, :, :].rearrange("p b (h s) -> p b h s", s=36)[:, :, :, 0:NQ],
                          z[:, ZQ:ZQ + H, TP:T].rearrange("p h (b q) -> p b h q", b=NB)).then_inc(qza_ready, 1)
            dve.wait_ge(so_in, 1)
            own.link(V.scalar_tensor_tensor(so[:, :, :], bank[7][0:32, 0:32].rearrange("p (b k) -> p b k", b=NB), SCALE,
                                            tb("own_bias")[0:32, :].unsqueeze(1).to_broadcast([32, NB, NQ]),
                                            ALU.mult, ALU.add))
            own.link(V.tensor_reduce(mo[:, :], so[:, :, :], AX.X, ALU.max))
            own.link(V.tensor_tensor(mm_[:, :], mo[:, :], m_all[:, :], ALU.max))
            V.tensor_tensor(so[:, :, :], so[:, :, :], mm_[:, :].unsqueeze(2).to_broadcast([32, NB, NQ]),
                            ALU.subtract).then_inc(so_sub, 1)
            V.tensor_tensor(eo[:, :], m_all[:, :], mm_[:, :], ALU.subtract).then_inc(so_sub, 1)
            for n in range(7, 16, 2):
                rows_out(n)
            mixed_lo(2)
            mixed_lo(3)
            for k in range(SLOTS):
                lo(tile_at(T_OUT + k))
            dve.wait_ge(so_exp, 2)
            dve.wait_ge(l_saved, NB)
            own.did(V.tensor_reduce(lo_[:, :], so[:, :, :], AX.X, ALU.add))
            own.did(V.tensor_tensor(mo[:, :], l_all[:, :], eo[:, :], ALU.mult))
            own.settle()
            own.link(V.tensor_tensor(lo_[:, :], lo_[:, :], mo[:, :], ALU.add))
            own.link(V.reciprocal(lo_[:, :], lo_[:, :]))
            own.did(V.tensor_tensor(so[:, :, :], so[:, :, :], lo_[:, :].unsqueeze(2).to_broadcast([32, NB, NQ]), ALU.mult))
            own.link(V.tensor_tensor(eo[:, :], eo[:, :], lo_[:, :], ALU.mult))
            dve.wait_ge(comb_saved, NB)
            V.tensor_tensor(o_all[:, :, :], o_all[:, :, :], eo[:, :].unsqueeze(2).to_broadcast([32, NB, DH]),
                            ALU.mult).then_inc(own_ready, 1)
            dve.wait_ge(pTo_in, 1)
            own.link(V.tensor_copy(pTo[:, :], bank[6][0:32, 0:32]))
            V.tensor_tensor(pTb[:, :, :, :], pTo[:, :].rearrange("p (h q) -> p h q", h=H).unsqueeze(2).to_broadcast(
                [32, H, NB, NQ]), tb("batch_of")[0:32, :].unsqueeze(1).unsqueeze(3).to_broadcast([32, H, NB, NQ]),
                ALU.mult).then_inc(pTb_ready, 1)
            dve.wait_ge(t1_in, 1)
            own.link(V.tensor_copy(t1[:, :, :], bank[6][:, 0:256].rearrange("p (b c) -> p b c", b=NB)))
            dve.wait_ge(t2_in, 1)
            V.tensor_tensor(mixs[:, :, :].rearrange("p h (b q) -> p h b q", b=NB),
                            bank[7][:, 0:256].rearrange("p (h b q) -> p h b q", h=H, b=NB),
                            t1[:, :, :].rearrange("p b (h q) -> p h b q", h=H), ALU.add).then_inc(smix, 1)
            dve.wait_ge(smix_hi, 1)
            V.tensor_tensor(hl[:, 0:H, TP:T], mixs[:, :, :], hh[:, 0:H, TP:T].bitcast(F32),
                            ALU.subtract).then_inc(smix_ready, 1)
            for r in range(4, 8):
                mixed_lo(r)

            def add_group(quad, m0, used):
                dve.wait_ge(w_used, used)
                for m in range(4):
                    ins = V.tensor_tensor(xT[:, m0 + m, :], xT[:, m0 + m, :], bank[4 * quad + m][:, 0:T], ALU.add)
                    ins.then_inc(quad_taken[quad], 1)

            def add_out(quad, c, used):
                dve.wait_ge(w_used, used)
                for m in range(4):
                    chunk = xT[:, bass.ds(4 * c + m, 1), :].rearrange("p a t -> p (a t)")
                    V.tensor_tensor(chunk, chunk, bank[4 * quad + m][:, 0:T], ALU.add).then_inc(quad_taken[quad], 1)

            with dve.Fori(0, 2) as i:
                for k in range(16):
                    lo(tile_at(T_OUT + 4 + k, i, 16))
                    if k % 8 == 7:
                        quad = k // 8
                        add_out(quad, 2 * i + quad, T_OUT + 16 * i + 8 * quad + 8)
            for c in range(KC + 1):
                if c < KC:
                    gained(1, c)
                if c:
                    gained_lo(1, c - 1)
                    if c % 2 == 0 and c >= 6:
                        lo(tile_at(T_FF + 4 + (c - 6) // 2))
            lo(tile_at(T_FF + 10))
            mean_sq(1)
            rstd_of(1)
            lo(tile_at(T_FF + 11))

            def gate_scaled(g):
                if not isinstance(g, int):
                    dve.wait_ge(af_ready, 4 * g)
                dve.wait_ge(w_used, T_FF + 8 if isinstance(g, int) else T_FF + 24 * g)
                for m in range(4):
                    V.tensor_tensor(sg[:, m, :], bank[m][:, 0:T], rstd[:, :], ALU.mult).then_inc(gs_ready, 1)

            def up_scaled(g):
                for m in range(4):
                    dve.wait_ge(sg_ready, 4 * g + m + 1)
                    V.tensor_tensor(sg[:, m, :], sg[:, m, :], rstd[:, :], ALU.mult).then_inc(sr_ready, 1)

            def mul_act(g):
                def product(m):
                    dve.wait_ge(sr_ready, 4 * g + m + 1)
                    if m >= 2:
                        dve.wait_ge(act_ready, 4 * g + m - 1)
                    V.tensor_tensor(af[:, m % 2, :], sg[:, m, :], bank[4 + m][:, 0:T], ALU.mult).then_inc(af_ready, 1)

                dve.wait_ge(w_used, T_FF + 16 + 24 * g)
                product(0)
                for m in range(4):
                    if m < 3:
                        product(m + 1)
                    dve.wait_ge(ah_ready, 4 * g + m + 1)
                    V.tensor_tensor(al[:, m, :], af[:, m % 2, :], ah[:, m, :].bitcast(F32),
                                    ALU.subtract).then_inc(act_ready, 1)

            gate_scaled(0)
            up_scaled(0)
            with dve.Fori(0, NG - 1) as g:
                for k in range(24):
                    lo(tile_at(T_FF + 12 + k, g, 24))
                    if k == 7:
                        mul_act(g)
                    if k == 15:
                        gate_scaled(g + 1)
                    if k == 16:
                        up_scaled(g + 1)
                    if k >= 16 and k % 2 == 1:
                        c = (k - 17) // 2
                        add_group((c + 1) % 2, 4 * c, T_FF + 24 + 24 * g + 2 * c + 2)
            for k in range(12):
                lo(tile_at(T_END - 12 + k))
                if k == 7:
                    mul_act(NG - 1)
            dve.wait_ge(stored, 16 * STORES)
            own.link(V.memset(fm[:, :], 1.0))

            def final_gain(c):
                dve.wait_ge(sq_ready, 2 * KC + c + 1)
                V.tensor_scalar(xT[:, c, :], xT[:, c, :], gains[:, 32 + c:33 + c], None, ALU.mult).then_inc(xf_ready, 1)

            for c in range(5):
                if c < 4:
                    dve.wait_ge(w_used, T_END - 8 + 2 * c + 2)
                    for m in range(4):
                        V.tensor_tensor(xT[:, 4 * c + m, :], xT[:, 4 * c + m, :], bank[4 * (c % 2) + m][:, 0:T],
                                        ALU.add).then_inc(x_ready, 1)
                if c:
                    for m in range(4):
                        final_gain(4 * c - 4 + m)
            dve.wait_ge(sq_summed, 3)
            for n in range(3):
                rows = P if n < 2 else TS
                V.tensor_scalar(fm[0:rows, n:n + 1], bank[4 + n][0:rows, 0:1], 1.0 / D, EPS, ALU.mult,
                                ALU.add).then_inc(fms, 1)
            dve.wait_ge(froot, 1)
            inverse_root(rf[:, :], fm[:, :], ft[:, :]).then_inc(rf_ready, 1)
            dve.wait_ge(rf_ready, 1)
            for n in range(1, 12, 2):
                part, c, rows = final_step(n)
                dve.wait_ge(fy_in, n + 1)
                V.tensor_scalar(yt[0:rows, part, 512 * c:512 * c + 512], bank[n % 8][0:rows, :],
                                rf[0:rows, part:part + 1], None, ALU.mult).then_inc(fy_dve, 1)

        @block.gpsimd
        def _(pool):
            own = Steps(pool, pool_own)
            G = nc.gpsimd

            def sum_squares(stage):
                for c in range(KC):
                    n = KC * stage + c
                    pool.wait_ge(sq_ready, n + 1)
                    if c == 0:
                        if stage:
                            pool.wait_ge(sq_summed, stage)
                        G.tensor_copy(ssq[:, :], sq[:, 0, :]).then_inc(sq_added, 1)
                    else:
                        pool.wait_ge(sq_added, n)
                        G.tensor_tensor(ssq[:, :], ssq[:, :], sq[:, c % 2, :], ALU.add).then_inc(sq_added, 1)

            sum_squares(0)
            pool.wait_ge(sq_added, KC)
            pool.wait_ge(z_ready, 3 * NB)
            d = sq[:, :, :]
            L = HIST + NQ
            for r, g in enumerate((3, 2, 1, 0)):
                w = WINDOWS[g]
                src, n, shift = z[:, ZU + 2 * g:ZU + 2 * g + 2, 0:TP], 0, 1
                while shift < w:
                    dst = win[:, n % 2, :, :]
                    own.did(G.tensor_copy(dst[:, :, 0:shift], src[:, :, 0:shift]))
                    own.did(G.tensor_tensor(dst[:, :, shift:TP], src[:, :, shift:TP], src[:, :, 0:TP - shift], ALU.add))
                    own.settle()
                    src, n, shift = dst, n + 1, 2 * shift
                if r:
                    pool.wait_ge(y_in, 2 * r)
                own.did(G.tensor_tensor(d[:, :, 0:16], src[:, :, 0:16],
                                        inv_count[:, g, :].unsqueeze(1).to_broadcast([P, 2, 16]), ALU.mult))
                own.did(G.tensor_scalar(d[:, :, 16:TP], src[:, :, 16:TP], 1.0 / w, None, ALU.mult))
                if r == 0:
                    pool.wait_ge(ext_ready, 2)
                for c in range(2):
                    own.did(G.tensor_copy(ext[:, 2 * g + c, :, HIST:L],
                                          z[:, ZU + 2 * g + c, TP:T].rearrange("p (b q) -> p b q", b=NB)))
                own.settle()
                src, n, shift = ext[:, 2 * g:2 * g + 2, :, :], 0, 1
                while shift < w:
                    dst = wins[:, n % 2, :, :, :]
                    for c in range(2):
                        own.did(G.tensor_tensor(dst[:, c, :, 2 * shift - 1:L], src[:, c, :, 2 * shift - 1:L],
                                                src[:, c, :, shift - 1:L - shift], ALU.add))
                    own.settle()
                    src, n, shift = dst, n + 1, 2 * shift
                for c in range(2):
                    own.did(G.tensor_scalar(d[:, c, TP:T].rearrange("p (b q) -> p b q", b=NB), src[:, c, :, HIST:L],
                                            1.0 / w, None, ALU.mult))
                own.settle()
                G.tensor_tensor(d, d, z[:, ZU + 2 * g:ZU + 2 * g + 2, :], ALU.subtract).then_inc(d_ready, 1)
                pool.wait_ge(d_ready, r + 1)
            sum_squares(1)
            sum_squares(2)

        @block.tensor
        def _(pe):
            PE = nc.tensor

            def w_tile(t, width, chunks, banks, xh, xl, start, stop):
                n, _, s = t
                pe.wait_ge(lo_ready, n + 1)
                for m, out in enumerate(banks):
                    for i, c in enumerate(chunks):
                        a = width * i + P * m
                        wh, wl = w_hi[:, s, a:a + P], w_lo[:, s, a:a + P]
                        o = out[:, 0:T]
                        PE.matmul(o, wh, xh[:, c, :], start=start and i == 0, stop=False)
                        PE.matmul(o, wh, xl[:, c, :], start=False, stop=False)
                        last = PE.matmul(o, wl, xh[:, c, :], start=False, stop=stop and i == 1)
                last.then_inc(w_used, 1)

            def turn(out, in_, rows):
                return PE.transpose(out, in_, ident[0:rows, 0:rows])

            pe.wait_ge(tab_in, 16)
            pe.wait_ge(vec_in, 64)
            turn(bank[6][:, 0:56], vec[:, :], 56).then_inc(vecT, 1)
            pe.wait_ge(x_in, 48)

            def x_turned(c):
                if c >= 2:
                    pe.wait_ge(x_ready, c - 1)
                for n in range(3):
                    rows = P if n < 2 else TS
                    last = turn(bank[4 + c % 2][:, P * n:P * n + rows], xs[0:rows, n, P * c:P * c + P], rows)
                last.then_inc(xT_in, 1)

            def sum_sq(stage):
                pe.wait_ge(sq_added, KC * stage + KC)
                PE.matmul(bank[7][:, 0:T], ones, ssq[:, :], start=True, stop=True).then_inc(sq_summed, 1)

            for c in range(2):
                x_turned(c)
            for k in range(16):
                c, j = k // 8, k % 8
                if c == 0:
                    for n in (2 * j + 2, 2 * j + 3):
                        if n < KC:
                            x_turned(n)
                    pe.wait_ge(h_ready, 2 * j + 2)
                if k == 8:
                    sum_sq(0)
                    pe.wait_ge(ms_ready, 1)
                w_tile(tile_at(k), 512, (2 * j, 2 * j + 1), bank[4 * c:4 * c + 4], hh, hl, j == 0, j == 7)

            def block_sums(i, has_comb):
                pe.wait_ge(dn_ready, i)
                if has_comb:
                    pe.wait_ge(o7_taken, i - 1)
                PE.matmul(OB[1][:, 0:8], same, dn[:, :, :].rearrange("p j u -> p (j u)"), start=True,
                          stop=True).then_inc(bs_done, 1)

            def joint_max(i):
                pe.wait_ge(dm_ready, i)
                PE.matmul(OB[1][:, 8:12], same, dm[:, :], start=True, stop=True).then_inc(mx_done, 1)

            def p_turned(i, has_comb):
                pe.wait_ge(p_ready, i)
                PE.matmul(OB[1][:, 12:13], same, lsum[:, :], start=True, stop=True).then_inc(l_done, 1)
                if has_comb:
                    pe.wait_ge(comb_saved, i - 1)
                for j in range(4):
                    last = turn(OB[0][:, P * j:P * j + P], ss[:, j, :], P)
                last.then_inc(pt_in, 1)

            def values(i, j):
                pe.wait_ge(v_in, 256 * i + 64 * j - 192)
                if j == 0:
                    pe.wait_ge(pt_ready, i)
                    pe.wait_ge(l_saved, i)
                for x in range(2):
                    for g in range(4):
                        last = PE.matmul(OB[x][32 * g:32 * g + 32, :], pT[:, j, 32 * g:32 * g + 32],
                                         vpage[:, g, 512 * x:512 * x + 512], start=j == 0, stop=j == NQUADS - 1)
                last.then_inc(v_done, 1)

            def kv_step(i, has_v, has_comb, first=False):
                def transposes(j, h):
                    n = 32 * i + 8 * j + h
                    if first and j == 0 and h < 2:
                        for c in range(2):
                            pe.wait_ge(quad_taken[c], QT0)
                    else:
                        pe.wait_ge(kt_out, n - 1)
                    if h == 0:
                        pe.wait_ge(k_in[j % 2], 128 * i + 64 * (j // 2) + 64)
                    for g in range(4):
                        last = turn(KTP[h % 2][:, P * g:P * g + P], kpage[:, j % 2, g, DH * h:DH * h + DH], P)
                    last.then_inc(kt_in, 1)

                def logits(j, h):
                    n = 32 * i + 8 * j + h
                    pe.wait_ge(kt_out, n + 1)
                    if j == 0 and h == 0:
                        pe.wait_ge(qz_ready, i + 1)
                        if not first:
                            pe.wait_ge(dn_ready, i)
                    for g in range(4):
                        last = PE.matmul(S[32 * g:32 * g + 32, P * j:P * j + P], qz[:, 32 * h:32 * h + 32],
                                         kT[:, h % 2, P * g:P * g + P], start=h == 0, stop=h == H - 1)
                    last.then_inc(qk_done, 1)

                for j in range(NQUADS):
                    transposes(j, 0)
                    for h in range(1, H):
                        transposes(j, h)
                        logits(j, h - 1)
                        if j == 0 and has_v:
                            if h == 2:
                                block_sums(i, has_comb)
                            if h == 3 and has_comb:
                                combine(i - 1)
                            if h == 5:
                                joint_max(i)
                    if j == 0 and not first:
                        pe.wait_ge(z_ready, 3 * i)
                    for k in (2 * j, 2 * j + 1):
                        w_tile(tile_at(T_KVU + k, i, 8), CW, (2 * k, 2 * k + 1), WB, hh, hl, k == 0, k == 7)
                        if k % 2 == 0:
                            logits(j, H - 1)
                            if j == 0 and has_v:
                                p_turned(i, has_comb)
                    if has_v:
                        values(i, j)

            def combine(count):
                pe.wait_ge(o6_taken, count)
                pe.wait_ge(o7_taken, count)
                for h in range(H):
                    last = PE.matmul(OB[0][0:32, 0:DH], headsel[:, h, :], osb[:, DH * h:DH * h + DH],
                                     start=h == 0, stop=h == H - 1)
                last.then_inc(comb_done, 1)

            kv_step(0, False, False, first=True)
            kv_step(1, True, False)
            with pe.Fori(2, NB) as i:
                kv_step(i, True, True)

            def rows_turned(n):
                if n == 0:
                    pe.wait_ge(z_ready, 3 * NB)
                elif n == 3:
                    pe.wait_ge(kt_out, 32 * NB)
                elif n == 6:
                    pe.wait_ge(mix_ready, H)
                elif n == 8:
                    pe.wait_ge(pt2_ready, H)
                if n in (4, 5) or n >= 8:
                    pe.wait_ge((tok_act, tok_dve)[n % 2], (n - 4) // 2 + 1)
                chunk, a, b = tok_src(n)
                for m in range(4):
                    last = turn(bank[n % 4][0:b - a, P * m:P * m + P], z[:, chunk + m, a:b], P)
                last.then_inc(tok_in, 1)

            def mixer(r):
                g, e = 3 - r // 2, r % 2
                pe.wait_ge(d_ready, r // 2 + 1)
                if r >= 2:
                    pe.wait_ge(y_sc, r - 1)
                for c in range(2):
                    last = PE.matmul(bank[4 + r % 2][:, 0:T], wpool[:, g, c, P * e:P * e + P], sq[:, c, :],
                                     start=c == 0, stop=c == 1)
                last.then_inc(y_in, 1)

            block_sums(NB, True)
            rows_turned(0)
            rows_turned(1)
            combine(NB - 1)
            rows_turned(2)
            rows_turned(3)
            joint_max(NB)
            rows_turned(4)
            rows_turned(5)
            p_turned(NB, True)
            pe.wait_ge(hist_in, 16)
            pe.wait_ge(tok_act, 2)
            pe.wait_ge(tok_dve, 2)
            for n in range(2):
                for m in range(4):
                    last = turn(bank[2 + n][:, 120 * m:120 * m + 120], hist[:, 512 * n + P * m:512 * n + P * m + P],
                                NB * HIST)
            last.then_inc(hist_T, 1)
            for s in range(H + 2):
                if s < H:
                    if s >= 2:
                        pe.wait_ge(a_out, s - 1)
                    A_ = bank[4 + s % 2]
                    PE.matmul(A_[:, 0:P], z[:, ZQ + s, 0:P], z[:, ZK + s, 0:P], start=True, stop=True)
                    PE.matmul(A_[:, P:384], z[:, ZQ + s, P:TP], z[:, ZK + s, 0:TP], start=True,
                              stop=True).then_inc(a_in, 1)
                if 1 <= s <= H:
                    h = s - 1
                    pe.wait_ge(pn_ready, 2 * h + 2)
                    if h == 0:
                        pe.wait_ge(tok_act, 3)
                        pe.wait_ge(tok_dve, 3)
                    if h >= 2:
                        pe.wait_ge(pt2_ready, h - 1)
                    B_ = bank[h % 2]
                    turn(B_[:, 0:P], px[:, h % 2, 0:P], P)
                    turn(B_[:, P:TP], px[:, h % 2, P:TP], P)
                    turn(B_[:, TP:384], px[:, h % 2, TP:384], P).then_inc(pt2_in, 1)
                if s >= 2:
                    h = s - 2
                    o = bank[2 + h % 2]
                    pe.wait_ge(pt2_ready, h + 1)
                    if h == 0:
                        pe.wait_ge(ext_ready, 2)
                    if h >= 2:
                        pe.wait_ge(mix_ready, h - 1)
                    PE.matmul(o[:, 0:TP], vtok[:, 0, DH * h:DH * h + DH], ptp[:, h % 2, 0:TP], start=True, stop=False)
                    PE.matmul(o[:, P:TP], vtok[:, 1, DH * h:DH * h + DH], ptp[:, h % 2, TP:384], start=False,
                              stop=True).then_inc(po_in, 1)
                if s % 2 and s < 8:
                    values(NB, s // 2)
            pe.wait_ge(a_out, H)
            mixer(0)
            mixer(1)
            combine(NB)
            pe.wait_ge(qza_ready, 1)
            for b in range(NB):
                for h in range(H):
                    last = PE.matmul(bank[7][0:32, NQ * b:NQ * b + NQ], qza[:, b, 32 * h:32 * h + 32],
                                     z[:, ZK + h, TP + NQ * b:TP + NQ * b + NQ], start=h == 0, stop=h == H - 1)
            last.then_inc(so_in, 1)
            for n in range(6, 16):
                rows_turned(n)
            mixer(2)
            mixer(3)
            pe.wait_ge(own_ready, 1)
            turn(bank[6][0:32, 0:32], so[:, :, :].rearrange("p b k -> p (b k)"), 32).then_inc(pTo_in, 1)
            pe.wait_ge(pTb_ready, 1)
            for b in range(NB):
                last = turn(bank[6][:, 32 * b:32 * b + 32], o_all[:, b, :], 32)
            last.then_inc(t1_in, 1)
            for h in range(H):
                last = PE.matmul(bank[7][:, 32 * h:32 * h + 32], stok[0:TS, DH * h:DH * h + DH],
                                 pTb[:, h, :, :].rearrange("p b q -> p (b q)"), start=True, stop=True)
            last.then_inc(t2_in, 1)
            for r in range(4, 8):
                mixer(r)
            pe.wait_ge(tok_act, 8)
            pe.wait_ge(tok_dve, 8)
            pe.wait_ge(pool_mix, 8)
            pe.wait_ge(smix_ready, 1)
            with pe.Fori(0, 2) as i:
                for k in range(16):
                    c, j = k // 8, k % 8
                    if j == 0:
                        pe.wait_ge(quad_taken[c], QT0 + 4 * i)
                    w_tile(tile_at(T_OUT + k, i, 16), 512, (2 * j, 2 * j + 1), bank[4 * c:4 * c + 4], hh, hl,
                           j == 0, j == 7)
            def gate_up(t0, quad):
                for j in range(8):
                    w_tile(tile_at(*((t0[0] + j,) + t0[1:])), 512, (2 * j, 2 * j + 1), bank[4 * quad:4 * quad + 4],
                           hh, hl, j == 0, j == 7)

            pe.wait_ge(quad_taken[0], QT)
            for j in range(8):
                pe.wait_ge(h_ready, KC + 2 * j + 2)
                w_tile(tile_at(T_FF + j), 512, (2 * j, 2 * j + 1), bank[0:4], hh, hl, j == 0, j == 7)
                if j == 6:
                    sum_sq(1)
            pe.wait_ge(ms_ready, 2)

            def down(t0, g, quads, taken):
                for c in range(4):
                    quad = quads[c]
                    if taken[c]:
                        pe.wait_ge(*taken[c])
                    if c == 0:
                        pe.wait_ge(af_ready, 4 * g + 4)
                    for j in range(2):
                        if c == 0:
                            pe.wait_ge(act_ready, 4 * g + 2 * j + 2)
                        w_tile(tile_at(*((t0[0] + 2 * c + j,) + t0[1:])), 512, (2 * j, 2 * j + 1),
                               bank[4 * quad:4 * quad + 4], ah, al, j == 0, j == 1)

            with pe.Fori(0, NG - 1) as g:
                pe.wait_ge(quad_taken[1], QT + 8 * g)
                gate_up((T_FF + 8, g, 24), 1)
                pe.wait_ge(gs_ready, 4 * g + 4)
                pe.wait_ge(quad_taken[0], QT + 8 * g)
                gate_up((T_FF + 16, g, 24), 0)
                down((T_FF + 24, g, 24), g, (1, 0, 1, 0),
                     (None, (gs_ready, 4 * g + 8), (quad_taken[1], QT + 4 + 8 * g), (quad_taken[0], QT + 4 + 8 * g)))
            pe.wait_ge(quad_taken[1], QT + 8 * (NG - 1))
            gate_up((T_END - 16,), 1)
            pe.wait_ge(quad_taken[0], QT + 8 * (NG - 1))
            pe.wait_ge(gs_ready, 4 * NG)
            down((T_END - 8,), NG - 1, (0, 1, 0, 1),
                 (None, (act_ready, 4 * NG), (x_ready, KC + 4), (x_ready, KC + 8)))
            pe.wait_ge(x_ready, KC + 12)
            for n in range(12):
                part, c, rows = final_step(n)
                if n == 3:
                    pe.wait_ge(sq_added, 3 * KC)
                    pe.wait_ge(x_ready, 2 * KC)
                    for m in range(3):
                        width = P if m < 2 else TS
                        last = PE.matmul(bank[4 + m][0:width, 0:1], ssq[:, P * m:P * m + width], ones[:, 0:1],
                                         start=True, stop=True)
                    last.then_inc(sq_summed, 1)
                if n == 4:
                    pe.wait_ge(fms, 3)
                if n >= 8:
                    pe.wait_ge((fy_act, fy_dve)[n % 2], (n - 8) // 2 + 1)
                pe.wait_ge(xf_ready, 4 * c + 4)
                for m in range(4):
                    last = turn(bank[n % 8][0:rows, P * m:P * m + P], xT[:, 4 * c + m, P * part:P * part + rows], P)
                last.then_inc(fy_in, 1)


STORES = 6 + 1 + 1 + NB

_INS = ["x_prompt", "x_sample", "cache_k", "cache_v", "state_pool", "page_table", "norm1_g", "w_in", "w_pool",
        "pool_scale", "w_out", "norm2_g", "w_gate", "w_up", "w_down", "norm_f_g"]
_OUTS = [("y_prompt", (1, TP, D)), ("y_sample", (NB, NQ, D)), ("k_prompt", (1, 1, TP, H, DH)),
         ("v_prompt", (1, 1, TP, H, DH)), ("pool_prompt", (1, 1, HIST, AW)), ("k_sample", (1, NB, NQ, H, DH)),
         ("v_sample", (1, NB, NQ, H, DH)), ("pool_sample", (1, NB, HIST, AW))]


def kernel(**inputs):
    import concourse.bacc as bacc
    from concourse.bass_utils import run_bass_kernel_spmd

    nc = bacc.Bacc("TRN2", target_bir_lowering=False, num_devices=1, dynamic_dma_scratch_size=64)
    table, at = tables()
    arrays = {name: np.ascontiguousarray(inputs[name]) for name in _INS}
    arrays["tables"] = table
    ins = {name: nc.dram_tensor(f"in_{name}", a.shape, mybir.dt.from_np(a.dtype), kind="ExternalInput").ap()
           for name, a in arrays.items()}
    outs = {name: nc.dram_tensor(f"out_{name}", shape, F32, kind="ExternalOutput").ap() for name, shape in _OUTS}
    step_program(nc, ins, outs, at)
    r = run_bass_kernel_spmd(nc, [{f"in_{name}": a for name, a in arrays.items()}], core_ids=[0])
    return tuple(r.results[0][f"out_{name}"] for name, _ in _OUTS)
```

```python
from contextlib import ExitStack

import numpy as np

import concourse.bass as bass
from concourse import mybir

F32 = mybir.dt.float32
F32R = mybir.dt.float32r
I32 = mybir.dt.int32
ALU = mybir.AluOpType
ACT = mybir.ActivationFunctionType
AX = mybir.AxisListType

P = 128
D = 2048
KC = D // P
TP = 256
NB, NQ = 8, 4
TS = NB * NQ
T = TP + TS
H, DH = 8, 128
AW = H * DH
NPAGES = 16
NQUADS = NPAGES // 4
PAST = NPAGES * P
FF = 5632
NG = FF // 512
HIST = 15
WINDOWS = (2, 4, 8, 16)
EPS = 1e-6
SCALE = DH ** -0.5
NEG = -1e30
TOPK = 3
ZQ, ZK, ZV, ZU = 0, 8, 16, 24
T_Q = 0
T_KVU = T_Q + 16
T_OP = T_KVU + 8 * NB
T_OA = T_OP + KC
T_FF = T_OA + 16
T_END = T_FF + 24 * NG
CW = 384
SLOTS = 4
TE = 2 * 512
QT0 = 4
QT = QT0 + 8
DVE_STEPS = 15
ROWS_AT = ((6, 7, 8, 9), (10, 11, 12, 13), (14, 15)) + ((),) * 8


def tables():
    p = np.arange(P)
    g, h, q = p // 32, (p // 4) % H, p % NQ
    slope = 2.0 ** -(h + 1.0)
    j4, r, n8 = np.arange(4), np.arange(P), np.arange(8)
    key = (4 * j4[None, :, None] + g[:, None, None]) * P + r[None, None, :]
    t16 = np.arange(16)
    qi, ki = p[:, None], np.arange(TP)[None, :]
    parts = {
        "ident": np.eye(P),
        "ones": np.ones((P, P)),
        "same": (p[:, None] % 32 == p[None, :] % 32),
        "headsel": (h[:, None, None] == n8[None, :, None]) & (p[:, None, None] % 32 == np.arange(32)),
        "past_bias": slope[:, None, None] * (key - (PAST + q[:, None, None])),
        "half": (g[:, None] // 2 == np.arange(2)),
        "gsel": (g[:, None] == j4[None, :]),
        "before": n8[None, None, :] < (2 * j4[None, :, None] + g[:, None, None] // 2),
        "own_bias": np.where(np.arange(NQ) <= q[:, None], slope[:, None] * (np.arange(NQ) - q[:, None]), NEG),
        "batch_of": (p[:, None] // NQ == n8[None, :]),
        "rel": np.concatenate(
            [np.where(ki[:, :P] <= qi, ki[:, :P] - qi, -1e33), np.where(ki <= qi + P, ki - (qi + P), -1e33)], 1),
        "inv_count": np.broadcast_to(1.0 / np.minimum(t16 + 1, np.array(WINDOWS)[:, None]), (P, 4, 16)),
    }
    at, cols = {}, 0
    flat = []
    for name, a in parts.items():
        a = np.asarray(a, np.float64).reshape(P, -1)
        at[name] = (cols, cols + a.shape[1])
        cols += a.shape[1]
        flat.append(a)
    return np.concatenate(flat, 1).astype(np.float32), at


class Steps:

    def __init__(self, eng, sem):
        self.eng, self.sem, self.base, self.k = eng, sem, 0, 0

    def did(self, ins):
        ins.then_inc(self.sem, 1)
        self.k += 1

    def settle(self):
        self.eng.wait_ge(self.sem, self.base + self.k)

    def link(self, ins):
        self.did(ins)
        self.settle()


def tile_at(k, i=0, per=0):
    return k + per * i, k // SLOTS + (per // SLOTS) * i, k % SLOTS


def step_program(nc, A, O, at):
    ctx = ExitStack()
    with ctx:
        def sem(name):
            return ctx.enter_context(nc.semaphore(name))

        def sb(name, shape, dt=F32, stack=None):
            return (stack or ctx).enter_context(nc.sbuf_tensor(name, shape, dt))

        tab = sb("tab", [P, A["tables"].shape[1]])
        xT = sb("xT", [P, KC, T])
        hh = sb("hh", [P, KC, T], F32R)
        hl = sb("hl", [P, KC, T], F32R)
        w_raw = sb("w_raw", [P, SLOTS, TE])
        w_hi = sb("w_hi", [P, SLOTS, TE], F32R)
        w_lo = sb("w_lo", [P, SLOTS, TE], F32R)
        gains = sb("gains", [P, 56])
        rstd = sb("rstd", [P, T])
        ms = sb("ms", [P, T])
        ssq = sb("ssq", [P, T])
        sq = sb("sq", [P, 2, T])
        nrm = sb("nrm", [P, 2, T])
        mid = ExitStack()
        z = sb("z", [P, 32, T], stack=mid)
        o_all = sb("o_all", [32, NB, DH], stack=mid)
        m_all = sb("m_all", [32, NB], stack=mid)
        l_all = sb("l_all", [32, NB], stack=mid)
        ext = sb("ext", [P, 8, NB, HIST + NQ], stack=mid)
        u_sample = ssq[:, 0:8 * TS].rearrange("p (c t) -> p c t", c=8)
        gt = ms[:, 0:32].rearrange("p (j m) -> p j m", j=4)
        eq = ms[:, 32:64].rearrange("p (j m) -> p j m", j=4)
        u_last = ms[:, 64:64 + 8 * HIST].rearrange("p (c t) -> p c t", c=8)
        t1 = nrm[:, 0, 0:256]
        mixs = nrm[:, 1, 0:256].rearrange("p (h t) -> p h t", h=H)
        kv = ExitStack()
        kpage = sb("kpage", [P, 2, 4, AW], stack=kv)
        kT = sb("kT", [P, 2, 512], stack=kv)
        qz = sb("qz", [P, H * 36], stack=kv)
        pages = sb("pages", [1, NB * NPAGES], I32, stack=kv)
        vpage = sb("vpage", [P, 4, AW], stack=kv)
        ss = sb("ss", [P, 4, P], stack=kv)
        pT = sb("pT", [P, 4, P], stack=kv)
        osb = sb("osb", [P, AW], stack=kv)
        d4 = sb("d4", [P, 4], stack=kv)
        dn = sb("dn", [P, 4, 2], stack=kv)
        bsc = sb("bsc", [P, 8], stack=kv)
        bsh = sb("bsh", [P, 4, 2], stack=kv)
        bown = sb("bown", [P, 4], stack=kv)
        cnt = sb("cnt", [P, 4], stack=kv)
        mx = sb("mx", [P, 1], stack=kv)
        dm = sb("dm", [P, 4], stack=kv)
        negm = sb("negm", [P, 1], stack=kv)
        lsum = sb("lsum", [P, 1], stack=kv)
        kv.close()
        pre = ExitStack()
        xs = sb("xs", [P, 3, D], stack=pre)
        vec = sb("vec", [56, P], stack=pre)
        hist = sb("hist", [NB * HIST, AW], stack=pre)
        pre.close()
        post = ExitStack()
        vtok = sb("vtok", [P, 2, AW], stack=post)
        stok = sb("stok", [P, AW], stack=post)
        ktok = sb("ktok", [P, 2, AW], stack=post)
        px = sb("px", [P, 2, 384], stack=post)
        ptp = sb("ptp", [P, 2, 384], stack=post)
        pm = sb("pm", [P, 2, 2], stack=post)
        pl = sb("pl", [P, 2, 2], stack=post)
        so = sb("so", [32, NB, NQ], stack=post)
        mo = sb("mo", [32, NB], stack=post)
        mm_ = sb("mm_", [32, NB], stack=post)
        eo = sb("eo", [32, NB], stack=post)
        lo_ = sb("lo_", [32, NB], stack=post)
        pTo = sb("pTo", [32, 32], stack=post)
        pTb = sb("pTb", [32, H, NB, NQ], stack=post)
        mix_w = ExitStack()
        wpool = sb("wpool", [P, 4, 2, 256], stack=mix_w)
        mix_w.close()
        qza = sb("qza", [P, NB, H * 36], stack=post)
        post.close()
        mid.close()
        late = ExitStack()
        sg = sb("sg", [P, 4, T], stack=late)
        af = sb("af", [P, 2, T], stack=late)
        ah = sb("ah", [P, 4, T], F32R, stack=late)
        al = sb("al", [P, 4, T], F32R, stack=late)
        yt = sb("yt", [P, 3, D], stack=late)
        rf = sb("rf", [P, 3], stack=late)
        fm = sb("fm", [P, 3], stack=late)
        ft = sb("ft", [P, 3], stack=late)
        late.close()

        bank = [ctx.enter_context(nc.psum_tensor(f"bank{n}", [P, 512], F32)) for n in range(8)]
        WB = bank[0:3]
        KTP = bank[3:5]
        S = bank[5]
        OB = bank[6:8]

        def tb(name):
            a, b = at[name]
            return tab[:, a:b]

        ident, ones, same = tb("ident"), tb("ones"), tb("same")
        headsel = tb("headsel").rearrange("p (h c) -> p h c", h=H)
        past_bias = tb("past_bias")
        half = tb("half")
        before = tb("before").rearrange("p (j m) -> p j m", j=4)
        inv_count = tb("inv_count").rearrange("p (g t) -> p g t", g=4)

        tab_in, x_in, vec_in, pages_in = sem("tab_in"), sem("x_in"), sem("vec_in"), sem("pages_in")
        w_in_s = [sem(f"w_slot{n}_in") for n in range(SLOTS)]
        hi_ready, lo_ready, w_used = sem("hi_ready"), sem("lo_ready"), sem("w_used")
        k_in = [sem("k_in0"), sem("k_in1")]
        v_in = sem("v_in")
        vecT, gains_ready = sem("vec_transposed"), sem("gains_ready")
        xT_in, x_ready = sem("x_transposed"), sem("x_ready")
        sq_ready, sq_added, sq_summed = sem("sq_ready"), sem("sq_added"), sem("sq_summed")
        ms_ready, root_ready, rf_ready = sem("ms_ready"), sem("root_ready"), sem("rf_ready")
        nrm_ready, nrm_hi, h_ready = sem("nrm_ready"), sem("nrm_hi"), sem("h_ready")
        z_ready = sem("z_ready")
        qz_ready = sem("qz_ready")
        kt_in, kt_out, qk_done = sem("kt_in"), sem("kt_out"), sem("qk_done")
        dn_ready, bs_done = sem("dn_ready"), sem("bs_done")
        dm_ready, mx_done, m_ready = sem("dm_ready"), sem("mx_done"), sem("m_ready")
        p_ready, l_done, l_saved = sem("p_ready"), sem("l_done"), sem("l_saved")
        pt_in, pt_ready, v_done = sem("pt_in"), sem("pt_ready"), sem("v_done")
        o6_taken, o7_taken = sem("o6_taken"), sem("o7_taken")
        comb_done, comb_saved = sem("comb_done"), sem("comb_saved")
        tok_in, tok_act, tok_dve = sem("tok_in"), sem("tok_act"), sem("tok_dve")
        hist_in, wpool_in = sem("hist_in"), sem("wpool_in")
        hist_T, ext_ready = sem("hist_transposed"), sem("ext_ready")
        a_in, a_out, a_bias = sem("a_in"), sem("a_out"), sem("a_bias")
        pm_ready, pe_ready, pn_ready = sem("pm_ready"), sem("pexp_ready"), sem("pn_ready")
        pt2_in, pt2_ready, po_in = sem("ptp_in"), sem("ptp_ready"), sem("po_in")
        po_hi, mix_ready = sem("po_hi"), sem("mix_ready")
        d_ready, y_in, y_sc, y_hi, pool_mix = sem("d_ready"), sem("y_in"), sem("y_scaled"), sem("y_hi"), sem("pool_mix")
        qza_ready, so_in, so_sub, so_exp = sem("qza_ready"), sem("so_in"), sem("so_sub"), sem("so_exp")
        own_ready, pTo_in, pTb_ready, t1_in, t2_in, t1_saved = (
            sem("own_ready"), sem("pTo_in"), sem("pTb_ready"), sem("t1_in"), sem("t2_in"), sem("t1_saved"))
        smix, smix_hi, smix_ready = sem("smix"), sem("smix_hi"), sem("smix_ready")
        wo_taken, own_scaled = sem("wo_taken"), sem("own_scaled")
        quad_taken = [sem("quadA_taken"), sem("quadB_taken")]
        gs_ready, sg_ready, sr_ready, af_ready, ah_ready, act_ready = (
            sem("gs_ready"), sem("sg_ready"), sem("sr_ready"), sem("af_ready"), sem("ah_ready"), sem("act_ready"))
        fms, froot = sem("fms"), sem("froot")
        xf_ready, fy_in, fy_act, fy_dve = sem("xf_ready"), sem("fy_in"), sem("fy_act"), sem("fy_dve")
        dve_own, pool_own = sem("dve_own"), sem("pool_own")
        stored = sem("stored")

        ck = A["cache_k"][0].rearrange("n t h d -> n t (h d)")
        cv = A["cache_v"][0].rearrange("n t h d -> n t (h d)")
        w_in_d, w_out_d = A["w_in"][0], A["w_out"][0]
        wg_d, wu_d, wd_d = A["w_gate"][0], A["w_up"][0], A["w_down"][0]

        def final_step(n):
            part = n // 4
            return part, n % 4, P if part < 2 else TS

        def pool_chunk(r):
            return 8 + 2 * (3 - r // 2) + r % 2

        def tok_dst(n):
            half_ = n % 2
            kind, part = (n // 2) // 3, (n // 2) % 3
            cols = slice(512 * half_, 512 * half_ + 512)
            if kind < 2 and part < 2:
                return P, (vtok, ktok)[kind][:, part, cols]
            rows, at_ = ((TS, 32 * kind), (TS, 64), (HIST, 96))[0 if kind < 2 else 1 + part]
            return rows, stok[at_:at_ + rows, cols]

        def tok_src(n):
            half_ = n % 2
            kind, part = (n // 2) // 3, (n // 2) % 3
            if kind < 2:
                a = P * part
                return z, (ZV, ZK)[kind] + 4 * half_, a, a + (P if part < 2 else TS)
            return (u_sample, 4 * half_, 0, TS) if part == 0 else (u_last, 4 * half_, 0, HIST)

        def row_bank(n):
            return bank[n % 4 if n < 6 else n % 2]

        block = ctx.enter_context(nc.Block())

        @block.sync
        def _(sp):
            xp, xsam = A["x_prompt"][0], A["x_sample"].rearrange("b q d -> (b q) d")
            sp.dma_start(tab[:, :], A["tables"]).then_inc(tab_in, 16)
            for n in range(2):
                sp.dma_start(xs[:, n, :], xp[n * P:(n + 1) * P, :]).then_inc(x_in, 16)
            sp.dma_start(xs[0:TS, 2, :], xsam).then_inc(x_in, 16)
            for n, name in enumerate(("norm1_g", "norm2_g", "norm_f_g", "pool_scale")):
                g = A[name] if name == "norm_f_g" else A[name][0]
                sp.dma_start(vec[16 * n:min(16 * n + 16, 56), :], g.rearrange("(c p) -> c p", p=P)).then_inc(vec_in, 16)

            def load(t, src, free=True):
                n, _, s = t
                if free:
                    sp.wait_ge(lo_ready, n - 3)
                k, w = src.shape[0] // P, src.shape[1]
                sp.dma_start(w_raw[:, s, 0:k * w].rearrange("p (k n) -> p k n", k=k),
                             src.rearrange("(k p) n -> p k n", p=P)).then_inc(w_in_s[s], 16)

            for k in range(16):
                c, j = k // 8, k % 8
                if k == SLOTS:
                    sp.dma_start(hist[:, :], A["state_pool"][0].rearrange("b i c -> (b i) c")).then_inc(hist_in, 16)
                load(tile_at(T_Q + k), w_in_d[256 * j:256 * j + 256, 512 * c:512 * c + 512], free=k >= SLOTS)
            sp.wait_ge(xT_in, KC)
            sp.wait_ge(hist_T, 2)
            sp.dma_start(pages[:, :], A["page_table"].rearrange("b n -> (b n)").rearrange("(a n) -> a n", a=1)
                         ).then_inc(pages_in, 16)
            sp.wait_ge(pages_in, 16)

            def page(pool, b, n):
                e = NPAGES * b + n
                idx = sp.value_load(pages[0:1, bass.ds(e, 1)], min_val=0, max_val=pool.shape[0] - 1)
                return pool[bass.ds(idx, 1), :, :].rearrange("a t n -> (a t) n")

            def load_k(i, j, free=True):
                if free:
                    sp.wait_ge(kt_in, 32 * i + 8 * j - 8)
                for g in range(4):
                    sp.dma_start(kpage[:, j % 2, g, :], page(ck, i, 4 * j + g)).then_inc(k_in[j % 2], 16)

            def load_v(i, j, free=True):
                if free:
                    sp.wait_ge(v_done, 4 * i + j - 4)
                for g in range(4):
                    sp.dma_start(vpage[:, g, :], page(cv, i - 1, 4 * j + g)).then_inc(v_in, 16)

            def stream(i, has_v, next_k=True, first_v=False):
                for j in range(NQUADS):
                    for k in (2 * j, 2 * j + 1):
                        load(tile_at(T_KVU + k, i, 8), w_in_d[256 * k:256 * k + 256, bass.ds(i * (-CW) + (4 * AW - CW), CW)])
                    if j < NQUADS - 1:
                        load_k(i, j + 1, not (j == 0 and not has_v))
                    elif next_k:
                        load_k(i + 1, 0)
                    if has_v:
                        load_v(i, j, not (first_v and j == 0))

            load_k(0, 0, False)
            stream(0, False)
            stream(1, True, first_v=True)
            with sp.Fori(2, NB - 1) as i:
                stream(i, True)
            stream(NB - 1, True, next_k=False)
            sp.wait_ge(qk_done, 32 * NB)
            sp.dma_start(wpool[:, :, :, :], A["w_pool"][0].rearrange("g (k p) e -> p g k e", p=P)).then_inc(wpool_in, 16)

            def load_out_pool(ks_):
                for k in ks_:
                    load(tile_at(T_OP + k), w_out_d[AW:2 * AW, P * k:P * k + P])

            load_v(NB, 0)
            load_out_pool(range(4))
            load_v(NB, 1)
            load_out_pool(range(4, 8))
            load_v(NB, 2)
            load_out_pool(range(8, 10))
            load_v(NB, 3)
            load_out_pool(range(10, 12))
            n_stores = 0

            def store(dst, src):
                nonlocal n_stores
                sp.dma_start(dst, src).then_inc(stored, 16)
                n_stores += 1

            kp, vp = O["k_prompt"][0, 0].rearrange("t h d -> t (h d)"), O["v_prompt"][0, 0].rearrange("t h d -> t (h d)")
            ks = O["k_sample"][0].rearrange("b q h d -> (b q) (h d)")
            vs = O["v_sample"][0].rearrange("b q h d -> (b q) (h d)")
            sp.wait_ge(tok_act, 8)
            sp.wait_ge(tok_dve, 8)
            for n in range(2):
                store(kp[n * P:(n + 1) * P, :], ktok[:, n, :])
                store(vp[n * P:(n + 1) * P, :], vtok[:, n, :])
            store(vs, stok[0:TS, :])
            store(ks, stok[TS:2 * TS, :])
            store(O["pool_prompt"][0, 0], stok[96:96 + HIST, :])
            store(O["pool_sample"][0, :, 0:HIST - NQ, :], A["state_pool"][0, :, NQ:HIST, :])
            for b in range(NB):
                store(O["pool_sample"][0, b, HIST - NQ:HIST, :], stok[64 + NQ * b:64 + NQ * b + NQ, :])
            load_out_pool(range(12, 16))
            with sp.Fori(0, 2) as i:
                for k in range(8):
                    c, j = k // 4, k % 4
                    load(tile_at(T_OA + k, i, 8), w_out_d[256 * j:256 * j + 256, bass.ds(1024 * i + 512 * c, 512)])

            def load_gu(w, t0, g):
                for k in range(8):
                    load(tile_at(*((t0[0] + k,) + t0[1:])), w[256 * k:256 * k + 256, bass.ds(512 * g, 512)])

            def load_down(t0, g):
                for k in range(8):
                    c, j = k // 2, k % 2
                    load(tile_at(*((t0[0] + k,) + t0[1:])),
                         wd_d[bass.ds(512 * g + 256 * j, 256), 512 * c:512 * c + 512])

            load_gu(wg_d, (T_FF,), 0)
            with sp.Fori(0, NG - 1) as g:
                load_gu(wu_d, (T_FF + 8, g, 24), g)
                load_gu(wg_d, (T_FF + 16, g, 24), g + 1)
                load_down((T_FF + 24, g, 24), g)
            load_gu(wu_d, (T_END - 16,), NG - 1)
            load_down((T_END - 8,), NG - 1)
            for n in range(3):
                rows = P if n < 2 else TS
                sp.wait_ge(fy_act, 2 * n + 2)
                sp.wait_ge(fy_dve, 2 * n + 2)
                dst = O["y_prompt"][0, n * P:(n + 1) * P, :] if n < 2 else O["y_sample"].rearrange("b q d -> (b q) d")
                store(dst, yt[0:rows, n, :])
            sp.wait_ge(stored, 16 * n_stores)

        @block.scalar
        def _(act):
            def copy(out, in_):
                return nc.scalar.activation(out, in_, ACT.Copy)

            def hi(t, free=True):
                n, turn, s = t
                act.wait_ge(w_in_s[s], 16 * turn + 16)
                if free:
                    act.wait_ge(w_used, n - 3)
                copy(w_hi[:, s, :], w_raw[:, s, :]).then_inc(hi_ready, 1)

            def square(stage, c):
                n = KC * stage + c
                if n >= 2:
                    act.wait_ge(sq_added, n - 1)
                nc.scalar.activation(sq[:, c % 2, :], xT[:, c, :], ACT.Square).then_inc(sq_ready, 1)

            def gained(stage, c):
                act.wait_ge(nrm_ready, KC * stage + c + 1)
                copy(hh[:, c, :], nrm[:, c % 2, :]).then_inc(nrm_hi, 1)

            def root(stage):
                act.wait_ge(ms_ready, stage + 1)
                nc.scalar.activation(rstd[:, :], ms[:, :], ACT.Sqrt).then_inc(root_ready, 1)

            for c in range(KC):
                act.wait_ge(x_ready, c + 1)
                gained(0, c)
                square(0, c)
                if c % 2:
                    hi(tile_at(c // 2), c // 2 >= SLOTS)
            for k in range(4, 6):
                hi(tile_at(4 + k))
            root(0)
            for k in range(6, 12):
                hi(tile_at(4 + k))

            def kv_step(i, has_v, has_comb, first=False):
                for j in range(NQUADS):
                    for h in range(H):
                        n = 32 * i + 8 * j + h
                        act.wait_ge(kt_in, n + 1)
                        if not (first and j == 0 and h < 2):
                            act.wait_ge(qk_done, n - 1)
                        copy(kT[:, h % 2, :], KTP[h % 2][:, :]).then_inc(kt_out, 1)
                        if j == 0 and h == 4 and has_comb:
                            save_comb(i - 2, i - 1)
                    if j == 0 and has_v:
                        softmax_late(i)
                if has_v:
                    act.wait_ge(v_done, 4 * i)
                    if has_comb:
                        act.wait_ge(comb_done, i - 1)
                    copy(osb[:, 0:512], OB[0][:, :]).then_inc(o6_taken, 1)

            def save_comb(b, count):
                act.wait_ge(comb_done, count)
                copy(o_all[:, bass.ds(b, 1), :].rearrange("p a d -> p (a d)"), OB[0][0:32, 0:DH]).then_inc(comb_saved, 1)

            def softmax_late(i):
                act.wait_ge(m_ready, i)
                nc.scalar.activation(ss[:, :, :], ss[:, :, :], ACT.Exp, bias=negm[:, 0:1],
                                     accum_out=lsum[:, 0:1]).then_inc(p_ready, 1)
                act.wait_ge(pt_in, i)
                copy(pT[:, :, :], OB[0][:, :].rearrange("p (j k) -> p j k", j=4)).then_inc(pt_ready, 1)

            kv_step(0, False, False, first=True)
            kv_step(1, True, False)
            with act.Fori(2, NB) as i:
                kv_step(i, True, True)

            def rows_out(n):
                act.wait_ge(tok_in, n + 1)
                rows, dst = tok_dst(n)
                copy(dst, row_bank(n)[0:rows, :]).then_inc(tok_act, 1)

            rows_out(0)
            save_comb(NB - 2, NB - 1)
            rows_out(2)
            rows_out(4)
            softmax_late(NB)
            act.wait_ge(d_ready, 8)
            for r in range(8):
                act.wait_ge(y_in, r + 1)
                if r >= 2:
                    act.wait_ge(pool_mix, r - 1)
                c = pool_chunk(r)
                nc.scalar.activation(nrm[:, r % 2, :], bank[4 + r % 2][:, 0:T], ACT.Copy,
                                     scale=gains[:, 40 + c:41 + c]).then_inc(y_sc, 1)
                act.wait_ge(y_sc, r + 1)
                copy(hh[:, c, :], nrm[:, r % 2, :]).then_inc(y_hi, 1)

            def head_hi(h):
                act.wait_ge(po_in, h + 1)
                copy(hh[:, h, 0:TP], bank[3][:, 0:TP]).then_inc(po_hi, 1)

            for s in range(H + 2):
                if s >= 2:
                    h = s - 2
                    act.wait_ge(pt2_in, h + 1)
                    if h >= 2:
                        act.wait_ge(po_in, h - 1)
                    copy(ptp[:, h % 2, :], bank[2][:, 0:384]).then_inc(pt2_ready, 1)
                if s < H:
                    act.wait_ge(a_in, s + 1)
                    if s >= 2:
                        act.wait_ge(pt2_in, s - 1)
                    nc.scalar.activation(px[:, s % 2, :], bank[4][:, 0:384], ACT.Copy, scale=SCALE).then_inc(a_out, 1)
                if s >= 3:
                    head_hi(s - 3)
                if 1 <= s <= H:
                    u = (s - 1) % 2
                    act.wait_ge(pm_ready, 2 * s)
                    for n, (a, b) in enumerate(((0, P), (P, 384))):
                        nc.scalar.activation(px[:, u, a:b], px[:, u, a:b], ACT.Exp, bias=pm[:, u, n:n + 1],
                                             accum_out=pl[:, u, n:n + 1]).then_inc(pe_ready, 1)
                for n in ROWS_AT[s]:
                    if n % 2 == 0:
                        rows_out(n)
                if s == 2:
                    act.wait_ge(so_sub, 2)
                    nc.scalar.activation(so[:, :, :], so[:, :, :], ACT.Exp).then_inc(so_exp, 1)
                    nc.scalar.activation(eo[:, :], eo[:, :], ACT.Exp).then_inc(so_exp, 1)
                if s == H:
                    act.wait_ge(v_done, 4 * NB)
                    act.wait_ge(comb_done, NB - 1)
                    copy(osb[:, 0:512], OB[0][:, :]).then_inc(o6_taken, 1)
                if s >= 2:
                    for k in (2 * s - 4, 2 * s - 3):
                        hi(tile_at(T_OP + k))
                if s == H:
                    save_comb(NB - 1, NB)
            head_hi(H - 1)
            for k in range(2):
                hi(tile_at(T_OA + k))
            act.wait_ge(smix, 1)
            copy(hh[:, 0:H, TP:T], mixs).then_inc(smix_hi, 1)
            for k in range(2, SLOTS):
                hi(tile_at(T_OA + k))
            with act.Fori(0, 2) as i:
                for k in range(8):
                    hi(tile_at(T_OA + 4 + k, i, 8))
            for c in range(KC):
                gained(1, c)
                act.wait_ge(quad_taken[c // 4 % 2], QT0 + 4 * (c // 8) + c % 4 + 1)
                square(1, c)
                if c % 2 and c >= 5:
                    hi(tile_at(T_FF + 4 + (c - 5) // 2))
            hi(tile_at(T_FF + 10))
            root(1)
            hi(tile_at(T_FF + 11))

            def silu(g):
                for m in range(4):
                    act.wait_ge(gs_ready, 4 * g + m + 1)
                    nc.scalar.activation(sg[:, m, :], sg[:, m, :], ACT.Silu).then_inc(sg_ready, 1)

            def act_hi(g):
                for m in range(4):
                    act.wait_ge(af_ready, 4 * g + m + 1)
                    copy(ah[:, m, :], af[:, m % 2, :]).then_inc(ah_ready, 1)

            silu(0)
            with act.Fori(0, NG - 1) as g:
                for k in range(24):
                    hi(tile_at(T_FF + 12 + k, g, 24))
                    if k == 7:
                        act_hi(g)
                    if k == 15:
                        silu(g + 1)
            for k in range(12):
                hi(tile_at(T_END - 12 + k))
                if k == 7:
                    act_hi(NG - 1)
            for c in range(KC):
                act.wait_ge(x_ready, KC + c + 1)
                square(2, c)
            act.wait_ge(fms, 3)
            nc.scalar.activation(rf[:, :], fm[:, :], ACT.Sqrt).then_inc(froot, 1)
            act.wait_ge(rf_ready, 1)
            for n in range(0, 12, 2):
                part, c, rows = final_step(n)
                act.wait_ge(fy_in, n + 1)
                nc.scalar.activation(yt[0:rows, part, 512 * c:512 * c + 512], bank[n % 8][0:rows, :], ACT.Copy,
                                     scale=rf[0:rows, part:part + 1]).then_inc(fy_act, 1)

        @block.vector
        def _(dve):
            own = Steps(dve, dve_own)
            V = nc.vector

            def lo(t, width=TE):
                n, _, s = t
                dve.wait_ge(hi_ready, n + 1)
                V.tensor_tensor(w_lo[:, s, 0:width], w_raw[:, s, 0:width], w_hi[:, s, 0:width].bitcast(F32),
                                ALU.subtract).then_inc(lo_ready, 1)

            def hi_lo(t):
                n, turn, s = t
                dve.wait_ge(w_in_s[s], 16 * turn + 16)
                dve.wait_ge(w_used, n - 3)
                V.tensor_copy(w_hi[:, s, 0:2 * CW], w_raw[:, s, 0:2 * CW]).then_inc(hi_ready, 1)
                lo(t, 2 * CW)

            def gained(stage, c):
                if KC * stage + c >= 2:
                    dve.wait_ge(h_ready, KC * stage + c - 1)
                V.tensor_scalar(nrm[:, c % 2, :], xT[:, c, :], gains[:, 16 * stage + c:16 * stage + c + 1], None,
                                ALU.mult).then_inc(nrm_ready, 1)

            def gained_lo(stage, c):
                dve.wait_ge(nrm_hi, KC * stage + c + 1)
                V.tensor_tensor(hl[:, c, :], nrm[:, c % 2, :], hh[:, c, :].bitcast(F32),
                                ALU.subtract).then_inc(h_ready, 1)

            def mean_sq(stage):
                dve.wait_ge(sq_summed, stage + 1)
                V.tensor_scalar(ms[:, :], bank[7][:, 0:T], 1.0 / D, EPS, ALU.mult, ALU.add).then_inc(ms_ready, 1)

            def inverse_root(r, mean, tmp):
                own.link(V.reciprocal(r, r))
                own.link(V.tensor_tensor(tmp, r, r, ALU.mult))
                own.link(V.tensor_tensor(tmp, tmp, mean, ALU.mult))
                own.link(V.tensor_scalar(tmp, tmp, -0.5, 1.5, ALU.mult, ALU.add))
                return V.tensor_tensor(r, r, tmp, ALU.mult)

            def rstd_of(stage):
                dve.wait_ge(root_ready, stage + 1)
                dve.wait_ge(h_ready, KC * stage + KC)
                own.link(inverse_root(rstd[:, :], ms[:, :], nrm[:, 0, :]))

            dve.wait_ge(vecT, 1)
            V.tensor_copy(gains[:, :], bank[6][:, 0:56]).then_inc(gains_ready, 1)
            dve.wait_ge(gains_ready, 1)
            for c in range(KC + 1):
                if c < KC:
                    dve.wait_ge(xT_in, c + 1)
                    V.tensor_copy(xT[:, c, :], bank[4 + c % 2][:, 0:T]).then_inc(x_ready, 1)
                    dve.wait_ge(x_ready, c + 1)
                    gained(0, c)
                if c:
                    gained_lo(0, c - 1)
                    if c % 2 == 0:
                        lo(tile_at(c // 2 - 1))
                if c in (8, 14):
                    n = c // 14
                    dve.wait_ge(hist_T, n + 1)
                    V.tensor_copy(ext[:, 4 * n:4 * n + 4, :, 0:HIST],
                                  bank[6][:, 0:480].rearrange("p (c b i) -> p c b i", c=4, b=NB)).then_inc(ext_ready, 1)
            for k in range(4, 6):
                lo(tile_at(4 + k))
            mean_sq(0)
            rstd_of(0)
            own.link(V.memset(qz[:, :], 0.0))
            for k in range(6, 16):
                if k < 12:
                    lo(tile_at(4 + k))
                if k % 8 == 7:
                    c = k // 8
                    dve.wait_ge(w_used, T_Q + 8 * c + 8)
                    for m in range(4):
                        V.tensor_tensor(z[:, 4 * c + m, :], bank[4 * c + m][:, 0:T], rstd[:, :],
                                        ALU.mult).then_inc(quad_taken[c], 1)
            for c in range(2):
                dve.wait_ge(quad_taken[c], QT0)

            def pad_q(b):
                cols = bass.ds(TP + NQ * b, NQ)
                return V.tensor_copy(qz[:, :].rearrange("p (h s) -> p h s", s=36)[:, :, 0:NQ], z[:, ZQ:ZQ + H, cols])

            def scaled_logits(i, has_comb):
                if has_comb:
                    dve.wait_ge(pt_in, i - 1)
                own.did(V.scalar_tensor_tensor(ss[:, :, :].rearrange("p j k -> p (j k)"), S[:, :], SCALE, past_bias,
                                               ALU.mult, ALU.add))
                own.did(V.tensor_reduce(d4[:, :], S[:, :].rearrange("p (j k) -> p j k", j=4), AX.X, ALU.add))
                own.settle()
                V.tensor_tensor(dn[:, :, :], d4[:, :].unsqueeze(2).to_broadcast([P, 4, 2]),
                                half.unsqueeze(1).to_broadcast([P, 4, 2]), ALU.mult).then_inc(dn_ready, 1)

            def select_blocks(i):
                dve.wait_ge(bs_done, i)
                own.link(V.tensor_copy(bsc[:, :], OB[1][:, 0:8]))
                own.link(V.tensor_tensor(bsh[:, :, :], bsc[:, :].rearrange("p (j u) -> p j u", u=2),
                                         half.unsqueeze(1).to_broadcast([P, 4, 2]), ALU.mult))
                own.link(V.tensor_reduce(bown[:, :], bsh[:, :, :], AX.X, ALU.add))
                every = bsc[:, :].unsqueeze(1).to_broadcast([P, 4, 8])
                mine = bown[:, :].unsqueeze(2).to_broadcast([P, 4, 8])
                own.did(V.tensor_tensor(gt, every, mine, ALU.is_gt))
                own.link(V.tensor_tensor(eq, every, mine, ALU.is_equal))
                own.link(V.tensor_tensor(eq, eq, before, ALU.mult))
                own.link(V.tensor_tensor(gt, gt, eq, ALU.add))
                own.link(V.tensor_reduce(cnt[:, :], gt, AX.X, ALU.add))
                own.link(V.tensor_scalar(cnt[:, :], cnt[:, :], float(TOPK), NEG, ALU.is_ge, ALU.mult))
                own.link(V.tensor_tensor(ss[:, :, :], ss[:, :, :], cnt[:, :].unsqueeze(2).to_broadcast([P, 4, P]),
                                         ALU.add))
                own.link(V.tensor_reduce(mx[:, :], ss[:, :, :].rearrange("p j k -> p (j k)"), AX.X, ALU.max))
                V.tensor_scalar(dm[:, :], tb("gsel"), mx[:, 0:1], None, ALU.mult).then_inc(dm_ready, 1)

            def joint_max(i):
                dve.wait_ge(mx_done, i)
                own.link(V.tensor_reduce(mx[:, :], OB[1][:, 8:12], AX.X, ALU.max))
                V.tensor_scalar(negm[:, :], mx[:, :], -1.0, None, ALU.mult).then_inc(m_ready, 1)
                own.did(V.tensor_copy(m_all[:, bass.ds(i - 1, 1)], mx[0:32, :]))

            def joint_sum(i):
                dve.wait_ge(l_done, i)
                V.tensor_copy(l_all[:, bass.ds(i - 1, 1)], OB[1][0:32, 12:13]).then_inc(l_saved, 1)

            def kv_step(i, has_v, has_comb):
                if has_v:
                    dve.wait_ge(qk_done, 32 * i)
                pad_q(i).then_inc(qz_ready, 1)
                if has_v:
                    scaled_logits(i, has_comb)
                    select_blocks(i)
                hi_lo(tile_at(T_KVU, i, 8))
                if has_v:
                    joint_max(i)
                hi_lo(tile_at(T_KVU + 1, i, 8))
                if has_v:
                    joint_sum(i)
                for k in range(2, 8):
                    hi_lo(tile_at(T_KVU + k, i, 8))
                dve.wait_ge(w_used, T_KVU + 8 + 8 * i)
                for m in range(3):
                    V.tensor_tensor(z[:, bass.ds(ZK + 3 * (NB - 1) - 3 * i + m, 1), :].rearrange("p a t -> p (a t)"),
                                    WB[m][:, 0:T], rstd[:, :], ALU.mult).then_inc(z_ready, 1)
                if has_v:
                    dve.wait_ge(v_done, 4 * i)
                    if has_comb:
                        dve.wait_ge(comb_done, i - 1)
                    V.tensor_copy(osb[:, 512:1024], OB[1][:, :]).then_inc(o7_taken, 1)

            kv_step(0, False, False)
            kv_step(1, True, False)
            done, own.k = own.k, 0
            with dve.Fori(2, NB) as i:
                own.base = done + DVE_STEPS * (i - 2)
                kv_step(i, True, True)
                assert own.k == DVE_STEPS
            own.base, own.k = done + DVE_STEPS * (NB - 2), 0

            def rows_out(n):
                dve.wait_ge(tok_in, n + 1)
                rows, dst = tok_dst(n)
                V.tensor_copy(dst, row_bank(n)[0:rows, :]).then_inc(tok_dve, 1)

            dve.wait_ge(qk_done, 32 * NB)
            scaled_logits(NB, True)
            rows_out(1)
            select_blocks(NB)
            rows_out(3)
            joint_max(NB)
            rows_out(5)
            joint_sum(NB)
            def head_lo(h):
                dve.wait_ge(po_hi, h + 1)
                V.tensor_tensor(hl[:, h, 0:TP], bank[3][:, 0:TP], hh[:, h, 0:TP].bitcast(F32),
                                ALU.subtract).then_inc(mix_ready, 1)

            def add_pool_half(k):
                dve.wait_ge(w_used, T_OP + k + 1)
                V.tensor_tensor(xT[:, k, :], xT[:, k, :], bank[k % 2][:, 0:T], ALU.add).then_inc(wo_taken, 1)

            def own_logits():
                dve.wait_ge(so_in, 1)
                own.link(V.scalar_tensor_tensor(so[:, :, :], bank[5][0:32, 0:32].rearrange("p (b k) -> p b k", b=NB),
                                                SCALE, tb("own_bias")[0:32, :].unsqueeze(1).to_broadcast([32, NB, NQ]),
                                                ALU.mult, ALU.add))
                own.link(V.tensor_reduce(mo[:, :], so[:, :, :], AX.X, ALU.max))
                own.link(V.tensor_tensor(mm_[:, :], mo[:, :], m_all[:, :], ALU.max))
                V.tensor_tensor(so[:, :, :], so[:, :, :], mm_[:, :].unsqueeze(2).to_broadcast([32, NB, NQ]),
                                ALU.subtract).then_inc(so_sub, 1)
                V.tensor_tensor(eo[:, :], m_all[:, :], mm_[:, :], ALU.subtract).then_inc(so_sub, 1)

            def own_probs():
                dve.wait_ge(so_exp, 2)
                dve.wait_ge(l_saved, NB)
                own.did(V.tensor_reduce(lo_[:, :], so[:, :, :], AX.X, ALU.add))
                own.did(V.tensor_tensor(mo[:, :], l_all[:, :], eo[:, :], ALU.mult))
                own.settle()
                own.link(V.tensor_tensor(lo_[:, :], lo_[:, :], mo[:, :], ALU.add))
                own.link(V.reciprocal(lo_[:, :], lo_[:, :]))
                own.link(V.tensor_tensor(eo[:, :], eo[:, :], lo_[:, :], ALU.mult))
                V.tensor_tensor(so[:, :, :], so[:, :, :], lo_[:, :].unsqueeze(2).to_broadcast([32, NB, NQ]),
                                ALU.mult).then_inc(own_ready, 1)

            def own_spread():
                dve.wait_ge(pTo_in, 1)
                own.link(V.tensor_copy(pTo[:, :], bank[5][0:32, 0:32]))
                V.tensor_tensor(pTb[:, :, :, :], pTo[:, :].rearrange("p (h q) -> p h q", h=H).unsqueeze(2).to_broadcast(
                    [32, H, NB, NQ]), tb("batch_of")[0:32, :].unsqueeze(1).unsqueeze(3).to_broadcast([32, H, NB, NQ]),
                    ALU.mult).then_inc(pTb_ready, 1)

            for s in range(H + 2):
                if s == H:
                    dve.wait_ge(v_done, 4 * NB)
                    dve.wait_ge(comb_done, NB - 1)
                    V.tensor_copy(osb[:, 512:1024], OB[1][:, :]).then_inc(o7_taken, 1)
                if s >= 4:
                    add_pool_half(2 * s - 8)
                if 1 <= s <= H:
                    u = (s - 1) % 2
                    dve.wait_ge(pe_ready, 2 * s)
                    own.link(V.reciprocal(pl[:, u, :], pl[:, u, :]))
                    for n, (a, b) in enumerate(((0, P), (P, 384))):
                        V.tensor_scalar(px[:, u, a:b], px[:, u, a:b], pl[:, u, n:n + 1], None,
                                        ALU.mult).then_inc(pn_ready, 1)
                if s < H:
                    dve.wait_ge(a_out, s + 1)
                    own.link(V.scalar_tensor_tensor(px[:, s % 2, :], tb("rel"), 2.0 ** -(s + 1), px[:, s % 2, :],
                                                    ALU.mult, ALU.add))
                    for n, (a, b) in enumerate(((0, P), (P, 384))):
                        V.tensor_reduce(pm[:, s % 2, n:n + 1], px[:, s % 2, a:b], AX.X, ALU.max,
                                        negate=True).then_inc(pm_ready, 1)
                if s >= 4:
                    add_pool_half(2 * s - 7)
                if s >= 3:
                    head_lo(s - 3)
                for n in ROWS_AT[s]:
                    if n % 2:
                        rows_out(n)
                if s == 0:
                    dve.wait_ge(y_in, 8)
                    own.link(V.memset(qza[:, :, :], 0.0))
                    V.tensor_copy(qza[:, :, :].rearrange("p b (h s) -> p b h s", s=36)[:, :, :, 0:NQ],
                                  z[:, ZQ:ZQ + H, TP:T].rearrange("p h (b q) -> p b h q", b=NB)).then_inc(qza_ready, 1)
                if s == 2:
                    own_logits()
                if s == 3:
                    own_probs()
                if s == 4:
                    own_spread()
                if s == 6:
                    dve.wait_ge(t2_in, 1)
                    dve.wait_ge(pool_mix, 8)
                    V.tensor_copy(t1, bank[5][:, 0:256]).then_inc(t1_saved, 1)
                if s >= 2:
                    for k in (2 * s - 4, 2 * s - 3):
                        lo(tile_at(T_OP + k))
                if s == H + 1:
                    dve.wait_ge(comb_saved, NB)
                    V.tensor_tensor(o_all[:, :, :], o_all[:, :, :], eo[:, :].unsqueeze(2).to_broadcast([32, NB, DH]),
                                    ALU.mult).then_inc(own_scaled, 1)
            add_pool_half(12)
            add_pool_half(13)
            head_lo(H - 1)
            for k in range(2):
                lo(tile_at(T_OA + k))
            dve.wait_ge(t1_in, 1)
            dve.wait_ge(t1_saved, 1)
            V.tensor_tensor(mixs.rearrange("p h (b q) -> p h b q", b=NB),
                            bank[7][:, 0:256].rearrange("p (b h q) -> p h b q", h=H, b=NB),
                            t1.rearrange("p (h b q) -> p h b q", h=H, b=NB), ALU.add).then_inc(smix, 1)
            add_pool_half(14)
            dve.wait_ge(smix_hi, 1)
            V.tensor_tensor(hl[:, 0:H, TP:T], mixs, hh[:, 0:H, TP:T].bitcast(F32),
                            ALU.subtract).then_inc(smix_ready, 1)
            add_pool_half(15)
            for k in range(2, SLOTS):
                lo(tile_at(T_OA + k))
            dve.wait_ge(wo_taken, KC)

            def add_group(quad, m0, used):
                dve.wait_ge(w_used, used)
                for m in range(4):
                    ins = V.tensor_tensor(xT[:, m0 + m, :], xT[:, m0 + m, :], bank[4 * quad + m][:, 0:T], ALU.add)
                    ins.then_inc(quad_taken[quad], 1)

            def add_out(quad, c, used):
                dve.wait_ge(w_used, used)
                for m in range(4):
                    chunk = xT[:, bass.ds(4 * c + m, 1), :].rearrange("p a t -> p (a t)")
                    V.tensor_tensor(chunk, chunk, bank[4 * quad + m][:, 0:T], ALU.add).then_inc(quad_taken[quad], 1)

            with dve.Fori(0, 2) as i:
                for k in range(8):
                    lo(tile_at(T_OA + 4 + k, i, 8))
                    if k % 4 == 3:
                        quad = k // 4
                        add_out(quad, 2 * i + quad, T_OA + 8 * i + 4 * quad + 4)
            for c in range(KC + 1):
                if c < KC:
                    gained(1, c)
                if c:
                    gained_lo(1, c - 1)
                    if c % 2 == 0 and c >= 6:
                        lo(tile_at(T_FF + 4 + (c - 6) // 2))
            lo(tile_at(T_FF + 10))
            mean_sq(1)
            rstd_of(1)
            lo(tile_at(T_FF + 11))

            def gate_scaled(g, first=False):
                if not first:
                    dve.wait_ge(af_ready, 4 * g)
                dve.wait_ge(w_used, T_FF + 8 if first else T_FF + 24 * g)
                for m in range(4):
                    V.tensor_tensor(sg[:, m, :], bank[m][:, 0:T], rstd[:, :], ALU.mult).then_inc(gs_ready, 1)

            def up_scaled(g):
                for m in range(4):
                    dve.wait_ge(sg_ready, 4 * g + m + 1)
                    V.tensor_tensor(sg[:, m, :], sg[:, m, :], rstd[:, :], ALU.mult).then_inc(sr_ready, 1)

            def mul_act(g):
                def product(m):
                    dve.wait_ge(sr_ready, 4 * g + m + 1)
                    if m >= 2:
                        dve.wait_ge(act_ready, 4 * g + m - 1)
                    V.tensor_tensor(af[:, m % 2, :], sg[:, m, :], bank[4 + m][:, 0:T], ALU.mult).then_inc(af_ready, 1)

                dve.wait_ge(w_used, T_FF + 16 + 24 * g)
                product(0)
                for m in range(4):
                    if m < 3:
                        product(m + 1)
                    dve.wait_ge(ah_ready, 4 * g + m + 1)
                    V.tensor_tensor(al[:, m, :], af[:, m % 2, :], ah[:, m, :].bitcast(F32),
                                    ALU.subtract).then_inc(act_ready, 1)

            gate_scaled(0, first=True)
            up_scaled(0)
            with dve.Fori(0, NG - 1) as g:
                for k in range(24):
                    lo(tile_at(T_FF + 12 + k, g, 24))
                    if k == 7:
                        mul_act(g)
                    if k == 15:
                        gate_scaled(g + 1)
                    if k == 16:
                        up_scaled(g + 1)
                    if k >= 16 and k % 2 == 1:
                        c = (k - 17) // 2
                        add_group((c + 1) % 2, 4 * c, T_FF + 24 + 24 * g + 2 * c + 2)
            for k in range(12):
                lo(tile_at(T_END - 12 + k))
                if k == 7:
                    mul_act(NG - 1)
            dve.wait_ge(stored, 16 * STORES)
            own.link(V.memset(fm[:, :], 1.0))

            def final_gain(c):
                dve.wait_ge(sq_ready, 2 * KC + c + 1)
                V.tensor_scalar(xT[:, c, :], xT[:, c, :], gains[:, 32 + c:33 + c], None, ALU.mult).then_inc(xf_ready, 1)

            for c in range(5):
                if c < 4:
                    dve.wait_ge(w_used, T_END - 8 + 2 * c + 2)
                    for m in range(4):
                        V.tensor_tensor(xT[:, 4 * c + m, :], xT[:, 4 * c + m, :], bank[4 * (c % 2) + m][:, 0:T],
                                        ALU.add).then_inc(x_ready, 1)
                if c:
                    for m in range(4):
                        final_gain(4 * c - 4 + m)
            dve.wait_ge(sq_summed, 3)
            for n in range(3):
                rows = P if n < 2 else TS
                V.tensor_scalar(fm[0:rows, n:n + 1], bank[4 + n][0:rows, 0:1], 1.0 / D, EPS, ALU.mult,
                                ALU.add).then_inc(fms, 1)
            dve.wait_ge(froot, 1)
            inverse_root(rf[:, :], fm[:, :], ft[:, :]).then_inc(rf_ready, 1)
            dve.wait_ge(rf_ready, 1)
            for n in range(1, 12, 2):
                part, c, rows = final_step(n)
                dve.wait_ge(fy_in, n + 1)
                V.tensor_scalar(yt[0:rows, part, 512 * c:512 * c + 512], bank[n % 8][0:rows, :],
                                rf[0:rows, part:part + 1], None, ALU.mult).then_inc(fy_dve, 1)

        @block.gpsimd
        def _(pool):
            own = Steps(pool, pool_own)
            G = nc.gpsimd

            def sum_squares(stage):
                for c in range(KC):
                    n = KC * stage + c
                    pool.wait_ge(sq_ready, n + 1)
                    if c == 0:
                        if stage:
                            pool.wait_ge(sq_summed, stage)
                        G.tensor_copy(ssq[:, :], sq[:, 0, :]).then_inc(sq_added, 1)
                    else:
                        pool.wait_ge(sq_added, n)
                        G.tensor_tensor(ssq[:, :], ssq[:, :], sq[:, c % 2, :], ALU.add).then_inc(sq_added, 1)

            sum_squares(0)
            pool.wait_ge(sq_added, KC)
            L = HIST + NQ
            done = 0
            for g in (3, 2, 1, 0):
                w, first = WINDOWS[g], ZU + 2 * g
                pool.wait_ge(z_ready, 3 * ((ZU + 7 - first) // 3 + 1))
                for c in (first, first + 1):
                    u, us = z[:, c, 0:TP], z[:, c, TP:T].rearrange("p (b q) -> p b q", b=NB)
                    own.did(G.tensor_copy(u_sample[:, c - ZU, :], z[:, c, TP:T]))
                    own.did(G.tensor_copy(u_last[:, c - ZU, :], z[:, c, TP - HIST:TP]))
                    pool.wait_ge(ext_ready, 2)
                    own.did(G.tensor_copy(ext[:, c - ZU, :, HIST:L], us))
                    src, n, shift = u, 0, 1
                    while shift < w:
                        dst = sq[:, n % 2, 0:TP]
                        own.did(G.tensor_copy(dst[:, 0:shift], src[:, 0:shift]))
                        own.did(G.tensor_tensor(dst[:, shift:TP], src[:, shift:TP], src[:, 0:TP - shift], ALU.add))
                        own.settle()
                        src, n, shift = dst, n + 1, 2 * shift
                    dst = sq[:, n % 2, 0:TP]
                    own.did(G.tensor_tensor(dst[:, 0:16], src[:, 0:16], inv_count[:, g, :], ALU.mult))
                    own.did(G.tensor_scalar(dst[:, 16:TP], src[:, 16:TP], 1.0 / w, None, ALU.mult))
                    own.settle()
                    own.did(G.tensor_tensor(u, dst, u, ALU.subtract))
                    src, n, shift = ext[:, c - ZU, :, :], 0, 1
                    while shift < w:
                        dst = nrm[:, n % 2, 0:NB * L].rearrange("p (b l) -> p b l", b=NB)
                        own.link(G.tensor_tensor(dst[:, :, 2 * shift - 1:L], src[:, :, 2 * shift - 1:L],
                                                 src[:, :, shift - 1:L - shift], ALU.add))
                        src, n, shift = dst, n + 1, 2 * shift
                    dst = nrm[:, n % 2, 0:TS].rearrange("p (b q) -> p b q", b=NB)
                    own.link(G.tensor_scalar(dst, src[:, :, HIST:L], 1.0 / w, None, ALU.mult))
                    G.tensor_tensor(us, dst, us, ALU.subtract).then_inc(d_ready, 1)
                    done += 1
                    pool.wait_ge(d_ready, done)
            for r in range(8):
                c = pool_chunk(r)
                pool.wait_ge(y_hi, r + 1)
                G.tensor_tensor(hl[:, c, :], nrm[:, r % 2, :], hh[:, c, :].bitcast(F32),
                                ALU.subtract).then_inc(pool_mix, 1)
            sum_squares(1)
            sum_squares(2)

        @block.tensor
        def _(pe):
            PE = nc.tensor

            def w_tile(t, width, chunks, banks, xh, xl, start, stop):
                n, _, s = t
                pe.wait_ge(lo_ready, n + 1)
                for m, out in enumerate(banks):
                    for i, c in enumerate(chunks):
                        a = width * i + P * m
                        wh, wl = w_hi[:, s, a:a + P], w_lo[:, s, a:a + P]
                        o = out[:, 0:T]
                        PE.matmul(o, wh, xh[:, c, :], start=start and i == 0, stop=False)
                        PE.matmul(o, wh, xl[:, c, :], start=False, stop=False)
                        last = PE.matmul(o, wl, xh[:, c, :], start=False, stop=stop and i == len(chunks) - 1)
                last.then_inc(w_used, 1)

            def turn(out, in_, rows):
                return PE.transpose(out, in_, ident[0:rows, 0:rows])

            pe.wait_ge(tab_in, 16)
            pe.wait_ge(vec_in, 64)
            turn(bank[6][:, 0:56], vec[:, :], 56).then_inc(vecT, 1)
            pe.wait_ge(x_in, 48)

            def x_turned(c):
                if c >= 2:
                    pe.wait_ge(x_ready, c - 1)
                for n in range(3):
                    rows = P if n < 2 else TS
                    last = turn(bank[4 + c % 2][:, P * n:P * n + rows], xs[0:rows, n, P * c:P * c + P], rows)
                last.then_inc(xT_in, 1)

            def sum_sq(stage):
                pe.wait_ge(sq_added, KC * stage + KC)
                PE.matmul(bank[7][:, 0:T], ones, ssq[:, :], start=True, stop=True).then_inc(sq_summed, 1)

            for c in range(2):
                x_turned(c)
            for k in range(16):
                c, j = k // 8, k % 8
                if c == 0:
                    for n in (2 * j + 2, 2 * j + 3):
                        if n < KC:
                            x_turned(n)
                    pe.wait_ge(h_ready, 2 * j + 2)
                if k in (2, 5):
                    n = k // 5
                    pe.wait_ge(hist_in, 16)
                    pe.wait_ge(*((gains_ready, 1), (ext_ready, 1))[n])
                    for m in range(4):
                        last = turn(bank[6][:, 120 * m:120 * m + 120], hist[:, 512 * n + P * m:512 * n + P * m + P],
                                    NB * HIST)
                    last.then_inc(hist_T, 1)
                if k == 8:
                    pe.wait_ge(ext_ready, 2)
                    sum_sq(0)
                    pe.wait_ge(ms_ready, 1)
                w_tile(tile_at(k), 512, (2 * j, 2 * j + 1), bank[4 * c:4 * c + 4], hh, hl, j == 0, j == 7)

            def block_sums(i, has_comb):
                pe.wait_ge(dn_ready, i)
                if has_comb:
                    pe.wait_ge(o7_taken, i - 1)
                PE.matmul(OB[1][:, 0:8], same, dn[:, :, :].rearrange("p j u -> p (j u)"), start=True,
                          stop=True).then_inc(bs_done, 1)

            def joint_max(i):
                pe.wait_ge(dm_ready, i)
                PE.matmul(OB[1][:, 8:12], same, dm[:, :], start=True, stop=True).then_inc(mx_done, 1)

            def p_turned(i, has_comb):
                pe.wait_ge(p_ready, i)
                PE.matmul(OB[1][:, 12:13], same, lsum[:, :], start=True, stop=True).then_inc(l_done, 1)
                if has_comb:
                    pe.wait_ge(comb_saved, i - 1)
                for j in range(4):
                    last = turn(OB[0][:, P * j:P * j + P], ss[:, j, :], P)
                last.then_inc(pt_in, 1)

            def values(i, j):
                pe.wait_ge(v_in, 256 * i + 64 * j - 192)
                if j == 0:
                    pe.wait_ge(pt_ready, i)
                    pe.wait_ge(l_saved, i)
                for x in range(2):
                    for g in range(4):
                        last = PE.matmul(OB[x][32 * g:32 * g + 32, :], pT[:, j, 32 * g:32 * g + 32],
                                         vpage[:, g, 512 * x:512 * x + 512], start=j == 0, stop=j == NQUADS - 1)
                last.then_inc(v_done, 1)

            def kv_step(i, has_v, has_comb, first=False):
                def transposes(j, h):
                    n = 32 * i + 8 * j + h
                    if first and j == 0 and h < 2:
                        for c in range(2):
                            pe.wait_ge(quad_taken[c], QT0)
                    else:
                        pe.wait_ge(kt_out, n - 1)
                    if h == 0:
                        pe.wait_ge(k_in[j % 2], 128 * i + 64 * (j // 2) + 64)
                    for g in range(4):
                        last = turn(KTP[h % 2][:, P * g:P * g + P], kpage[:, j % 2, g, DH * h:DH * h + DH], P)
                    last.then_inc(kt_in, 1)

                def logits(j, h):
                    n = 32 * i + 8 * j + h
                    pe.wait_ge(kt_out, n + 1)
                    if j == 0 and h == 0:
                        pe.wait_ge(qz_ready, i + 1)
                        if not first:
                            pe.wait_ge(dn_ready, i)
                    for g in range(4):
                        last = PE.matmul(S[32 * g:32 * g + 32, P * j:P * j + P], qz[:, 32 * h:32 * h + 32],
                                         kT[:, h % 2, P * g:P * g + P], start=h == 0, stop=h == H - 1)
                    last.then_inc(qk_done, 1)

                for j in range(NQUADS):
                    transposes(j, 0)
                    for h in range(1, H):
                        transposes(j, h)
                        logits(j, h - 1)
                        if j == 0 and has_v:
                            if h == 2:
                                block_sums(i, has_comb)
                            if h == 3 and has_comb:
                                combine(i - 1)
                            if h == 5:
                                joint_max(i)
                    if j == 0 and not first:
                        pe.wait_ge(z_ready, 3 * i)
                    for k in (2 * j, 2 * j + 1):
                        w_tile(tile_at(T_KVU + k, i, 8), CW, (2 * k, 2 * k + 1), WB, hh, hl, k == 0, k == 7)
                        if k % 2 == 0:
                            logits(j, H - 1)
                            if j == 0 and has_v:
                                p_turned(i, has_comb)
                    if has_v:
                        values(i, j)

            def combine(count):
                pe.wait_ge(o6_taken, count)
                pe.wait_ge(o7_taken, count)
                for h in range(H):
                    last = PE.matmul(OB[0][0:32, 0:DH], headsel[:, h, :], osb[:, DH * h:DH * h + DH],
                                     start=h == 0, stop=h == H - 1)
                last.then_inc(comb_done, 1)

            kv_step(0, False, False, first=True)
            kv_step(1, True, False)
            with pe.Fori(2, NB) as i:
                kv_step(i, True, True)

            def rows_turned(n):
                if n == 0:
                    pe.wait_ge(z_ready, 3 * NB)
                elif n == 3:
                    pe.wait_ge(kt_out, 32 * NB)
                if n in (4, 5):
                    pe.wait_ge((tok_act, tok_dve)[n % 2], 1)
                if n >= 6:
                    pe.wait_ge((tok_act, tok_dve)[n % 2], n // 2)
                buf, chunk, a, b = tok_src(n)
                for m in range(4):
                    last = turn(row_bank(n)[0:b - a, P * m:P * m + P], buf[:, chunk + m, a:b], P)
                last.then_inc(tok_in, 1)

            def mixer(r):
                g, e = 3 - r // 2, r % 2
                pe.wait_ge(d_ready, 2 * (r // 2) + 2)
                if r >= 2:
                    pe.wait_ge(y_sc, r - 1)
                for c in range(2):
                    last = PE.matmul(bank[4 + r % 2][:, 0:T], wpool[:, g, c, P * e:P * e + P],
                                     z[:, ZU + 2 * g + c, :], start=c == 0, stop=c == 1)
                last.then_inc(y_in, 1)

            def w_out_pool(k):
                if k >= 2:
                    pe.wait_ge(wo_taken, k - 1)
                w_tile(tile_at(T_OP + k), P, range(8, KC), bank[k % 2:k % 2 + 1], hh, hl, True, True)

            rows_turned(0)
            rows_turned(1)
            combine(NB - 1)
            block_sums(NB, True)
            rows_turned(2)
            rows_turned(3)
            joint_max(NB)
            rows_turned(4)
            rows_turned(5)
            pe.wait_ge(wpool_in, 16)
            mixer(0)
            mixer(1)
            p_turned(NB, True)
            for r in range(2, 8):
                mixer(r)
            for s in range(H + 2):
                if s < H:
                    if s == 0:
                        pe.wait_ge(y_sc, 8)
                    else:
                        pe.wait_ge(a_out, s)
                    PE.matmul(bank[4][:, 0:P], z[:, ZQ + s, 0:P], z[:, ZK + s, 0:P], start=True, stop=True)
                    PE.matmul(bank[4][:, P:384], z[:, ZQ + s, P:TP], z[:, ZK + s, 0:TP], start=True,
                              stop=True).then_inc(a_in, 1)
                if s == 3:
                    pe.wait_ge(tok_act, 8)
                    pe.wait_ge(tok_dve, 8)
                    pe.wait_ge(pool_mix, 8)
                if s >= 3:
                    w_out_pool(2 * s - 6)
                    w_out_pool(2 * s - 5)
                if 1 <= s <= H:
                    h = s - 1
                    pe.wait_ge(pn_ready, 2 * h + 2)
                    if h == 0:
                        pe.wait_ge(tok_act, 3)
                        pe.wait_ge(tok_dve, 3)
                    else:
                        pe.wait_ge(pt2_ready, h)
                    turn(bank[2][:, 0:P], px[:, h % 2, 0:P], P)
                    turn(bank[2][:, P:TP], px[:, h % 2, P:TP], P)
                    turn(bank[2][:, TP:384], px[:, h % 2, TP:384], P).then_inc(pt2_in, 1)
                if s >= 2:
                    h = s - 2
                    pe.wait_ge(pt2_ready, h + 1)
                    if h:
                        pe.wait_ge(mix_ready, h)
                    PE.matmul(bank[3][:, 0:TP], vtok[:, 0, DH * h:DH * h + DH], ptp[:, h % 2, 0:TP],
                              start=True, stop=False)
                    PE.matmul(bank[3][:, P:TP], vtok[:, 1, DH * h:DH * h + DH], ptp[:, h % 2, TP:384], start=False,
                              stop=True).then_inc(po_in, 1)
                if s % 2 and s < 8:
                    values(NB, s // 2)
                for n in ROWS_AT[s]:
                    rows_turned(n)
                if s == 1:
                    pe.wait_ge(qza_ready, 1)
                    for b in range(NB):
                        for h in range(H):
                            last = PE.matmul(bank[5][0:32, NQ * b:NQ * b + NQ], qza[:, b, 32 * h:32 * h + 32],
                                             z[:, ZK + h, TP + NQ * b:TP + NQ * b + NQ], start=h == 0, stop=h == H - 1)
                    last.then_inc(so_in, 1)
                if s == 4:
                    pe.wait_ge(own_ready, 1)
                    turn(bank[5][0:32, 0:32], so[:, :, :].rearrange("p b k -> p (b k)"), 32).then_inc(pTo_in, 1)
                if s == 5:
                    pe.wait_ge(pTb_ready, 1)
                    for h in range(H):
                        last = PE.matmul(bank[5][:, 32 * h:32 * h + 32], stok[0:TS, DH * h:DH * h + DH],
                                         pTb[:, h, :, :].rearrange("p b q -> p (b q)"), start=True, stop=True)
                    last.then_inc(t2_in, 1)
                if s == H:
                    combine(NB)
            pe.wait_ge(own_scaled, 1)
            for b in range(NB):
                last = turn(bank[7][:, 32 * b:32 * b + 32], o_all[:, b, :], 32)
            last.then_inc(t1_in, 1)
            w_out_pool(14)
            w_out_pool(15)
            pe.wait_ge(wo_taken, KC)
            pe.wait_ge(mix_ready, H)
            pe.wait_ge(smix_ready, 1)
            pe.wait_ge(t1_saved, 1)
            with pe.Fori(0, 2) as i:
                for k in range(8):
                    c, j = k // 4, k % 4
                    if j == 0:
                        pe.wait_ge(quad_taken[c], QT0 + 4 * i)
                    w_tile(tile_at(T_OA + k, i, 8), 512, (2 * j, 2 * j + 1), bank[4 * c:4 * c + 4], hh, hl,
                           j == 0, j == 3)
            def gate_up(t0, quad):
                for j in range(8):
                    w_tile(tile_at(*((t0[0] + j,) + t0[1:])), 512, (2 * j, 2 * j + 1), bank[4 * quad:4 * quad + 4],
                           hh, hl, j == 0, j == 7)

            pe.wait_ge(quad_taken[0], QT)
            for j in range(8):
                pe.wait_ge(h_ready, KC + 2 * j + 2)
                w_tile(tile_at(T_FF + j), 512, (2 * j, 2 * j + 1), bank[0:4], hh, hl, j == 0, j == 7)
                if j == 6:
                    sum_sq(1)
            pe.wait_ge(ms_ready, 2)

            def down(t0, g, quads, taken):
                for c in range(4):
                    quad = quads[c]
                    if taken[c]:
                        pe.wait_ge(*taken[c])
                    if c == 0:
                        pe.wait_ge(af_ready, 4 * g + 4)
                    for j in range(2):
                        if c == 0:
                            pe.wait_ge(act_ready, 4 * g + 2 * j + 2)
                        w_tile(tile_at(*((t0[0] + 2 * c + j,) + t0[1:])), 512, (2 * j, 2 * j + 1),
                               bank[4 * quad:4 * quad + 4], ah, al, j == 0, j == 1)

            with pe.Fori(0, NG - 1) as g:
                pe.wait_ge(quad_taken[1], QT + 8 * g)
                gate_up((T_FF + 8, g, 24), 1)
                pe.wait_ge(gs_ready, 4 * g + 4)
                pe.wait_ge(quad_taken[0], QT + 8 * g)
                gate_up((T_FF + 16, g, 24), 0)
                down((T_FF + 24, g, 24), g, (1, 0, 1, 0),
                     (None, (gs_ready, 4 * g + 8), (quad_taken[1], QT + 4 + 8 * g), (quad_taken[0], QT + 4 + 8 * g)))
            pe.wait_ge(quad_taken[1], QT + 8 * (NG - 1))
            gate_up((T_END - 16,), 1)
            pe.wait_ge(quad_taken[0], QT + 8 * (NG - 1))
            pe.wait_ge(gs_ready, 4 * NG)
            down((T_END - 8,), NG - 1, (0, 1, 0, 1),
                 (None, (act_ready, 4 * NG), (x_ready, KC + 4), (x_ready, KC + 8)))
            pe.wait_ge(x_ready, KC + 12)
            for n in range(12):
                part, c, rows = final_step(n)
                if n == 3:
                    pe.wait_ge(sq_added, 3 * KC)
                    pe.wait_ge(x_ready, 2 * KC)
                    for m in range(3):
                        width = P if m < 2 else TS
                        last = PE.matmul(bank[4 + m][0:width, 0:1], ssq[:, P * m:P * m + width], ones[:, 0:1],
                                         start=True, stop=True)
                    last.then_inc(sq_summed, 1)
                if n == 4:
                    pe.wait_ge(fms, 3)
                if n >= 8:
                    pe.wait_ge((fy_act, fy_dve)[n % 2], (n - 8) // 2 + 1)
                pe.wait_ge(xf_ready, 4 * c + 4)
                for m in range(4):
                    last = turn(bank[n % 8][0:rows, P * m:P * m + P], xT[:, 4 * c + m, P * part:P * part + rows], P)
                last.then_inc(fy_in, 1)


STORES = 6 + 1 + 1 + NB

_INS = ["x_prompt", "x_sample", "cache_k", "cache_v", "state_pool", "page_table", "norm1_g", "w_in", "w_pool",
        "pool_scale", "w_out", "norm2_g", "w_gate", "w_up", "w_down", "norm_f_g"]
_OUTS = [("y_prompt", (1, TP, D)), ("y_sample", (NB, NQ, D)), ("k_prompt", (1, 1, TP, H, DH)),
         ("v_prompt", (1, 1, TP, H, DH)), ("pool_prompt", (1, 1, HIST, AW)), ("k_sample", (1, NB, NQ, H, DH)),
         ("v_sample", (1, NB, NQ, H, DH)), ("pool_sample", (1, NB, HIST, AW))]


def kernel(**inputs):
    import concourse.bacc as bacc
    from concourse.bass_utils import run_bass_kernel_spmd

    nc = bacc.Bacc("TRN2", target_bir_lowering=False, num_devices=1, dynamic_dma_scratch_size=64)
    table, at = tables()
    arrays = {name: np.ascontiguousarray(inputs[name]) for name in _INS}
    arrays["tables"] = table
    ins = {name: nc.dram_tensor(f"in_{name}", a.shape, mybir.dt.from_np(a.dtype), kind="ExternalInput").ap()
           for name, a in arrays.items()}
    outs = {name: nc.dram_tensor(f"out_{name}", shape, F32, kind="ExternalOutput").ap() for name, shape in _OUTS}
    step_program(nc, ins, outs, at)
    r = run_bass_kernel_spmd(nc, [{f"in_{name}": a for name, a in arrays.items()}], core_ids=[0])
    return tuple(r.results[0][f"out_{name}"] for name, _ in _OUTS)
```
